# Optimizing a Trainium2 kernel written in Bass

```python
import math
import jax, jax.numpy as jnp
from jax import lax
import numpy as np

D_MODEL = 1024
BATCH = 1
SEQ = 1024
DEPTH = 2

CTX_LEN = 256
GRID_W = 64
DA_HEADS = 4
DA_HEAD_DIM = 64
DA_V_DIM = 2 * DA_HEAD_DIM
DA_WIDTH = DA_HEADS * DA_V_DIM
SSD_HEADS = 8
SSD_HEAD_DIM = 64
SSD_WIDTH = SSD_HEADS * SSD_HEAD_DIM
SSD_GROUPS = 2
SSD_STATE = 128
SSD_CONV = 5
SSD_CHUNK = 128
SSD_CONV_CH = SSD_WIDTH + 2 * SSD_GROUPS * SSD_STATE
D_MIX = DA_WIDTH + SSD_WIDTH
D_FF = ((8 * D_MODEL + 3 * 256 - 1) // (3 * 256)) * 256
Q_BLOCK = 128
ROPE_BASE = 10000.0
EPS = 1e-6
N_MOD = 6
QK_COLS = DA_HEADS * 2 * DA_HEAD_DIM
Q_END = QK_COLS
K_END = Q_END + QK_COLS
V_END = K_END + DA_WIDTH
Z_END = V_END + SSD_WIDTH
XBC_END = Z_END + SSD_CONV_CH
IN_COLS = XBC_END + 2 * SSD_HEADS

kernel_name = "hymba_diffattn_ssd_prefix_dit"

def rmsnorm(u, g):
    uf = u.astype(jnp.float32)
    y = uf * lax.rsqrt(jnp.mean(uf * uf, axis=-1, keepdims=True) + EPS)
    return (y * g.astype(jnp.float32)).astype(u.dtype)

def modulate(u, shift, scale):
    return u * (1 + scale) + shift

def axial_rope_tables(L):
    rows = L // GRID_W
    row = jnp.repeat(jnp.arange(rows, dtype=jnp.float32), GRID_W)
    col = jnp.tile(jnp.arange(GRID_W, dtype=jnp.float32), rows)
    nf = DA_HEAD_DIM // 4
    inv = ROPE_BASE ** (-jnp.arange(nf, dtype=jnp.float32) / nf)
    ang = jnp.concatenate([row[:, None] * inv, col[:, None] * inv], axis=-1)
    return jnp.cos(ang), jnp.sin(ang)

def apply_rope(u, cos, sin):
    u1, u2 = jnp.split(u, 2, axis=-1)
    c = cos[None, :, None, None, :].astype(u.dtype)
    s = sin[None, :, None, None, :].astype(u.dtype)
    return jnp.concatenate([u1 * c - u2 * s, u1 * s + u2 * c], axis=-1)

def dwconv_centred(u, w, b):
    ch = u.shape[-1]
    out = lax.conv_general_dilated(
        u, w[:, None, :].astype(u.dtype), window_strides=(1,),
        padding=[(SSD_CONV // 2, SSD_CONV // 2)],
        dimension_numbers=('NWC', 'WIO', 'NWC'), feature_group_count=ch)
    return jax.nn.silu(out + b)

def diff_attn_block(q, k, v, lam):
    s = jnp.einsum('bqhmd,bkhmd->bhmqk', q, k).astype(jnp.float32) * (DA_HEAD_DIM ** -0.5)
    p = jax.nn.softmax(s, axis=-1)
    pd = p[:, :, 0] - lam * p[:, :, 1]
    return jnp.einsum('bhqk,bkhe->bqhe', pd.astype(v.dtype), v)

def diff_attn_latent(q, k_all, v_all, lam):
    bsz, L, H, _, d = q.shape
    nb = L // Q_BLOCK
    qb = jnp.moveaxis(q.reshape(bsz, nb, Q_BLOCK, H, 2, d), 1, 0)
    o = lax.map(lambda qi: diff_attn_block(qi, k_all, v_all, lam), qb)
    return jnp.moveaxis(o, 0, 1).reshape(bsz, L, H, DA_V_DIM)

def ssd_scan(x, dt, A, Bm, Cm, h0):
    bsz, L, H, P = x.shape
    G, N = Bm.shape[2], Bm.shape[3]
    R = H // G
    nc = L // SSD_CHUNK

    def chunks(a):
        return jnp.moveaxis(a.reshape(bsz, nc, SSD_CHUNK, *a.shape[2:]), 1, 0)

    xs = chunks(x.astype(jnp.float32).reshape(bsz, L, G, R, P))
    dts = chunks(dt.reshape(bsz, L, G, R))
    bs = chunks(Bm.astype(jnp.float32))
    cs = chunks(Cm.astype(jnp.float32))
    a_g = A.reshape(G, R)
    lower = jnp.tril(jnp.ones((SSD_CHUNK, SSD_CHUNK), dtype=bool))[None, :, :, None, None]

    def step(h, inp):
        xc, dtc, bc, cc = inp
        cum = jnp.cumsum(dtc * a_g, axis=1)
        seg = cum[:, :, None] - cum[:, None, :]
        lmat = jnp.exp(jnp.where(lower, seg, -jnp.inf))
        xdt = xc * dtc[..., None]
        cb = jnp.einsum('bign,bjgn->bijg', cc, bc)
        y_diag = jnp.einsum('bijg,bijgr,bjgrp->bigrp', cb, lmat, xdt)
        y_off = jnp.einsum('bign,bgrpn,bigr->bigrp', cc, h, jnp.exp(cum))
        decay_end = jnp.exp(cum[:, -1:] - cum)
        h_new = h * jnp.exp(cum[:, -1])[..., None, None] + jnp.einsum(
            'bjgn,bjgr,bjgrp->bgrpn', bc, decay_end, xdt)
        return h_new, y_diag + y_off

    h_fin, ys = lax.scan(step, h0, (xs, dts, bs, cs))
    y = jnp.moveaxis(ys, 0, 1).reshape(bsz, L, H, P)
    return y, h_fin

def ssd_inputs(xbc, dtr, dt_bias):
    bsz, L, _ = xbc.shape
    gn = SSD_GROUPS * SSD_STATE
    xs = xbc[..., :SSD_WIDTH].reshape(bsz, L, SSD_HEADS, SSD_HEAD_DIM)
    bm = xbc[..., SSD_WIDTH:SSD_WIDTH + gn].reshape(bsz, L, SSD_GROUPS, SSD_STATE)
    cm = xbc[..., SSD_WIDTH + gn:].reshape(bsz, L, SSD_GROUPS, SSD_STATE)
    dt = jax.nn.softplus(dtr.astype(jnp.float32).reshape(bsz, L, 2, SSD_HEADS)
                         + dt_bias.astype(jnp.float32))
    return xs, bm, cm, dt

def gated_out_norm(y, z, g):
    bsz, L = z.shape[0], z.shape[1]
    u = y.reshape(bsz, L, SSD_WIDTH) * jax.nn.silu(z.astype(jnp.float32))
    return rmsnorm(u, g).astype(z.dtype)

def hybrid_mixer(h_l, h_c, w_in, conv_w, conv_b, a_log, dt_bias, d_skip, ssd_g,
                 lam_vec, sub_g, w_out, lam_init, cos, sin, need_ctx):
    p_l = h_l @ w_in
    p_c = h_c @ w_in
    bsz, L, _ = p_l.shape
    Lc = p_c.shape[1]

    def qkv(p, n):
        q = p[..., :Q_END].reshape(bsz, n, DA_HEADS, 2, DA_HEAD_DIM)
        k = p[..., Q_END:K_END].reshape(bsz, n, DA_HEADS, 2, DA_HEAD_DIM)
        v = p[..., K_END:V_END].reshape(bsz, n, DA_HEADS, DA_V_DIM)
        return q, k, v

    q_l, k_l, v_l = qkv(p_l, L)
    q_c, k_c, v_c = qkv(p_c, Lc)
    q_l = apply_rope(q_l, cos, sin)
    k_l = apply_rope(k_l, cos, sin)
    lv = lam_vec.astype(jnp.float32)
    lam = jnp.exp(jnp.sum(lv[0] * lv[1])) - jnp.exp(jnp.sum(lv[2] * lv[3])) + lam_init
    k_all = jnp.concatenate([k_c, k_l], axis=1)
    v_all = jnp.concatenate([v_c, v_l], axis=1)
    o_l = diff_attn_latent(q_l, k_all, v_all, lam)
    attn_l = (rmsnorm(o_l, sub_g) * (1.0 - lam_init)).reshape(bsz, L, DA_WIDTH)

    z_l, z_c = p_l[..., V_END:Z_END], p_c[..., V_END:Z_END]
    xbc_l = dwconv_centred(p_l[..., Z_END:XBC_END], conv_w, conv_b)
    xbc_c = dwconv_centred(p_c[..., Z_END:XBC_END], conv_w, conv_b)
    xl, bl, cl, dtl = ssd_inputs(xbc_l, p_l[..., XBC_END:], dt_bias)
    xc, bc, cc, dtc = ssd_inputs(xbc_c, p_c[..., XBC_END:], dt_bias)
    A = -jnp.exp(a_log.astype(jnp.float32))
    dsk = d_skip.astype(jnp.float32)[:, None]
    h0 = jnp.zeros((bsz, SSD_GROUPS, SSD_HEADS // SSD_GROUPS, SSD_HEAD_DIM, SSD_STATE),
                   jnp.float32)
    flip = lambda a: jnp.flip(a, axis=1)
    y_cf, h_cf = ssd_scan(xc, dtc[:, :, 0], A[0], bc, cc, h0)
    y_lf, _ = ssd_scan(xl, dtl[:, :, 0], A[0], bl, cl, h_cf)
    y_cb, h_cb = ssd_scan(flip(xc), flip(dtc[:, :, 1]), A[1], flip(bc), flip(cc), h0)
    y_lb, _ = ssd_scan(flip(xl), flip(dtl[:, :, 1]), A[1], flip(bl), flip(cl), h_cb)
    y_l = y_lf + flip(y_lb) + dsk * xl.astype(jnp.float32)
    ssd_l = gated_out_norm(y_l, z_l, ssd_g)

    mix_l = jnp.concatenate([attn_l, ssd_l], axis=-1) @ w_out
    if not need_ctx:
        return mix_l, None
    o_c = diff_attn_block(q_c, k_c, v_c, lam)
    attn_c = (rmsnorm(o_c, sub_g) * (1.0 - lam_init)).reshape(bsz, Lc, DA_WIDTH)
    y_c = y_cf + flip(y_cb) + dsk * xc.astype(jnp.float32)
    ssd_c = gated_out_norm(y_c, z_c, ssd_g)
    mix_c = jnp.concatenate([attn_c, ssd_c], axis=-1) @ w_out
    return mix_l, mix_c

def swiglu(h, w1, w2):
    gate, up = jnp.split(h @ w1, 2, axis=-1)
    return (jax.nn.silu(gate) * up) @ w2

def setup_inputs(seed: int = 0) -> dict:
    key = jax.random.key(seed)
    ks = jax.random.split(key, 20)
    f32 = jnp.float32
    s = D_MODEL ** -0.5
    dt0 = jnp.exp(jax.random.uniform(ks[9], (DEPTH, 2, SSD_HEADS), f32,
                                     math.log(1e-3), math.log(1e-1)))
    return {
        'x': jax.random.normal(ks[0], (BATCH, SEQ, D_MODEL), f32),
        'c': jax.random.normal(ks[1], (BATCH, D_MODEL), f32),
        'ctx': jax.random.normal(ks[2], (BATCH, CTX_LEN, D_MODEL), f32),
        'c_ctx': jax.random.normal(ks[3], (D_MODEL,), f32),
        'w_ada': jax.random.normal(ks[4], (DEPTH, D_MODEL, N_MOD * D_MODEL), f32) * (0.5 * s),
        'b_ada': jax.random.normal(ks[5], (DEPTH, N_MOD * D_MODEL), f32) * 0.01,
        'norm_g': 1.0 + 0.05 * jax.random.normal(ks[6], (DEPTH, 4, D_MODEL), f32),
        'w_in': jax.random.normal(ks[7], (DEPTH, D_MODEL, IN_COLS), f32) * s,
        'conv_w': jax.random.normal(ks[8], (DEPTH, SSD_CONV, SSD_CONV_CH), f32) * (SSD_CONV ** -0.5),
        'conv_b': jax.random.normal(ks[10], (DEPTH, SSD_CONV_CH), f32) * 0.01,
        'a_log': jnp.log(jax.random.uniform(ks[11], (DEPTH, 2, SSD_HEADS), f32, 1.0, 16.0)),
        'dt_bias': dt0 + jnp.log(-jnp.expm1(-dt0)),
        'd_skip': 1.0 + 0.05 * jax.random.normal(ks[12], (DEPTH, SSD_HEADS), f32),
        'ssd_norm_g': 1.0 + 0.05 * jax.random.normal(ks[13], (DEPTH, SSD_WIDTH), f32),
        'diff_lambda': 0.1 * jax.random.normal(ks[14], (DEPTH, 4, DA_HEAD_DIM), f32),
        'subln_g': 1.0 + 0.05 * jax.random.normal(ks[15], (DEPTH, DA_V_DIM), f32),
        'w_out': jax.random.normal(ks[16], (DEPTH, D_MIX, D_MODEL), f32) * (D_MIX ** -0.5),
        'w_ffn_in': jax.random.normal(ks[17], (DEPTH, D_MODEL, 2 * D_FF), f32) * s,
        'w_ffn_out': jax.random.normal(ks[18], (DEPTH, D_FF, D_MODEL), f32) * (D_FF ** -0.5),
    }

def reference(x, c, ctx, c_ctx, w_ada, b_ada, norm_g, w_in, conv_w, conv_b, a_log,
              dt_bias, d_skip, ssd_norm_g, diff_lambda, subln_g, w_out, w_ffn_in, w_ffn_out):
    L = x.shape[1]
    cos, sin = axial_rope_tables(L)
    sc = jax.nn.silu(c)
    scc = jax.nn.silu(c_ctx)
    for i in range(DEPTH):
        need_ctx = i < DEPTH - 1
        lam_init = 0.8 - 0.6 * math.exp(-0.3 * i)
        mod_l = (sc @ w_ada[i] + b_ada[i])[:, None, :]
        mod_c = (scc @ w_ada[i] + b_ada[i])[None, None, :]
        sh1, sc1, g1, sh2, sc2, g2 = jnp.split(mod_l, N_MOD, axis=-1)
        csh1, csc1, cg1, csh2, csc2, cg2 = jnp.split(mod_c, N_MOD, axis=-1)

        h_l = modulate(rmsnorm(x, norm_g[i, 0]), sh1, sc1)
        h_c = modulate(rmsnorm(ctx, norm_g[i, 0]), csh1, csc1)
        mix_l, mix_c = hybrid_mixer(h_l, h_c, w_in[i], conv_w[i], conv_b[i], a_log[i],
                                    dt_bias[i], d_skip[i], ssd_norm_g[i], diff_lambda[i],
                                    subln_g[i], w_out[i], lam_init, cos, sin, need_ctx)
        x = x + g1 * rmsnorm(mix_l, norm_g[i, 1])
        f_l = swiglu(modulate(rmsnorm(x, norm_g[i, 2]), sh2, sc2), w_ffn_in[i], w_ffn_out[i])
        x = x + g2 * rmsnorm(f_l, norm_g[i, 3])
        if need_ctx:
            ctx = ctx + cg1 * rmsnorm(mix_c, norm_g[i, 1])
            f_c = swiglu(modulate(rmsnorm(ctx, norm_g[i, 2]), csh2, csc2), w_ffn_in[i], w_ffn_out[i])
            ctx = ctx + cg2 * rmsnorm(f_c, norm_g[i, 3])
    return x


_drawn_inputs = setup_inputs


def setup_inputs(seed=0):
    import zlib

    import numpy as np

    out = dict(_drawn_inputs(seed))
    spreads = {}
    factors = {'conv_b': 8.0, 'd_skip': 8.0, 'ssd_norm_g': 3.35, 'subln_g': 4.413}
    for name, (base, spread) in spreads.items():
        noise = np.random.default_rng([zlib.crc32(name.encode()), seed]).standard_normal(out[name].shape)
        drawn = base * np.exp(spread * noise) if base else spread * noise
        out[name] = __import__('jax').numpy.asarray(drawn.astype(out[name].dtype))
    for name, factor in factors.items():
        out[name] = (out[name] * factor).astype(out[name].dtype)
    return out
```

```python
from contextlib import ExitStack, contextmanager

import concourse.bass as bass
from concourse import mybir

F32 = mybir.dt.float32
F32R = mybir.dt.float32r
ALU = mybir.AluOpType
ACT = mybir.ActivationFunctionType
AX = mybir.AxisListType

P = 128
D_MODEL = 1024
KD = D_MODEL // P
CTX, LAT = 256, 1024
T = CTX + LAT
NT = T // P
HEADS = 4
SH = 8
SW = 512
NG = 2
DFF = 2816
KF = DFF // P
QK_TILES = 8
V_END = 1536
XBC0 = 2048
DT0 = 3072
IN_COLS = 3088
DTP = 40
BWD = 32
EPS = 1e-6
CHUNKS = [(0, 256), (256, 512), (768, 512)]
LAM_INIT = [0.2, 0.8 - 0.6 * 0.7408182206817179]
ROW_ADA, ROW_NG, ROW_CW, ROW_CB = 0, 48, 80, 120
ROW_SG, ROW_SUB, ROW_C = 0, 4, 5
SH1, SC1, G1, SH2, SC2, G2 = range(6)


class Chain:

    def __init__(self, eng, sem):
        self.eng, self.sem, self.n, self.off = eng, sem, 0, 0

    def __call__(self, ins):
        self.n += 1
        ins.then_inc(self.sem, 1)
        self.eng.wait_ge(self.sem, self.off + self.n)

    @contextmanager
    def over(self, i, count, per):
        start, self.off = self.n, i * per
        yield
        assert self.n - start == per, (self.n - start, per)
        self.n, self.off = start + per * count, 0


class Stage:

    def __init__(self, nc, name):
        self.nc, self.name, self.ctx, self.sems = nc, name, ExitStack(), []

    def __enter__(self):
        self.ctx.__enter__()
        return self

    def __exit__(self, *a):
        done = self.ctx.__exit__(*a)
        if a[0] is None:
            self.nc.clear_and_free_semaphores(self.sems)
            self.nc.all_engine_barrier()
        return done

    def sb(self, name, shape, dt=F32):
        return self.ctx.enter_context(self.nc.sbuf_tensor(f"{self.name}_{name}", shape, dt))

    def ps(self, name, shape):
        return self.ctx.enter_context(self.nc.psum_tensor(f"{self.name}_{name}", shape, F32))

    def sem(self, name):
        self.sems.append(self.nc.alloc_semaphore(f"{self.name}_{name}"))
        return self.sems[-1]

    def block(self):
        return self.ctx.enter_context(self.nc.Block())


class WeightRing:

    def __init__(self, st, tiles=KD, width=P):
        self.raw = st.sb("w_raw", [P, 2, tiles, width])
        self.hi = st.sb("w_hi", [P, 2, tiles, width], F32R)
        self.lo = st.sb("w_lo", [P, 2, tiles, width], F32R)
        self.landed = [st.sem(f"w_landed{s}") for s in range(2)]
        self.rounded, self.split, self.used = st.sem("w_rounded"), st.sem("w_split"), st.sem("w_used")

    def start_vector(self, dve):
        dve.sem_inc(self.split, 2)

    def start_tensor(self, pe):
        pe.sem_inc(self.used, 2)

    def load(self, sp, v, s, src, tiles=KD):
        sp.wait_ge(self.split, 2 * v + s + 1)
        sp.dma_start(self.raw[:, s, 0:tiles], src).then_inc(self.landed[s], 16)

    def round(self, act, nc, v, s, tiles=KD):
        act.wait_ge(self.landed[s], 16 * v + 16)
        act.wait_ge(self.used, 2 * v + s + 1)
        nc.scalar.activation(self.hi[:, s, 0:tiles], self.raw[:, s, 0:tiles], ACT.Copy).then_inc(self.rounded, 1)

    def rest(self, dve, nc, v, s, tiles=KD):
        dve.wait_ge(self.rounded, 2 * v + s + 1)
        nc.vector.tensor_tensor(self.lo[:, s, 0:tiles], self.raw[:, s, 0:tiles], self.hi[:, s, 0:tiles],
                                ALU.subtract).then_inc(self.split, 1)

    def ready(self, pe, v, s):
        pe.wait_ge(self.split, 2 * v + s + 3)

    def count_used(self, v, s):
        return 2 * v + s + 3


def product3(nc, out, w_hi, w_lo, x_hi, x_lo, tiles, first=True, last=True):
    for k in range(tiles):
        a, b = first and k == 0, last and k == tiles - 1
        nc.tensor.matmul(out, w_hi[:, k], x_hi[:, k], start=a, stop=False)
        nc.tensor.matmul(out, w_hi[:, k], x_lo[:, k], start=False, stop=False)
        ins = nc.tensor.matmul(out, w_lo[:, k], x_hi[:, k], start=False, stop=b)
    return ins


class RowNorm:

    def __init__(self, st, name, n, features, psum, ones, tiles):
        self.n, self.features, self.psum, self.ones, self.tiles = n, features, psum, ones, tiles
        self.ss = st.sb(f"{name}_ss", [P, n])
        self.m = st.sb(f"{name}_m", [P, n])
        self.r = st.sb(f"{name}_r", [P, n])
        self.squared, self.summed, self.total, self.mean, self.guess = (
            st.sem(f"{name}_{x}") for x in ("squared", "summed", "total", "mean", "guess"))

    def square(self, nc, sq, u):
        nc.scalar.activation(sq, u, ACT.Square).then_inc(self.squared, 1)

    def add_tiles(self, dve, nc, sq):
        dve.wait_ge(self.squared, 1)
        nc.vector.tensor_reduce(self.ss[:], sq.rearrange("p k n -> p n k"), AX.X, ALU.add).then_inc(self.summed, 1)

    def add_partitions(self, pe, nc, src=None):
        pe.wait_ge(self.summed, 1)
        nc.tensor.matmul(self.psum[:, 0:self.n], self.ones[:], self.ss[:] if src is None else src,
                         start=True, stop=True).then_inc(self.total, 1)

    def mean_eps(self, dve, nc):
        dve.wait_ge(self.total, 1)
        nc.vector.tensor_scalar(self.m[:], self.psum[:, 0:self.n], 1.0 / self.features, EPS,
                                ALU.mult, ALU.add).then_inc(self.mean, 1)

    def root(self, act, nc, chain):
        act.wait_ge(self.mean, 1)
        chain(nc.scalar.activation(self.r[:], self.m[:], ACT.Ln))
        nc.scalar.activation(self.r[:], self.r[:], ACT.Exp, scale=-0.5).then_inc(self.guess, 1)

    def refine(self, dve, nc, chain):
        dve.wait_ge(self.guess, 1)
        chain(nc.vector.tensor_tensor(self.ss[:], self.r[:], self.r[:], ALU.mult))
        chain(nc.vector.scalar_tensor_tensor(self.ss[:], self.ss[:], -0.5, self.m[:], ALU.mult, ALU.mult))
        chain(nc.vector.scalar_tensor_tensor(self.r[:], self.ss[:], 1.5, self.r[:], ALU.add, ALU.mult))


def setup_stage(nc, g):
    with Stage(nc, "setup") as st:
        xtok = st.sb("xtok", [P, 2, D_MODEL])
        xt = st.sb("xt", [P, 2, KD, P])
        tp = st.ps("tp", [P, 2, KD, P])
        const_in = st.sem("const_in")
        x_in = [st.sem(f"x_in{s}") for s in range(2)]
        turned, copied = st.sem("turned"), st.sem("copied")
        stored = [st.sem(f"stored{s}") for s in range(2)]
        block = st.block()

        @block.sync
        def _(sp):
            sp.dma_start(g.ident[:], g.ident_d).then_inc(const_in, 16)
            sp.dma_start(g.masks[:], g.masks_d.rearrange("d j i -> j d i")).then_inc(const_in, 16)
            with sp.Fori(0, NT // 2) as v:
                for s in range(2):
                    sp.wait_ge(turned, 2 * v + s + 1)
                    sp.dma_start(xtok[:, s], g.x_in[bass.ds((2 * v + s) * P, P), :]).then_inc(x_in[s], 16)

        @block.tensor
        def _(pe):
            pe.sem_inc(turned, 2)
            pe.wait_ge(const_in, 32)
            with pe.Fori(0, NT // 2) as v:
                for s in range(2):
                    pe.wait_ge(x_in[s], 16 * v + 16)
                    pe.wait_ge(copied, 2 * v + s + 1)
                    for k in range(KD):
                        last = nc.tensor.transpose(tp[:, s, k], xtok[:, s, k * P:(k + 1) * P], g.ident[:])
                    last.then_inc(turned, 1)

        @block.vector
        def _(dve):
            dve.sem_inc(copied, 2)
            nc.vector.memset(g.ones[:], 1.0)
            for s in range(2):
                dve.sem_inc(stored[s], 16)
            with dve.Fori(0, NT // 2) as v:
                for s in range(2):
                    dve.wait_ge(turned, 2 * v + s + 3)
                    dve.wait_ge(stored[s], 16 * v + 16)
                    nc.vector.tensor_copy(xt[:, s], tp[:, s]).then_inc(copied, 1)

        @block.scalar
        def _(act):
            with act.Fori(0, NT // 2) as v:
                for s in range(2):
                    act.wait_ge(copied, 2 * v + s + 3)
                    act.dma_start(g.xT.rearrange("(k p) t -> p k t", p=P)[:, :, bass.ds((2 * v + s) * P, P)],
                                  xt[:, s]).then_inc(stored[s], 16)
            for s in range(2):
                act.wait_ge(stored[s], 16 * (NT // 2 + 1))


def ada_stage(nc, g, layer):
    STEP = 512
    steps = 6 * D_MODEL // STEP
    sub = STEP // P
    with Stage(nc, f"ada{layer}") as st:
        rows_a = st.sb("rows_a", [P, P])
        rows_b = st.sb("rows_b", [21, P])
        lam_in = st.sb("lam_in", [P, 4, 64])
        lam_t = st.sb("lam_t", [P, 2, 64])
        skip_in = st.sb("skip_in", [P, SH])
        lam_s = st.sb("lam_s", [P, 2])
        silu_c = st.sb("silu_c", [P, KD, 2])
        e_c = st.sb("e_c", [P, 2 * KD])
        wa = st.sb("wa", [P, 2, KD, STEP])
        psv = st.ps("psv", [P, 2, P])
        row = st.sb("row", [2, 2, STEP])
        psr = st.ps("psr", [2, 2, 512])
        psm = st.ps("psm", [P, 2, 512])
        vec_in, lam_land = st.sem("vec_in"), st.sem("lam_land")
        wa_in = [st.sem(f"wa_in{s}") for s in range(2)]
        turned, cols_done, c_exp, c_silu = st.sem("turned"), st.sem("cols_done"), st.sem("c_exp"), st.sem("c_silu")
        columns = st.sem("columns")
        done, mod_done, lam_sum, lam_exp = st.sem("done"), st.sem("mod_done"), st.sem("lam_sum"), st.sem("lam_exp")
        a_land, a_exp = st.sem("a_land"), st.sem("a_exp")
        a_zero, row_done = st.sem("a_zero"), st.sem("row_done")
        chain_v = st.sem("chain_v")
        block = st.block()

        @block.sync
        def _(sp):
            for row, src in ((ROW_ADA, g.b_ada[layer].rearrange("(r q) -> r q", q=P)),
                             (ROW_NG, g.norm_g[layer].rearrange("v (r q) -> (v r) q", q=P)),
                             (ROW_CW, g.conv_w[layer].rearrange("v (r q) -> (v r) q", q=P)),
                             (ROW_CB, g.conv_b[layer].rearrange("(r q) -> r q", q=P))):
                sp.dma_start(rows_a[row:row + src.shape[0]], src).then_inc(vec_in, 16)
            for row, src in ((ROW_SG, g.ssd_g[layer].rearrange("(r q) -> r q", q=P)),
                             (ROW_SUB, g.sub_g[layer].rearrange("(r q) -> r q", q=P)),
                             (ROW_C, g.c_ctx.rearrange("(r q) -> r q", q=P)),
                             (ROW_C + KD, g.c.rearrange("b (r q) -> (b r) q", q=P))):
                sp.dma_start(rows_b[row:row + src.shape[0]], src).then_inc(vec_in, 16)
            with sp.Fori(0, steps // 2) as v:
                for s in range(2):
                    sp.wait_ge(done, 2 * v + s + 1)
                    sp.dma_start(wa[:, s], g.w_ada[layer].rearrange("(k p) n -> p k n", p=P)[
                        :, :, bass.ds((2 * v + s) * STEP, STEP)]).then_inc(wa_in[s], 16)

        @block.gpsimd
        def _(pool):
            nc.gpsimd.memset(g.a_neg[:], 0.0).then_inc(a_zero, 1)
            nc.gpsimd.memset(g.dt_bias[:], 0.0).then_inc(a_zero, 1)
            pool.wait_ge(a_zero, 2)
            for d in range(2):
                pool.dma_start(g.a_neg[BWD * d:BWD * d + SH, :], g.a_log[layer, d].rearrange("(h o) -> h o", o=1)).then_inc(a_land, 16)
                pool.dma_start(g.dt_bias[BWD * d:BWD * d + SH, :], g.dt_bias_d[layer, d].rearrange("(h o) -> h o", o=1)).then_inc(a_land, 16)
            pool.dma_start(skip_in[:], g.d_skip[layer:layer + 1].to_broadcast([P, SH])).then_inc(a_land, 16)
            pool.dma_start(lam_in[:], g.lam_d[layer:layer + 1].to_broadcast([P, 4, 64])).then_inc(lam_land, 16)
            pool.wait_ge(lam_land, 16)
            pool.wait_ge(a_land, 16 * 5)

        @block.tensor
        def _(pe):
            pe.sem_inc(done, 2)
            pe.wait_ge(row_done, 2)
            pe.wait_ge(vec_in, 16 * 8)
            nc.tensor.transpose(psv[:, 0], rows_a[:], g.ident[:])
            nc.tensor.transpose(psv[:, 1, 0:21], rows_b[:], g.ident[0:21, 0:21]).then_inc(turned, 1)
            pe.wait_ge(c_silu, 1)
            with pe.Fori(0, steps // 2) as v:
                for s in range(2):
                    pe.wait_ge(wa_in[s], 16 * v + 16)
                    pe.wait_ge(row_done, 2 * v + s + 1)
                    for k in range(KD):
                        last = nc.tensor.matmul(psr[:, s, 0:STEP], silu_c[:, k], wa[:, s, k], start=k == 0, stop=k == KD - 1)
                    last.then_inc(done, 1)
                    pe.wait_ge(row_done, 2 * v + s + 3)
                    pe.wait_ge(mod_done, 2 * v + s + 1)
                    for j in range(sub):
                        last = nc.tensor.matmul(psm[:, s, 2 * j:2 * j + 2], row[:, s, j * P:(j + 1) * P], g.ident[0:2, 0:2],
                                                start=True, stop=True)
                    last.then_inc(columns, 1)

        @block.scalar
        def _(act):
            act.sem_inc(row_done, 2)
            act.wait_ge(cols_done, 1)
            nc.scalar.activation(e_c[:], g.cols_b[:, ROW_C:ROW_C + 2 * KD], ACT.Exp, scale=-1.0).then_inc(c_exp, 1)
            act.wait_ge(a_land, 16 * 5)
            nc.scalar.activation(g.a_neg[:], g.a_neg[:], ACT.Exp).then_inc(a_exp, 1)
            act.wait_ge(lam_sum, 1)
            nc.scalar.activation(lam_s[:], lam_s[:], ACT.Exp).then_inc(lam_exp, 1)
            with act.Fori(0, steps // 2) as v:
                for s in range(2):
                    act.wait_ge(done, 2 * v + s + 3)
                    nc.scalar.activation(row[:, s], psr[:, s, 0:STEP], ACT.Copy).then_inc(row_done, 1)

        @block.vector
        def _(dve):
            chain = Chain(dve, chain_v)
            dve.sem_inc(mod_done, 2)
            dve.wait_ge(turned, 1)
            nc.vector.tensor_copy(g.cols_a[:], psv[:, 0])
            nc.vector.tensor_copy(g.cols_b[:], psv[:, 1, 0:21]).then_inc(cols_done, 1)
            dve.wait_ge(c_exp, 1)
            chain(nc.vector.tensor_scalar_add(e_c[:], e_c[:], 1.0))
            chain(nc.vector.reciprocal(e_c[:], e_c[:]))
            nc.vector.tensor_tensor(silu_c.rearrange("p k v -> p v k"), g.cols_b[:, ROW_C:ROW_C + 2 * KD].rearrange("p (v k) -> p v k", v=2),
                                    e_c.rearrange("p (v k) -> p v k", v=2), ALU.mult).then_inc(c_silu, 1)
            dve.wait_ge(a_exp, 1)
            chain(nc.vector.tensor_scalar(g.a_neg[:], g.a_neg[:], -1.0, None, ALU.mult))
            dve.wait_ge(lam_land, 16)
            pairs = lam_in.rearrange("p (a b) d -> p a b d", b=2)
            chain(nc.vector.tensor_tensor(lam_t[:], pairs[:, :, 0], pairs[:, :, 1], ALU.mult))
            nc.vector.tensor_reduce(lam_s[:], lam_t[:], AX.X, ALU.add).then_inc(lam_sum, 1)
            dve.wait_ge(lam_exp, 1)
            chain(nc.vector.tensor_tensor(g.neg_lam[:], lam_s[:, 1:2], lam_s[:, 0:1], ALU.subtract))
            chain(nc.vector.tensor_scalar_add(g.neg_lam[:], g.neg_lam[:], -LAM_INIT[layer]))
            chain(nc.vector.tensor_scalar(g.sub_col[:], g.cols_b[:, ROW_SUB:ROW_SUB + 1], 1.0 - LAM_INIT[layer], None, ALU.mult))
            for e in range(2):
                half = slice(64 * e, 64 * e + 64)
                chain(nc.vector.tensor_copy(g.dskip_b[half], skip_in[half].rearrange("p (t e) -> p t e", e=2)[:, :, e:e + 1].broadcast_to([64, 4, P])))
            with dve.Fori(0, steps // 2) as v:
                for s in range(2):
                    dve.wait_ge(columns, 2 * v + s + 1)
                    cols = bass.ds((2 * v + s) * sub, sub)
                    nc.vector.tensor_tensor(g.mod[:, :, cols], psm[:, s, 0:2 * sub].rearrange("p (j v) -> p v j", v=2),
                                            g.cols_a[:, cols].unsqueeze(1).broadcast_to([P, 2, sub]), ALU.add).then_inc(mod_done, 1)
            dve.wait_ge(mod_done, steps + 2)
            for which, scale, norm in ((0, SC1, 0), (1, SC2, 2)):
                chain(nc.vector.scalar_tensor_tensor(
                    g.pre[:, which], g.mod[:, :, scale * KD:(scale + 1) * KD], 1.0,
                    g.cols_a[:, ROW_NG + norm * KD:ROW_NG + (norm + 1) * KD].unsqueeze(1).broadcast_to([P, 2, KD]), ALU.add, ALU.mult))
            for which, gate, norm in ((0, G1, 1), (1, G2, 3)):
                chain(nc.vector.tensor_tensor(
                    g.post[:, which], g.mod[:, :, gate * KD:(gate + 1) * KD],
                    g.cols_a[:, ROW_NG + norm * KD:ROW_NG + (norm + 1) * KD].unsqueeze(1).broadcast_to([P, 2, KD]), ALU.mult))


class Prenorm:

    def __init__(self, st, g, n, psum, which):
        self.g, self.n, self.which = g, n, which
        self.x = st.sb("x", [P, KD, n])
        self.sq = st.sb("sq", [P, KD, n])
        self.hi = st.sb("h_hi", [P, KD, n], F32R)
        self.lo = st.sb("h_lo", [P, KD, n], F32R)
        self.x_in, self.scaled, self.rounded, self.ready = st.sem("x_in"), st.sem("scaled"), st.sem("h_rounded"), st.sem("h_ready")
        self.norm = RowNorm(st, "pre", n, D_MODEL, psum, g.ones, KD)

    def load(self, sp, c0):
        sp.dma_start(self.x[:], self.g.xT.rearrange("(k p) t -> p k t", p=P)[:, :, c0:c0 + self.n]).then_inc(self.x_in, 16)

    def scalar(self, act, nc, chain, shift):
        act.wait_ge(self.x_in, 16)
        self.norm.square(nc, self.sq[:], self.x[:])
        self.norm.root(act, nc, chain)
        for k in range(KD):
            act.wait_ge(self.scaled, k + 1)
            nc.scalar.activation(self.hi[:, k], self.x[:, k], ACT.Identity, bias=shift[:, k:k + 1]).then_inc(self.rounded, 1)

    def vector(self, dve, nc, chain, scale, shift):
        self.norm.add_tiles(dve, nc, self.sq[:])
        self.norm.mean_eps(dve, nc)
        self.norm.refine(dve, nc, chain)

        def low(k):
            dve.wait_ge(self.scaled, k + 1)
            dve.wait_ge(self.rounded, k + 1)
            nc.vector.scalar_tensor_tensor(self.lo[:, k], self.x[:, k], shift[:, k:k + 1], self.hi[:, k],
                                           ALU.add, ALU.subtract).then_inc(self.ready, 1)
        for k in range(KD):
            nc.vector.scalar_tensor_tensor(self.x[:, k], self.x[:, k], scale[:, k:k + 1], self.norm.r[:],
                                           ALU.mult, ALU.mult).then_inc(self.scaled, 1)
            if k:
                low(k - 1)
        low(KD - 1)


class Residual:

    def __init__(self, st, g, n, psum, f, x):
        self.g, self.n, self.f, self.x = g, n, f, x
        self.tmp = st.sb("res_tmp", [P, 2, n])
        self.x_in, self.scaled, self.summed, self.out, self.zeroed, self.squared, self.added, self.copied = (
            st.sem(f"res_{x}") for x in ("in", "scaled", "summed", "out", "zeroed", "squared", "added", "copied"))
        self.drained = [st.sem(f"res_drained{s}") for s in range(2)]
        self.norm = RowNorm(st, "post", n, D_MODEL, psum, g.ones, KD)

    def view(self, c0):
        return self.g.xT.rearrange("(k p) t -> p k t", p=P)[:, :, c0:c0 + self.n]

    def load(self, sp, c0):
        sp.dma_start(self.x, self.view(c0)).then_inc(self.x_in, 16)

    def start_vector(self, dve):
        for s in range(2):
            dve.sem_inc(self.drained[s], 1)

    def square_tile(self, act, nc, o, half):
        act.wait_ge(self.copied, 2 * o + (half + 1))
        act.wait_ge(self.added, 2 * o + (half + 1))
        nc.scalar.activation(self.tmp[:, half], self.f[:, bass.ds(2 * o + half, 1)].rearrange("p o t -> p (o t)"),
                             ACT.Square).then_inc(self.squared, 1)

    def copy_tile(self, dve, nc, o, half, src):
        nc.vector.tensor_copy(self.f[:, bass.ds(2 * o + half, 1)].rearrange("p o t -> p (o t)"), src).then_inc(self.copied, 1)
        dve.wait_ge(self.copied, 2 * o + (half + 1))
        dve.sem_inc(self.drained[half], 1)

    def bank_free(self, pe, o, half):
        pe.wait_ge(self.drained[half], o + 1)

    def pool(self, pool, nc):
        pool.sem_inc(self.added, 2)
        nc.gpsimd.memset(self.norm.ss[:], 0.0).then_inc(self.zeroed, 1)
        pool.wait_ge(self.zeroed, 1)
        with pool.Fori(0, KD // 2) as o:
            for half in range(2):
                pool.wait_ge(self.squared, 2 * o + (half + 1))
                pool.wait_ge(self.added, 2 * o + (half + 2))
                nc.gpsimd.tensor_tensor(self.norm.ss[:], self.norm.ss[:], self.tmp[:, half], ALU.add).then_inc(self.added, 1)
        pool.wait_ge(self.x_in, 16)
        for k in range(KD):
            pool.wait_ge(self.scaled, k + 1)
            nc.gpsimd.tensor_tensor(self.x[:, k], self.x[:, k], self.f[:, k], ALU.add).then_inc(self.summed, 1)

    def tensor(self, pe, nc):
        pe.wait_ge(self.added, KD + 2)
        nc.tensor.matmul(self.norm.psum[:, 0:self.n], self.g.ones[:], self.norm.ss[:],
                         start=True, stop=True).then_inc(self.norm.total, 1)

    def scalar(self, act, nc, chain):
        self.norm.root(act, nc, chain)

    def vector(self, dve, nc, chain, gate):
        self.norm.mean_eps(dve, nc)
        self.norm.refine(dve, nc, chain)
        for k in range(KD):
            nc.vector.scalar_tensor_tensor(self.f[:, k], self.f[:, k], gate[:, k:k + 1], self.norm.r[:],
                                           ALU.mult, ALU.mult).then_inc(self.scaled, 1)

    def store(self, sp, c0):
        sp.wait_ge(self.summed, KD)
        sp.dma_start(self.view(c0), self.x).then_inc(self.out, 16)
        sp.wait_ge(self.out, 16)


def in_proj_stage(nc, g, m, layer, ci):
    c0, n = CHUNKS[ci]
    stream = 0 if ci == 0 else 1
    w_view = g.w_in[layer].rearrange("(k p) n -> p k n", p=P)
    QKV, QKVZX = 6, 12
    with Stage(nc, f"in{layer}{ci}") as st:
        psn = st.ps("psn", [P, 512])
        psd = st.ps("psd", [P, 512])
        psu = st.ps("psu", [P, 2, 512])
        pre = Prenorm(st, g, n, psn, 0)
        ring = WeightRing(st)
        rope, swap, turn, stage = (pre.sq[:, i:i + 2] for i in (0, 2, 4, 6))
        split_hi = st.sb("split_hi", [P, 2, n], F32R)
        split_lo = st.sb("split_lo", [P, 2, n])
        wdt = st.sb("wdt", [P, KD, P])
        wdt_hi = st.sb("wdt_hi", [P, KD, P], F32R)
        wdt_lo = st.sb("wdt_lo", [P, KD, P], F32R)
        rope_in, dt_in, dt_zero, dt_round, dt_split, dt_done, dt_out = (st.sem(x) for x in (
            "rope_in", "dt_in", "dt_zero", "dt_round", "dt_split", "dt_done", "dt_out"))
        drained = [st.sem(f"drained{s}") for s in range(2)]
        swapped, staged, turned, hi_made, lo_made = (st.sem(x) for x in ("swapped", "staged", "turned", "hi_made", "lo_made"))
        split_out = [st.sem(f"split_out{s}") for s in range(2)]
        stored = [st.sem(f"stored{s}") for s in range(2)]
        chain_v, chain_a = st.sem("chain_v"), st.sem("chain_a")
        shift = g.mod[:, stream, SH1 * KD:(SH1 + 1) * KD]
        scale = g.pre[:, 0, stream]
        block = st.block()

        @block.sync
        def _(sp):
            pre.load(sp, c0)
            sp.wait_ge(dt_zero, 1)
            for d in range(2):
                sp.dma_start(wdt[:, :, BWD * d:BWD * d + SH], w_view[:, :, DT0 + SH * d:DT0 + SH * (d + 1)]).then_inc(dt_in, 16)
            sp.wait_ge(pre.norm.summed, 1)
            sp.dma_start(rope, g.rope_d.rearrange("r p t -> p r t")[:, :, c0:c0 + n]).then_inc(rope_in, 16)
            for s in range(2):
                ring.load(sp, 0, s, w_view[:, :, s * P:(s + 1) * P])

            def store_split(v, s, dst):
                sp.wait_ge(lo_made, 2 * v + (s + 1))
                sp.dma_start(dst[0], split_hi[:, s].bitcast(F32)).then_inc(split_out[s], 16)
                sp.dma_start(dst[1], split_lo[:, s]).then_inc(split_out[s], 16)
            with sp.Fori(0, QK_TILES // 2) as v:
                for s in range(2):
                    ring.load(sp, v + 1, s, w_view[:, :, bass.ds((2 * v + (2 + s)) * P, P)])
                for s in range(2):
                    store_split(v, s, [g.qk_d[i, bass.ds(2 * v + s, 1), :, c0:c0 + n].rearrange("o p t -> p (o t)") for i in range(2)])
            for v in (4, 5):
                for s in range(2):
                    ring.load(sp, v + 1, s, w_view[:, :, (2 * v + 2 + s) * P:(2 * v + 3 + s) * P])
                for s in range(2):
                    sp.wait_ge(lo_made, 2 * v + s + 1)
                    for i, part in enumerate((split_hi[:, s].bitcast(F32), split_lo[:, s])):
                        sp.dma_start(g.v_d[i, 2 * (v - 4) + s, c0:c0 + n].rearrange("(t p) e -> p t e", p=P),
                                     part.rearrange("p (t e) -> p t e", e=P)).then_inc(split_out[s], 16)
            with sp.Fori(0, QKVZX - QKV - 1) as j:
                for s in range(2):
                    ring.load(sp, j + (QKV + 1), s, w_view[:, :, bass.ds((2 * j + (2 * QKV + 2 + s)) * P, P)])
                for s in range(2):
                    sp.wait_ge(staged, 2 * j + s + 1)
                    sp.dma_start(g.zx_d[bass.ds(2 * j + s, 1), :, c0:c0 + n].rearrange("o p t -> p (o t)"), stage[:, s]).then_inc(stored[s], 16)
            last = QKVZX - QKV - 1
            for s in range(2):
                sp.wait_ge(staged, 2 * last + s + 1)
                sp.dma_start(g.zx_d[2 * last + s, :, c0:c0 + n], stage[:, s]).then_inc(stored[s], 16)
            for s in range(2):
                sp.wait_ge(stored[s], 16 * (QKVZX - QKV) + 16)
                sp.wait_ge(split_out[s], 32 * QKV + 32)

        @block.gpsimd
        def _(pool):
            nc.gpsimd.memset(wdt[:], 0.0).then_inc(dt_zero, 1)

        @block.scalar
        def _(act):
            chain = Chain(act, chain_a)
            for s in range(2):
                act.sem_inc(stored[s], 16)
                act.sem_inc(split_out[s], 32)
            pre.scalar(act, nc, chain, shift)
            act.wait_ge(dt_in, 32)
            nc.scalar.activation(wdt_hi[:], wdt[:], ACT.Copy).then_inc(dt_round, 1)
            for s in range(2):
                ring.round(act, nc, 0, s)

            def swap_halves(v, s):
                act.wait_ge(ring.used, ring.count_used(v, s))
                for a in range(4):
                    b = a ^ 1
                    last = nc.scalar.activation(swap[32 * a:32 * a + 32, s], psu[32 * b:32 * b + 32, s, 0:n], ACT.Copy)
                last.then_inc(swapped, 1)

            with act.Fori(0, QK_TILES // 2) as v:
                for s in range(2):
                    swap_halves(v, s)
                    ring.round(act, nc, v + 1, s)
                    act.wait_ge(turned, 2 * v + (s + 1))
                    act.wait_ge(split_out[s], 32 * v + 32)
                    nc.scalar.activation(split_hi[:, s], turn[:, s], ACT.Copy).then_inc(hi_made, 1)
            for v in (4, 5):
                for s in range(2):
                    act.wait_ge(ring.used, ring.count_used(v, s))
                    act.wait_ge(split_out[s], 32 * v + 32)
                    nc.scalar.activation(split_hi[:, s], psu[:, s, 0:n], ACT.Copy).then_inc(hi_made, 1)
                    ring.round(act, nc, v + 1, s)
            for start, end, func in ((0, 2, ACT.Silu), (2, QKVZX - QKV - 1, ACT.Copy)):
                with act.Fori(start, end) as j:
                    for s in range(2):
                        act.wait_ge(ring.used, 2 * j + (2 * QKV + s + 3))
                        act.wait_ge(stored[s], 16 * j + 16)
                        nc.scalar.activation(stage[:, s], psu[:, s, 0:n], func).then_inc(staged, 1)
                        act.wait_ge(staged, 2 * j + (s + 1))
                        act.sem_inc(drained[s], 1)
                        ring.round(act, nc, j + (QKV + 1), s)
            last = QKVZX - QKV - 1
            for s in range(2):
                act.wait_ge(ring.used, ring.count_used(QKVZX - 1, s))
                act.wait_ge(stored[s], 16 * last + 16)
                nc.scalar.activation(stage[:, s], psu[:, s, 0:n], ACT.Copy).then_inc(staged, 1)
            act.wait_ge(dt_done, 1)
            nc.scalar.activation(m.dt[:, c0:c0 + n], psd[0:DTP, 0:n], ACT.Copy).then_inc(dt_out, 1)

        @block.vector
        def _(dve):
            chain = Chain(dve, chain_v)
            ring.start_vector(dve)
            for s in range(2):
                dve.sem_inc(drained[s], 1)
            pre.vector(dve, nc, chain, scale, shift)
            dve.wait_ge(dt_round, 1)
            nc.vector.tensor_tensor(wdt_lo[:], wdt[:], wdt_hi[:], ALU.subtract).then_inc(dt_split, 1)
            for s in range(2):
                ring.rest(dve, nc, 0, s)
            dve.wait_ge(rope_in, 16)
            with dve.Fori(0, QK_TILES // 2) as v, chain.over(v, QK_TILES // 2, 4):
                for s in range(2):
                    dve.wait_ge(swapped, 2 * v + s + 1)
                    chain(nc.vector.tensor_tensor(turn[:, s], psu[:, s, 0:n], rope[:, 0], ALU.mult))
                    chain(nc.vector.tensor_tensor(swap[:, s], swap[:, s], rope[:, 1], ALU.mult))
                    nc.vector.tensor_tensor(turn[:, s], turn[:, s], swap[:, s], ALU.add).then_inc(turned, 1)
                    dve.wait_ge(turned, 2 * v + (s + 1))
                    dve.sem_inc(drained[s], 1)
                    ring.rest(dve, nc, v + 1, s)
                    dve.wait_ge(hi_made, 2 * v + (s + 1))
                    nc.vector.tensor_tensor(split_lo[:, s], turn[:, s], split_hi[:, s], ALU.subtract).then_inc(lo_made, 1)
                    dve.wait_ge(lo_made, 2 * v + (s + 1))
            for v in (4, 5):
                for s in range(2):
                    dve.wait_ge(hi_made, 2 * v + s + 1)
                    nc.vector.tensor_tensor(split_lo[:, s], psu[:, s, 0:n], split_hi[:, s], ALU.subtract).then_inc(lo_made, 1)
                    dve.wait_ge(lo_made, 2 * v + s + 1)
                    dve.sem_inc(drained[s], 1)
                    ring.rest(dve, nc, v + 1, s)
            with dve.Fori(0, QKVZX - 1 - QKV) as v:
                for s in range(2):
                    ring.rest(dve, nc, v + (QKV + 1), s)

        @block.tensor
        def _(pe):
            ring.start_tensor(pe)
            pre.norm.add_partitions(pe, nc)
            for k in range(KD):
                pe.wait_ge(pre.ready, k + 1)

            def unit(v, s):
                ring.ready(pe, v, s)
                pe.wait_ge(drained[s], v + 1)

            def columns(v, s):
                unit(v, s)
                product3(nc, psu[:, s, 0:n], ring.hi[:, s], ring.lo[:, s], pre.hi, pre.lo, KD).then_inc(ring.used, 1)

            with pe.Fori(0, QK_TILES // 2) as v:
                for s in range(2):
                    columns(v, s)
            for v in (4, 5):
                for s in range(2):
                    unit(v, s)
                    for t in range(n // P):
                        tok = slice(t * P, (t + 1) * P)
                        last = product3(nc, psu[:, s, tok], pre.hi[:, :, tok], pre.lo[:, :, tok], ring.hi[:, s], ring.lo[:, s], KD)
                    last.then_inc(ring.used, 1)
            with pe.Fori(0, QKVZX - QKV) as j:
                for s in range(2):
                    pe.wait_ge(ring.split, 2 * j + (2 * QKV + s + 3))
                    pe.wait_ge(drained[s], j + (QKV + 1))
                    product3(nc, psu[:, s, 0:n], ring.hi[:, s], ring.lo[:, s], pre.hi, pre.lo, KD).then_inc(ring.used, 1)
            pe.wait_ge(dt_split, 1)
            product3(nc, psd[:, 0:n], wdt_hi, wdt_lo, pre.hi, pre.lo, KD).then_inc(dt_done, 1)


def out_proj_stage(nc, g, m, layer, ci):
    c0, n = CHUNKS[ci]
    stream = 0 if ci == 0 else 1
    w_view = g.w_out[layer].rearrange("(k p) n -> p k n", p=P)
    toks = slice(c0, c0 + n)
    with Stage(nc, f"out{layer}{ci}") as st:
        psn = st.ps("psn", [P, 4, 512])
        psq = st.ps("psq", [P, 512])
        psu = st.ps("psu", [P, 2, 512])
        ring = WeightRing(st)
        sq = st.sb("sq", [P, KD, n])
        hi = st.sb("hi", [P, KD, n], F32R)
        lo = st.sb("lo", [P, KD, n], F32R)
        f = st.sb("f", [P, KD, n])
        mean = st.sb("mean", [P, HEADS + 1, n])
        root = st.sb("root", [P, HEADS + 1, n])
        tmp = st.sb("tmp", [P, HEADS + 1, n])
        x = st.sb("x", [P, KD, n])
        res = Residual(st, g, n, psn[:, 0], f, x[:])
        squared, summed, totals, means, guesses = (st.sem(x) for x in ("squared", "summed", "totals", "means", "guesses"))
        scaled, rounded, ready = st.sem("scaled"), st.sem("rounded"), st.sem("ready")
        chain_v, chain_a = st.sem("chain_v"), st.sem("chain_a")
        block = st.block()

        def part(k):
            return m.att[:, k, toks] if k < HEADS else m.ssd[:, k - HEADS, toks]

        @block.sync
        def _(sp):
            res.load(sp, c0)
            with sp.Fori(0, KD // 2) as v:
                for s in range(2):
                    ring.load(sp, v, s, w_view[:, :, bass.ds((2 * v + s) * P, P)])
            res.store(sp, c0)

        @block.gpsimd
        def _(pool):
            res.pool(pool, nc)

        @block.scalar
        def _(act):
            chain = Chain(act, chain_a)
            nc.scalar.activation(sq[:, 0:HEADS], m.att[:, :, toks], ACT.Square).then_inc(squared, 1)
            nc.scalar.activation(sq[:, HEADS:KD], m.ssd[:, :, toks], ACT.Square).then_inc(squared, 1)
            act.wait_ge(means, 1)
            chain(nc.scalar.activation(root[:], mean[:], ACT.Ln))
            nc.scalar.activation(root[:], root[:], ACT.Exp, scale=-0.5).then_inc(guesses, 1)
            for k in range(KD):
                act.wait_ge(scaled, k + 1)
                nc.scalar.activation(hi[:, k], sq[:, k], ACT.Copy).then_inc(rounded, 1)
            for s in range(2):
                ring.round(act, nc, 0, s)
            def square_out(v, s):
                res.square_tile(act, nc, v, s)
            with act.Fori(0, KD // 2 - 1) as v:
                for s in range(2):
                    square_out(v, s)
                    ring.round(act, nc, v + 1, s)
            for s in range(2):
                square_out(KD // 2 - 1, s)
            res.scalar(act, nc, chain)

        @block.vector
        def _(dve):
            chain = Chain(dve, chain_v)
            ring.start_vector(dve)
            res.start_vector(dve)
            dve.wait_ge(squared, 2)
            nc.vector.tensor_reduce(tmp[:, HEADS], sq[:, HEADS:KD].rearrange("p k n -> p n k"), AX.X, ALU.add).then_inc(summed, 1)
            dve.wait_ge(totals, 1)
            nc.vector.tensor_scalar(mean[:, 0:HEADS], psn[:, :, 0:n], 1.0 / P, EPS, ALU.mult, ALU.add)
            nc.vector.tensor_scalar(mean[:, HEADS], psq[:, 0:n], 1.0 / SW, EPS, ALU.mult, ALU.add).then_inc(means, 1)
            dve.wait_ge(guesses, 1)
            chain(nc.vector.tensor_tensor(tmp[:], root[:], root[:], ALU.mult))
            chain(nc.vector.scalar_tensor_tensor(tmp[:], tmp[:], -0.5, mean[:], ALU.mult, ALU.mult))
            chain(nc.vector.scalar_tensor_tensor(root[:], tmp[:], 1.5, root[:], ALU.add, ALU.mult))

            def low(k):
                dve.wait_ge(scaled, k + 1)
                dve.wait_ge(rounded, k + 1)
                nc.vector.tensor_tensor(lo[:, k], sq[:, k], hi[:, k], ALU.subtract).then_inc(ready, 1)
            for k in range(KD):
                col = g.sub_col[:, 0:1] if k < HEADS else g.cols_b[:, ROW_SG + k - HEADS:ROW_SG + k - HEADS + 1]
                nc.vector.scalar_tensor_tensor(sq[:, k], part(k), col, root[:, min(k, HEADS)],
                                               ALU.mult, ALU.mult).then_inc(scaled, 1)
                if k:
                    low(k - 1)
            low(KD - 1)
            for s in range(2):
                ring.rest(dve, nc, 0, s)

            def copy_out(v, s):
                dve.wait_ge(ring.used, 2 * v + (s + 3))
                res.copy_tile(dve, nc, v, s, psu[:, s, 0:n])
            with dve.Fori(0, KD // 2 - 1) as v:
                for s in range(2):
                    copy_out(v, s)
                    ring.rest(dve, nc, v + 1, s)
            for s in range(2):
                copy_out(KD // 2 - 1, s)
            res.vector(dve, nc, chain, g.post[:, 0, stream])

        @block.tensor
        def _(pe):
            ring.start_tensor(pe)
            pe.wait_ge(squared, 2)
            for h in range(HEADS):
                nc.tensor.matmul(psn[:, h, 0:n], g.ones[:], sq[:, h], start=True, stop=True)
            pe.wait_ge(summed, 1)
            nc.tensor.matmul(psq[:, 0:n], g.ones[:], tmp[:, HEADS], start=True, stop=True).then_inc(totals, 1)
            pe.wait_ge(ready, KD)
            with pe.Fori(0, KD // 2) as v:
                for s in range(2):
                    ring.ready(pe, v, s)
                    res.bank_free(pe, v, s)
                    product3(nc, psu[:, s, 0:n], ring.hi[:, s], ring.lo[:, s], hi, lo, KD).then_inc(ring.used, 1)
            res.tensor(pe, nc)


def ffn_stage(nc, g, layer, ci):
    c0, n = CHUNKS[ci]
    stream = 0 if ci == 0 else 1
    w1 = g.w_ffn_in[layer].rearrange("(k p) n -> p k n", p=P)
    w2 = g.w_ffn_out[layer].rearrange("(k p) n -> p k n", p=P)
    KS = [(0, 8), (8, 8), (16, 6)]
    with Stage(nc, f"ffn{layer}{ci}") as st:
        psn = st.ps("psn", [P, 512])
        psu = st.ps("psu", [P, 2, 2, 512])
        psf = st.ps("psf", [P, 2, 512])
        pre = Prenorm(st, g, n, psn, 1)
        ring = WeightRing(st)
        a_hi = st.sb("a_hi", [P, KF, n], F32R)
        a_lo = st.sb("a_lo", [P, KF, n], F32R)
        sig = st.sb("sig", [P, 2, n])
        act_t = st.sb("act_t", [P, 2, n])
        res = Residual(st, g, n, psn, pre.sq, pre.x[:])
        chain_v, chain_a = st.sem("chain_v"), st.sem("chain_a")
        gated, multiplied, a_rounded, a_ready = st.sem("gated"), st.sem("multiplied"), st.sem("a_rounded"), st.sem("a_ready")
        shift = g.mod[:, stream, SH2 * KD:(SH2 + 1) * KD]
        scale = g.pre[:, 1, stream]
        block = st.block()
        DOWN = [(i // 3, KS[i % 3]) for i in range(6)]

        @block.sync
        def _(sp):
            pre.load(sp, c0)
            with sp.Fori(0, KF) as v:
                for s in range(2):
                    ring.load(sp, v, s, w1[:, :, bass.ds(v * P + s * DFF, P)])
            with sp.Fori(0, KD // 2) as o:
                for i, (half, (k0, nk)) in enumerate(DOWN):
                    ring.load(sp, 3 * o + (KF + i // 2), i % 2, w2[:, k0:k0 + nk, bass.ds((2 * o + half) * P, P)], nk)
            sp.wait_ge(pre.ready, KD)
            res.load(sp, c0)
            res.store(sp, c0)

        @block.gpsimd
        def _(pool):
            res.pool(pool, nc)

        @block.scalar
        def _(act):
            chain = Chain(act, chain_a)
            pre.scalar(act, nc, chain, shift)
            for s in range(2):
                ring.round(act, nc, 0, s)

            def gate(t, e):
                act.wait_ge(ring.used, 2 * t + 3)
                act.wait_ge(multiplied, t + 1)
                nc.scalar.activation(sig[:, e], psu[:, e, 0, 0:n], ACT.Silu).then_inc(gated, 1)

            def hidden_hi(t, e):
                act.wait_ge(multiplied, t + 3)
                nc.scalar.activation(a_hi[:, bass.ds(t, 1)].rearrange("p o t -> p (o t)"), act_t[:, e], ACT.Copy).then_inc(a_rounded, 1)
            with act.Fori(0, KF // 2) as w:
                for e in range(2):
                    gate(2 * w + e, e)
                    ring.round(act, nc, 2 * w + (e + 1), 0)
                    hidden_hi(2 * w + e, e)
                    ring.round(act, nc, 2 * w + (e + 1), 1)
            def round_(o, i):
                ring.round(act, nc, 3 * o + (KF + i // 2), i % 2, DOWN[i][1][1])

            def square_out(o, half):
                res.square_tile(act, nc, o, half)
            with act.Fori(0, KD // 2 - 1) as o:
                for i in (2, 3, 4, 5):
                    round_(o, i)
                square_out(o, 0)
                for i in (0, 1):
                    round_(o + 1, i)
                square_out(o, 1)
            for i in (2, 3, 4, 5):
                round_(KD // 2 - 1, i)
            square_out(KD // 2 - 1, 0)
            square_out(KD // 2 - 1, 1)
            res.scalar(act, nc, chain)

        @block.vector
        def _(dve):
            chain = Chain(dve, chain_v)
            ring.start_vector(dve)
            dve.sem_inc(multiplied, 2)
            res.start_vector(dve)
            pre.vector(dve, nc, chain, scale, shift)
            for s in range(2):
                ring.rest(dve, nc, 0, s)

            def hidden(t, e):
                dve.wait_ge(gated, t + 1)
                dve.wait_ge(ring.used, 2 * t + 4)
                nc.vector.tensor_tensor(act_t[:, e], sig[:, e], psu[:, e, 1, 0:n], ALU.mult).then_inc(multiplied, 1)

            def hidden_lo(t, e):
                dve.wait_ge(a_rounded, t + 1)
                nc.vector.tensor_tensor(a_lo[:, bass.ds(t, 1)].rearrange("p o t -> p (o t)"), act_t[:, e],
                                        a_hi[:, bass.ds(t, 1)].rearrange("p o t -> p (o t)"), ALU.subtract).then_inc(a_ready, 1)
                dve.wait_ge(a_ready, t + 1)
            with dve.Fori(0, KF // 2) as w:
                for e in range(2):
                    ring.rest(dve, nc, 2 * w + (e + 1), 0)
                    hidden(2 * w + e, e)
                    hidden_lo(2 * w + e, e)
                    ring.rest(dve, nc, 2 * w + (e + 1), 1)

            def copy_out(o, half):
                dve.wait_ge(ring.used, 6 * o + (2 * KF + 3 * half + 5))
                res.copy_tile(dve, nc, o, half, psf[:, half, 0:n])

            def rest(o, i):
                ring.rest(dve, nc, 3 * o + (KF + i // 2), i % 2, DOWN[i][1][1])
            with dve.Fori(0, KD // 2 - 1) as o:
                rest(o, 2)
                rest(o, 3)
                rest(o, 4)
                copy_out(o, 0)
                rest(o, 5)
                rest(o + 1, 0)
                rest(o + 1, 1)
                copy_out(o, 1)
            for i in (2, 3, 4):
                rest(KD // 2 - 1, i)
            copy_out(KD // 2 - 1, 0)
            rest(KD // 2 - 1, 5)
            copy_out(KD // 2 - 1, 1)
            res.vector(dve, nc, chain, g.post[:, 1, stream])

        @block.tensor
        def _(pe):
            ring.start_tensor(pe)
            pre.norm.add_partitions(pe, nc)
            for k in range(KD):
                pe.wait_ge(pre.ready, k + 1)
            with pe.Fori(0, KF // 2) as w:
                for e in range(2):
                    pe.wait_ge(multiplied, 2 * w + (e + 1))
                    for s in range(2):
                        ring.ready(pe, 2 * w + e, s)
                        product3(nc, psu[:, e, s, 0:n], ring.hi[:, s], ring.lo[:, s], pre.hi, pre.lo, KD).then_inc(ring.used, 1)
            pe.wait_ge(a_ready, KF)
            with pe.Fori(0, KD // 2) as o:
                for i, (half, (k0, nk)) in enumerate(DOWN):
                    pe.wait_ge(ring.split, 6 * o + (2 * KF + i + 3))
                    if i % 3 == 0:
                        res.bank_free(pe, o, half)
                    last = product3(nc, psf[:, half, 0:n], ring.hi[:, i % 2], ring.lo[:, i % 2],
                                    a_hi[:, k0:k0 + nk], a_lo[:, k0:k0 + nk], nk, i % 3 == 0, i % 3 == 2)
                    last.then_inc(ring.used, 1)
            res.tensor(pe, nc)


def attention_stage(nc, g, m, layer):
    tiles = [(t, CTX) for t in range(CTX // P)] if layer == 0 else []
    tiles += [(t, T) for t in range(CTX // P, NT)]
    n_tiles = len(tiles)
    groups = [(i, k, min(4, keys // P - k)) for i, (_, keys) in enumerate(tiles) for k in range(0, keys // P, 4)]
    of_tile = [[j for j, x in enumerate(groups) if x[0] == i] for i in range(n_tiles)]
    n_groups = len(groups)
    ES, GS = 3, 6
    with Stage(nc, f"att{layer}") as st:
        q = st.sb("q", [P, 2, T], F32R)
        k_hi = st.sb("k_hi", [P, 2, T], F32R)
        k_lo = st.sb("k_lo", [P, 2, T], F32R)
        v_hi = st.sb("v_hi", [P, NT, P], F32R)
        v_lo = st.sb("v_lo", [P, NT, P], F32R)
        e = st.sb("e", [P, ES, 2, T])
        pt = st.sb("pt", [P, GS, 4, P])
        pt_hi = st.sb("pt_hi", [P, GS, 4, P], F32R)
        pt_lo = st.sb("pt_lo", [P, GS, 4, P], F32R)
        diag = st.sb("diag", [P, ES, P])
        top = st.sb("top", [P, ES, 2])
        shift = st.sb("shift", [P, ES, 2])
        total = st.sb("total", [P, ES, 2])
        inv = st.sb("inv", [P, ES, 2])
        coef = st.sb("coef", [P, ES])
        ps_s = st.ps("ps_s", [P, 2, 3, 512])
        ps_t = st.ps("ps_t", [P, 4, P])
        ps_o = st.ps("ps_o", [P, 4, P])
        q_in, k_in, v_in = st.sem("q_in"), st.sem("k_in"), st.sem("v_in")
        scored, topped, shifted, exped, mixed, turned, copied, hi_made, lo_made, summed, out = (st.sem(x) for x in (
            "scored", "topped", "shifted", "exped", "mixed", "turned", "copied", "hi_made", "lo_made", "summed", "out"))
        chain_v = st.sem("chain_v")
        block = st.block()

        @block.sync
        def _(sp):
            def load_qk(h):
                for a in range(2):
                    rows = slice(64 * a, 64 * a + 64)
                    for part in range(2):
                        half = slice(64 * part, 64 * part + 64)
                        sp.dma_start(q[half, a].bitcast(F32), g.qk_d[part, bass.ds(h, 1), rows].rearrange("o p t -> p (o t)")).then_inc(q_in, 16)
                        for dst, which in ((k_hi, 0), (k_lo, 1)):
                            sp.dma_start(dst[half, a].bitcast(F32), g.qk_d[which, bass.ds(h + HEADS, 1), rows].rearrange("o p t -> p (o t)")).then_inc(k_in, 16)

            def load_v(h):
                for dst, part in ((v_hi, 0), (v_lo, 1)):
                    sp.dma_start(dst[:].bitcast(F32), g.v_d[part, bass.ds(h, 1)].rearrange("o (t p) e -> p (o t) e", p=P)).then_inc(v_in, 16)
            load_qk(0)
            load_v(0)
            with sp.Fori(1, HEADS) as h:
                sp.wait_ge(scored, 2 * n_tiles * h)
                load_qk(h)
                sp.wait_ge(summed, n_groups * h)
                load_v(h)

        @block.tensor
        def _(pe):
            with pe.Fori(0, HEADS) as h:
                pe.wait_ge(q_in, 64 * h + 64)
                pe.wait_ge(k_in, 128 * h + 128)

                def scores(i, a):
                    if i >= n_tiles:
                        return
                    t, keys = tiles[i]
                    pe.wait_ge(exped, 2 * n_tiles * h + (2 * i + a + 1))
                    for c in range(0, keys, 512):
                        w = min(512, keys - c)
                        nc.tensor.matmul(ps_s[:, a, c // 512, 0:w], q[:, a, t * P:(t + 1) * P], k_hi[:, a, c:c + w], start=True, stop=False)
                        last = nc.tensor.matmul(ps_s[:, a, c // 512, 0:w], q[:, a, t * P:(t + 1) * P], k_lo[:, a, c:c + w], start=False, stop=True)
                    last.then_inc(scored, 1)

                def transposes(j):
                    i, k0, nk = groups[j]
                    pe.wait_ge(mixed, n_tiles * h + (i + 1))
                    pe.wait_ge(copied, n_groups * h + (j + 1))
                    for x in range(nk):
                        last = nc.tensor.matmul(ps_t[:, x], e[:, i % ES, 1, (k0 + x) * P:(k0 + x + 1) * P], diag[:, i % ES], start=True, stop=True)
                    last.then_inc(turned, 1)

                def products(j):
                    i, k0, nk = groups[j]
                    pe.wait_ge(lo_made, n_groups * h + (j + 1))
                    if k0 == 0:
                        pe.wait_ge(out, n_tiles * h + (i + 1))
                    last = product3(nc, ps_o[:, 0], v_hi[:, k0:k0 + nk], v_lo[:, k0:k0 + nk], pt_hi[:, j % GS], pt_lo[:, j % GS], nk,
                                    k0 == 0, (k0 + nk) * P == tiles[i][1])
                    last.then_inc(summed, 1)

                scores(0, 0)
                scores(0, 1)
                pe.wait_ge(v_in, 32 * h + 32)
                for i in range(n_tiles):
                    scores(i + 1, 0)
                    scores(i + 1, 1)
                    late = list(of_tile[i - 1]) if i else []
                    for j in of_tile[i]:
                        transposes(j)
                        if late:
                            products(late.pop(0))
                    for j in late:
                        products(j)
                for j in of_tile[-1]:
                    products(j)

        @block.vector
        def _(dve):
            chain = Chain(dve, chain_v)
            with dve.Fori(0, HEADS) as h, chain.over(h, HEADS, 2 * n_tiles):
                def maximum(i, a):
                    if i >= n_tiles:
                        return
                    dve.wait_ge(scored, 2 * n_tiles * h + (2 * i + a + 1))
                    nc.vector.tensor_reduce(top[:, i % ES, a:a + 1], ps_s[:, a].rearrange("p c w -> p (c w)")[:, 0:tiles[i][1]],
                                            AX.X, ALU.max).then_inc(topped, 1)
                    dve.wait_ge(topped, 2 * n_tiles * h + (2 * i + a + 1))
                    nc.vector.tensor_scalar(shift[:, i % ES, a:a + 1], top[:, i % ES, a:a + 1], -0.125, None,
                                            ALU.mult).then_inc(shifted, 1)

                def mix(i):
                    keys, x = tiles[i][1], i % ES
                    dve.wait_ge(exped, 2 * n_tiles * h + (2 * i + 4))
                    chain(nc.vector.reciprocal(inv[:, x], total[:, x]))
                    chain(nc.vector.scalar_tensor_tensor(coef[:, x:x + 1], inv[:, x, 1:2], g.neg_lam[:], total[:, x, 0:1], ALU.mult, ALU.mult))
                    nc.vector.tensor_scalar(diag[:, x], g.ident[:], inv[:, x, 0:1], None, ALU.mult)
                    nc.vector.scalar_tensor_tensor(e[:, x, 1, 0:keys], e[:, x, 1, 0:keys], coef[:, x:x + 1],
                                                   e[:, x, 0, 0:keys], ALU.mult, ALU.add).then_inc(mixed, 1)

                def high(j):
                    dve.wait_ge(copied, n_groups * h + (j + 2))
                    nk = groups[j][2]
                    nc.vector.tensor_copy(pt_hi[:, j % GS, 0:nk], pt[:, j % GS, 0:nk]).then_inc(hi_made, 1)
                maximum(0, 0)
                maximum(0, 1)
                for i in range(n_tiles):
                    js = of_tile[i]
                    mix(i)
                    maximum(i + 1, 0)
                    maximum(i + 1, 1)
                    for j in js:
                        high(j)

        @block.gpsimd
        def _(pool):
            with pool.Fori(0, HEADS) as h:
                for j, (_, _, nk) in enumerate(groups):
                    pool.wait_ge(hi_made, n_groups * h + (j + 1))
                    nc.gpsimd.tensor_tensor(pt_lo[:, j % GS, 0:nk], pt[:, j % GS, 0:nk], pt_hi[:, j % GS, 0:nk], ALU.subtract).then_inc(lo_made, 1)

        @block.scalar
        def _(act):
            act.sem_inc(exped, 2)
            act.sem_inc(copied, 1)
            act.sem_inc(out, 1)
            with act.Fori(0, HEADS) as h:
                def exps(i, a):
                    if i >= n_tiles:
                        return
                    keys = tiles[i][1]
                    if i >= ES:
                        act.wait_ge(turned, n_groups * h + (of_tile[i - ES][-1] + 1))
                    act.wait_ge(shifted, 2 * n_tiles * h + (2 * i + a + 1))
                    nc.scalar.activation(e[:, i % ES, a, 0:keys], ps_s[:, a].rearrange("p c w -> p (c w)")[:, 0:keys], ACT.Exp,
                                         bias=shift[:, i % ES, a:a + 1], scale=0.125,
                                         accum_out=total[:, i % ES, a:a + 1]).then_inc(exped, 1)

                def copy_group(j):
                    nk = groups[j][2]
                    act.wait_ge(turned, n_groups * h + (j + 1))
                    if j >= GS:
                        act.wait_ge(summed, n_groups * h + (j - GS + 1))
                    nc.scalar.activation(pt[:, j % GS, 0:nk], ps_t[:, 0:nk], ACT.Copy).then_inc(copied, 1)

                def copy_out(i):
                    act.wait_ge(summed, n_groups * h + (of_tile[i][-1] + 1))
                    t = tiles[i][0]
                    nc.scalar.activation(m.att[:, bass.ds(h, 1), t * P:(t + 1) * P].rearrange("p o t -> p (o t)"), ps_o[:, 0],
                                         ACT.Copy).then_inc(out, 1)
                exps(0, 0)
                exps(0, 1)
                for i in range(n_tiles):
                    js = of_tile[i]
                    copy_group(js[0])
                    exps(i + 1, 0)
                    for j in js[1:2]:
                        copy_group(j)
                    exps(i + 1, 1)
                    for j in js[2:]:
                        copy_group(j)
                    if i:
                        copy_out(i - 1)
                copy_out(n_tiles - 1)


def scan_prep_stage(nc, g, layer, m):
    PAD = T + 6
    CONV_T = 8
    with Stage(nc, f"prep{layer}") as st:
        pad = st.sb("pad", [P, 2, PAD])
        taps = st.sb("taps", [P, 2, 6])
        acc = st.sb("acc", [P, 2, PAD - 4])
        cv = st.sb("cv", [P, 2, T])
        tok = st.sb("tok", [P, 2, NT, P])
        ps = st.ps("ps", [P, 2, 3, 4, P])
        psd = st.ps("psd", [P, 512])
        dt_t = st.sb("dt_t", [DTP, T])
        dta = st.sb("dta", [DTP, T])
        cum = st.sb("cum", [DTP, T])
        s1 = st.sb("s1", [DTP, T])
        s2 = st.sb("s2", [DTP, T])
        s3 = st.sb("s3", [DTP, T])
        reset = st.sb("reset", [DTP, T])
        dta_tok = st.sb("dta_tok", [P, NT, 2, SH])
        w_tok = st.sb("w_tok", [P, NT, 2, SH])
        pad_in = [st.sem(f"pad_in{s}") for s in range(2)]
        zeroed, tapped, first, summed, sig, done, turned, tok_done = (st.sem(x) for x in (
            "zeroed", "tapped", "first", "summed", "sig", "done", "turned", "tok_done"))
        cv_out = [st.sem(f"cv_out{s}") for s in range(2)]
        tok_out = [st.sem(f"tok_out{s}") for s in range(2)]
        reset_in, a_exp, dt_ready, dt_turned, dt_copied, tot, tot_copied, cum_out, acc_free = (st.sem(x) for x in (
            "reset_in", "a_exp", "dt_ready", "dt_turned", "dt_copied", "tot", "tot_copied", "cum_out", "acc_free"))
        chain_v, chain_a = st.sem("chain_v"), st.sem("chain_a")
        block = st.block()
        PAIRS = CONV_T // 2
        TURNED = 3

        @block.sync
        def _(sp):
            sp.dma_start(reset[:], g.reset_d).then_inc(reset_in, 16)
            sp.wait_ge(zeroed, 3)

            def load(v, s):
                sp.wait_ge(summed, 2 * v + (s + 1))
                src = g.zx_d[bass.ds(2 * v + (s + 4), 1)].rearrange("o p t -> p (o t)")
                sp.dma_start(pad[:, s, 2:2 + CTX], src[:, 0:CTX]).then_inc(pad_in[s], 16)
                sp.dma_start(pad[:, s, 4 + CTX:4 + T], src[:, CTX:T]).then_inc(pad_in[s], 16)
            for s in range(2):
                load(0, s)
            with sp.Fori(0, TURNED) as v:
                for s in range(2):
                    load(v + 1, s)
                for s in range(2):
                    sp.wait_ge(done, 2 * v + s + 1)
                    sp.dma_start(g.cv_d[bass.ds(2 * v + s, 1)].rearrange("o p t -> p (o t)"), cv[:, s]).then_inc(cv_out[s], 16)
                    sp.wait_ge(tok_done, 6 * v + (3 * s + 7))
                    sp.dma_start(g.tok_d.rearrange("c p f -> p c f")[:, :, bass.ds((2 * v + s) * P, P)], tok[:, s]).then_inc(tok_out[s], 16)
            for s in range(2):
                sp.wait_ge(done, 2 * TURNED + s + 1)
                sp.dma_start(g.cv_d[2 * TURNED + s], cv[:, s]).then_inc(cv_out[s], 16)
            sp.wait_ge(dt_ready, 1)
            for d in range(2):
                sp.dma_start(g.cum_d[SH * d:SH * d + SH, :], cum[BWD * d:BWD * d + SH, :]).then_inc(cum_out, 16)
            sp.wait_ge(cum_out, 32)
            for s in range(2):
                sp.wait_ge(cv_out[s], 16 * PAIRS + 16)
                sp.wait_ge(tok_out[s], 16 * TURNED + 16)

        @block.gpsimd
        def _(pool):
            for a, b in ((0, 2), (2 + CTX, 4 + CTX), (4 + T, 6 + T)):
                nc.gpsimd.memset(pad[:, :, a:b], 0.0).then_inc(zeroed, 1)

        @block.scalar
        def _(act):
            chain = Chain(act, chain_a)
            for s in range(2):
                act.sem_inc(cv_out[s], 16)
            act.wait_ge(acc_free, 1)
            nc.scalar.activation(s1[:], s1[:], ACT.Exp, scale=-1.0).then_inc(a_exp, 1)
            with act.Fori(0, PAIRS) as v:
                for s in range(2):
                    act.wait_ge(pad_in[s], 32 * v + 32)
                    act.wait_ge(tapped, 2 * v + s + 1)
                    nc.scalar.activation(acc[:, s], pad[:, s, 0:PAD - 4], ACT.Identity, bias=taps[:, s, 5:6],
                                         scale=taps[:, s, 0:1]).then_inc(first, 1)
                    act.wait_ge(summed, 2 * v + (s + 3))
                    act.wait_ge(cv_out[s], 16 * v + 16)
                    act.wait_ge(turned, 6 * v + (3 * s + 1))
                    nc.scalar.activation(cv[:, s, 0:CTX], acc[:, s, 0:CTX], ACT.Silu)
                    nc.scalar.activation(cv[:, s, CTX:T], acc[:, s, CTX + 2:T + 2], ACT.Silu).then_inc(done, 1)
            act.wait_ge(tot_copied, 1)
            chain(nc.scalar.activation(w_tok[:], w_tok[:], ACT.Exp))
            nc.scalar.activation(m.etot[:], m.etot[:], ACT.Exp).then_inc(a_exp, 1)

        @block.vector
        def _(dve):
            chain = Chain(dve, chain_v)
            dve.sem_inc(summed, 2)
            dve.sem_inc(tok_done, 4)
            for s in range(2):
                dve.sem_inc(tok_out[s], 16)
            chain(nc.vector.tensor_scalar(m.dt[:], m.dt[:], g.dt_bias[:], None, ALU.add))
            chain(nc.vector.tensor_scalar(s2[:], m.dt[:], -1.0, None, ALU.mult))
            nc.vector.tensor_tensor(s1[:], m.dt[:], s2[:], ALU.max).then_inc(acc_free, 1)
            dve.wait_ge(a_exp, 1)
            chain(nc.vector.tensor_scalar_add(s2[:], s1[:], 2.0))
            chain(nc.vector.reciprocal(s2[:], s2[:]))
            chain(nc.vector.tensor_tensor(s1[:], s1[:], s2[:], ALU.mult))
            chain(nc.vector.tensor_tensor(s2[:], s1[:], s1[:], ALU.mult))
            chain(nc.vector.tensor_scalar(s3[:], s2[:], 2.0 / 17, None, ALU.mult))
            for odd in (15, 13, 11, 9, 7, 5, 3):
                chain(nc.vector.scalar_tensor_tensor(s3[:], s3[:], 2.0 / odd, s2[:], ALU.add, ALU.mult))
            chain(nc.vector.scalar_tensor_tensor(s3[:], s3[:], 2.0, s1[:], ALU.add, ALU.mult))
            chain(nc.vector.scalar_tensor_tensor(dt_t[:], m.dt[:], 0.0, s3[:], ALU.max, ALU.add))
            chain(nc.vector.tensor_scalar(dta[:], dt_t[:], g.a_neg[:], None, ALU.mult))
            dve.wait_ge(reset_in, 16)
            chain(nc.vector.tensor_tensor_scan(cum[:], reset[:], dta[:], 0.0, ALU.mult, ALU.add))
            back = slice(BWD, DTP)
            ends = cum[back].rearrange("h (c t) -> h c t", t=P)[:, :, P - 1:P].broadcast_to([SH, NT, P])
            chain(nc.vector.tensor_tensor(s1[back].rearrange("h (c t) -> h c t", t=P), ends,
                                          dta[back].rearrange("h (c t) -> h c t", t=P), ALU.add))
            nc.vector.tensor_tensor(cum[back], s1[back], cum[back], ALU.subtract).then_inc(dt_ready, 1)
            for i, dst in ((0, m.dt_tok), (1, dta_tok), (2, m.cum_tok)):
                dve.wait_ge(dt_turned, i + 1)
                for d in range(2):
                    ins = nc.vector.tensor_copy(dst[:, :, d], psd[:, 0:NT * DTP].rearrange("p (c h) -> p c h", h=DTP)[
                        :, :, BWD * d:BWD * d + SH])
                ins.then_inc(dt_copied, 1)
            dve.wait_ge(tot, 1)
            totals = psd[:, 0:NT * 2 * SH].rearrange("p (c d h) -> p c d h", d=2, h=SH)
            nc.vector.tensor_copy(m.etot[:], totals)
            dve.wait_ge(dt_copied, 3)
            nc.vector.tensor_tensor(w_tok[:], totals, m.cum_tok[:], ALU.subtract).then_inc(tot_copied, 1)

            def tile(v, s):
                dve.wait_ge(first, 2 * v + (s + 1))
                for tap in range(1, 5):
                    ins = nc.vector.scalar_tensor_tensor(acc[:, s], pad[:, s, tap:tap + PAD - 4], taps[:, s, tap:tap + 1], acc[:, s],
                                                         ALU.mult, ALU.add)
                    if tap < 4:
                        chain(ins)
                    else:
                        ins.then_inc(summed, 1)

            def get_taps(v, s):
                col = bass.ds(2 * v + s, 1)
                chain(nc.vector.tensor_copy(taps[:, s, 0:5], g.cols_a[:, ROW_CW:ROW_CW + 40].rearrange("p (a t) -> p a t", t=CONV_T)[:, :, col].rearrange("p a o -> p (a o)")))
                nc.vector.tensor_copy(taps[:, s, 5:6], g.cols_a[:, ROW_CB:ROW_CB + CONV_T][:, col]).then_inc(tapped, 1)

            def copies(v, s):
                dve.wait_ge(tok_out[s], 16 * v + 16)
                for i in range(3):
                    k0, nk = 4 * i, min(4, NT - 4 * i)
                    dve.wait_ge(turned, 6 * v + (3 * s + i + 5))
                    nc.vector.tensor_copy(tok[:, s, k0:k0 + nk], ps[:, s, i, 0:nk]).then_inc(tok_done, 1)
            with dve.Fori(0, TURNED) as v, chain.over(v, TURNED, 8):
                for s in range(2):
                    get_taps(v, s)
                    tile(v, s)
                for s in range(2):
                    copies(v, s)
            for s in range(2):
                get_taps(TURNED, s)
                tile(TURNED, s)
            dve.wait_ge(a_exp, 2)
            nc.vector.tensor_tensor(m.w_tok[:], w_tok[:], m.dt_tok[:], ALU.mult)

        @block.tensor
        def _(pe):
            pe.sem_inc(turned, 4)
            pe.wait_ge(dt_ready, 1)
            for i, src in enumerate((dt_t, dta, cum)):
                pe.wait_ge(dt_copied, i) if i else None
                for c in range(NT):
                    last = nc.tensor.transpose(psd[:, c * DTP:(c + 1) * DTP], src[:, c * P:(c + 1) * P], g.ident[0:DTP, 0:DTP])
                last.then_inc(dt_turned, 1)
            pe.wait_ge(dt_copied, 3)
            nc.tensor.matmul(psd[:, 0:NT * 2 * SH], g.ones[:], dta_tok.rearrange("p c d h -> p (c d h)"), start=True, stop=True).then_inc(tot, 1)
            with pe.Fori(0, TURNED) as v:
                for s in range(2):
                    pe.wait_ge(done, 2 * v + s + 1)
                    pe.wait_ge(tok_done, 6 * v + (3 * s + 1))
                    for i in range(3):
                        for x in range(min(4, NT - 4 * i)):
                            c = 4 * i + x
                            last = nc.tensor.transpose(ps[:, s, i, x], cv[:, s, c * P:(c + 1) * P], g.ident[:])
                        last.then_inc(turned, 1)


def wait_if(eng, sem, value):
    if not isinstance(value, int) or value > 0:
        eng.wait_ge(sem, value)


def scan_state_stage(nc, g, m, layer):
    XB = SW + NG * P
    with Stage(nc, f"state{layer}") as st:
        tok = st.sb("tok", [P, 2, 2, XB])
        xw = st.sb("xw", [P, 2, 2, SW])
        h = st.sb("h", [P, 2, 2, SW])
        hd = st.sb("hd", [P, 2, 2, SW])
        ps = st.ps("ps", [P, 2, 2, SW])
        tok_in = [[st.sem(f"tok_in{d}{s}") for s in range(2)] for d in range(2)]
        weighted, pushed, updated, decayed = ([st.sem(f"{x}{d}") for d in range(2)] for x in ("weighted", "pushed", "updated", "decayed"))
        stored = [[st.sem(f"stored{d}{s}") for s in range(2)] for d in range(2)]
        zeroed = st.sem("zeroed")
        block = st.block()

        def steps(body, eng):
            for s in range(2):
                body(0, s, (s, 1 - s))
            down = eng.alloc_register(f"backward_chunk{layer}")
            eng.reg_mov(down, NT + 1)
            with eng.Fori(1, NT // 2) as v:
                eng.reg_sub(down, down, 2)
                back = eng.snap(down, min_val=3, max_val=NT - 1)
                for s in range(2):
                    body(v, s, (2 * v + s, back - s if s else back))

        @block.sync
        def _(sp):
            def body(v, s, c):
                for d in range(2):
                    wait_if(sp, pushed[d], 2 * v + (s - 1))
                    sp.dma_start(tok[:, d, s], g.tok_d[bass.ds(c[d], 1)].rearrange("o p f -> p (o f)")).then_inc(tok_in[d][s], 16)
                for d in range(2):
                    wait_if(sp, updated[d], 2 * v + s)
                    if isinstance(v, int) and s == 0:
                        sp.wait_ge(zeroed, 2)
                    sp.dma_start(g.h_d[d, bass.ds(c[d], 1)].rearrange("o p f -> p (o f)"), h[:, d, s]).then_inc(stored[d][s], 16)
            steps(body, sp)
            for d in range(2):
                for s in range(2):
                    sp.wait_ge(stored[d][s], 16 * (NT // 2))

        @block.gpsimd
        def _(pool):
            for d in range(2):
                nc.gpsimd.memset(h[:, d, 0], 0.0).then_inc(zeroed, 1)

            def body(v, s, c):
                for d in range(2):
                    pool.wait_ge(tok_in[d][s], 16 * v + 16)
                    wait_if(pool, pushed[d], 2 * v + (s - 1))
                    nc.gpsimd.tensor_tensor(xw[:, d, s].rearrange("p (h e) -> p h e", h=SH), tok[:, d, s, 0:SW].rearrange("p (h e) -> p h e", h=SH),
                                            m.w_tok[:, bass.ds(c[d], 1), d].rearrange("p o h -> p (o h)").unsqueeze(2).broadcast_to([P, SH, 64]),
                                            ALU.mult).then_inc(weighted[d], 1)
            steps(body, pool)

        @block.tensor
        def _(pe):
            def body(v, s, c):
                for d in range(2):
                    pe.wait_ge(weighted[d], 2 * v + (s + 1))
                    wait_if(pe, updated[d], 2 * v + (s - 1))
                    for q in range(NG):
                        w = SW // NG
                        last = nc.tensor.matmul(ps[:, d, s, q * w:(q + 1) * w], tok[:, d, s, SW + q * P:SW + (q + 1) * P],
                                                xw[:, d, s, q * w:(q + 1) * w], start=True, stop=True)
                    last.then_inc(pushed[d], 1)
            steps(body, pe)

        @block.vector
        def _(dve):
            def body(v, s, c):
                for d in range(2):
                    if isinstance(v, int) and s == 0:
                        dve.wait_ge(zeroed, 2)
                    wait_if(dve, updated[d], 2 * v + s)
                    nc.vector.tensor_tensor(hd[:, d, s].rearrange("p (h e) -> p h e", h=SH), h[:, d, s].rearrange("p (h e) -> p h e", h=SH),
                                            m.etot[:, bass.ds(c[d], 1), d].rearrange("p o h -> p (o h)").unsqueeze(2).broadcast_to([P, SH, 64]),
                                            ALU.mult).then_inc(decayed[d], 1)
                for d in range(2):
                    dve.wait_ge(decayed[d], 2 * v + (s + 1))
                    dve.wait_ge(pushed[d], 2 * v + (s + 1))
                    wait_if(dve, stored[d][1 - s], 16 * v + 16 * s)
                    nc.vector.tensor_tensor(h[:, d, 1 - s], hd[:, d, s], ps[:, d, s], ALU.add).then_inc(updated[d], 1)
            steps(body, dve)


def scan_out_stage(nc, g, m, layer):
    v0 = 0 if layer == 0 else 1
    n_v = NT // 2 - v0
    DH = 2 * SH
    with Stage(nc, f"scan{layer}") as st:
        cv = st.sb("cv", [P, 2, 8, P])
        z = st.sb("z", [P, 2, 4, P])
        xt = st.sb("xt", [P, 2, SW])
        h = st.sb("h", [P, 2, 2, SW])
        rows = st.sb("rows", [P, 2, DH, P])
        seg = st.sb("seg", [P, 2, DH, P])
        er = st.sb("er", [P, 2, DH, P])
        xdt = st.sb("xdt", [P, 2, 2, SW])
        cbm = st.sb("cbm", [P, 2, 2, NG, P])
        skip = st.sb("skip", [P, 2, 4, P])
        ps_c = st.ps("ps_c", [P, 2, 4, P])
        ps_y = st.ps("ps_y", [P, 2, 4, P])
        loaded = [st.sem(f"loaded{s}") for s in range(2)]
        rows_in = [st.sem(f"rows_in{s}") for s in range(2)]
        crossed, masked, clipped, diffed, decays, row_decays, c_scaled, x_scaled, intra, summed, skipped, added, gated = (st.sem(x) for x in (
            "crossed", "masked", "clipped", "diffed", "decays", "row_decays", "c_scaled", "x_scaled", "intra", "summed", "skipped", "added", "gated"))
        LOADS = 4
        block = st.block()

        def steps(body, eng):
            for s in range(2):
                body(0, s)
            with eng.Fori(1, n_v) as w:
                for s in range(2):
                    body(w, s)

        @block.sync
        def _(sp):
            def body(w, s):
                c = 2 * w + (2 * v0 + s)
                wait_if(sp, gated, 2 * w + (s - 1))
                toks = bass.ds(c * P, P)
                sp.dma_start(rows[:, s], g.cum_d[:, toks].unsqueeze(0).broadcast_to([P, DH, P])).then_inc(rows_in[s], 16)
                sp.dma_start(cv[:, s], g.cv_d.rearrange("t p k -> p t k")[:, :, toks]).then_inc(loaded[s], 16)
                sp.dma_start(xt[:, s], g.tok_d[bass.ds(c, 1), :, 0:SW].rearrange("o p f -> p (o f)")).then_inc(loaded[s], 16)
                sp.dma_start(h[:, s], g.h_d[:, bass.ds(c, 1)].rearrange("d o p f -> p d (o f)")).then_inc(loaded[s], 16)
                sp.dma_start(z[:, s], g.zx_d[0:4].rearrange("t p k -> p t k")[:, :, toks]).then_inc(loaded[s], 16)
            steps(body, sp)

        @block.tensor
        def _(pe):
            def body(w, s):
                pe.wait_ge(loaded[s], 16 * LOADS * w + 16 * LOADS)
                wait_if(pe, masked, 2 * w + (s - 1))
                for q in range(NG):
                    last = nc.tensor.matmul(ps_c[:, s, q], cv[:, s, 4 + q], cv[:, s, 6 + q], start=True, stop=True)
                last.then_inc(crossed, 1)
                pe.wait_ge(x_scaled, 2 * w + (s + 1))
                pe.wait_ge(c_scaled, 2 * w + (s + 1))
                pe.wait_ge(intra, 2 * w + (s + 1))
                wait_if(pe, added, 2 * w + (s - 1))
                for t in range(4):
                    for e in range(2):
                        hd = 2 * t + e
                        out = ps_y[64 * e:64 * e + 64, s, t]
                        cols = slice(64 * hd, 64 * hd + 64)
                        for d in range(2):
                            nc.tensor.matmul(out, xdt[:, s, d, cols], seg[:, s, SH * d + hd], start=d == 0, stop=False)
                            last = nc.tensor.matmul(out, h[:, s, d, cols], er[:, s, SH * d + hd], start=False, stop=d == 1)
                last.then_inc(summed, 1)
            steps(body, pe)

        @block.scalar
        def _(act):
            def body(w, s):
                act.wait_ge(rows_in[s], 16 * w + 16)
                wait_if(act, summed, 2 * w + (s - 1))
                nc.scalar.activation(er[:, s], rows[:, s], ACT.Exp).then_inc(row_decays, 1)
                act.wait_ge(diffed, 2 * w + (s + 1))
                nc.scalar.activation(seg[:, s], seg[:, s], ACT.Exp).then_inc(decays, 1)
            steps(body, act)

        @block.gpsimd
        def _(pool):
            def body(w, s):
                c = bass.ds(2 * w + (2 * v0 + s), 1)
                pool.wait_ge(loaded[s], 16 * LOADS * w + 16 * LOADS)
                wait_if(pool, summed, 2 * w + (s - 1))
                for d in range(2):
                    last = nc.gpsimd.tensor_tensor(xdt[:, s, d].rearrange("p (h e) -> p h e", h=SH), xt[:, s].rearrange("p (h e) -> p h e", h=SH),
                                                   m.dt_tok[:, c, d].rearrange("p o h -> p (o h)").unsqueeze(2).broadcast_to([P, SH, 64]), ALU.mult)
                last.then_inc(x_scaled, 1)
                pool.wait_ge(row_decays, 2 * w + (s + 1))
                for d in range(2):
                    view = er[:, s, SH * d:SH * d + SH].rearrange("p (q r) i -> p q r i", q=NG)
                    last = nc.gpsimd.tensor_tensor(view, view, cv[:, s, 6:8].unsqueeze(2).broadcast_to([P, NG, SH // NG, P]), ALU.mult)
                last.then_inc(c_scaled, 1)
            steps(body, pool)

        @block.vector
        def _(dve):
            def body(w, s):
                c = bass.ds(2 * w + (2 * v0 + s), 1)
                cum = m.cum_tok[:, c].rearrange("p o d h -> p (o d h)").unsqueeze(2).broadcast_to([P, DH, P])
                dve.wait_ge(rows_in[s], 16 * w + 16)
                wait_if(dve, summed, 2 * w + (s - 1))
                nc.vector.tensor_tensor(seg[:, s], rows[:, s], cum, ALU.min).then_inc(clipped, 1)
                dve.wait_ge(clipped, 2 * w + (s + 1))
                nc.vector.tensor_tensor(seg[:, s], seg[:, s], cum, ALU.subtract).then_inc(diffed, 1)
                dve.wait_ge(crossed, 2 * w + (s + 1))
                for d in range(2):
                    last = nc.vector.tensor_tensor(cbm[:, s, d], ps_c[:, s, 0:NG], g.masks[:, d].unsqueeze(1).broadcast_to([P, NG, P]), ALU.mult)
                last.then_inc(masked, 1)
                nc.vector.tensor_tensor(skip[:, s], cv[:, s, 0:4], g.dskip_b[:], ALU.mult).then_inc(skipped, 1)
                dve.wait_ge(masked, 2 * w + (s + 1))
                dve.wait_ge(decays, 2 * w + (s + 1))
                view = seg[:, s].rearrange("p (a r) i -> p a r i", r=SH // NG)
                nc.vector.tensor_tensor(view, view, cbm[:, s].rearrange("p d q i -> p (d q) i").unsqueeze(2).broadcast_to([P, 4, SH // NG, P]),
                                        ALU.mult).then_inc(intra, 1)
                dve.wait_ge(summed, 2 * w + (s + 1))
                dve.wait_ge(skipped, 2 * w + (s + 1))
                nc.vector.tensor_tensor(skip[:, s], skip[:, s], ps_y[:, s], ALU.add).then_inc(added, 1)
                dve.wait_ge(added, 2 * w + (s + 1))
                out = m.ssd[:, :, bass.ds((2 * w + (2 * v0 + s)) * P, P)]
                nc.vector.tensor_tensor(out, skip[:, s], z[:, s], ALU.mult).then_inc(gated, 1)
            steps(body, dve)


def output_stage(nc, g):
    tiles = LAT // P
    with Stage(nc, "output") as st:
        xt = st.sb("xt", [P, 2, KD, P])
        xtok = st.sb("xtok", [P, 2, KD, P])
        tp = st.ps("tp", [P, 2, KD, P])
        x_in = [st.sem(f"x_in{s}") for s in range(2)]
        stored = [st.sem(f"stored{s}") for s in range(2)]
        turned, copied = st.sem("turned"), st.sem("copied")
        block = st.block()

        @block.sync
        def _(sp):
            with sp.Fori(0, tiles // 2) as v:
                for s in range(2):
                    sp.wait_ge(turned, 2 * v + s + 1)
                    sp.dma_start(xt[:, s], g.xT.rearrange("(k p) t -> p k t", p=P)[:, :, bass.ds((2 * v + s) * P + CTX, P)]).then_inc(x_in[s], 16)

        @block.tensor
        def _(pe):
            pe.sem_inc(turned, 2)
            with pe.Fori(0, tiles // 2) as v:
                for s in range(2):
                    pe.wait_ge(x_in[s], 16 * v + 16)
                    pe.wait_ge(copied, 2 * v + s + 1)
                    for k in range(KD):
                        last = nc.tensor.transpose(tp[:, s, k], xt[:, s, k], g.ident[:])
                    last.then_inc(turned, 1)

        @block.vector
        def _(dve):
            dve.sem_inc(copied, 2)
            for s in range(2):
                dve.sem_inc(stored[s], 16)
            with dve.Fori(0, tiles // 2) as v:
                for s in range(2):
                    dve.wait_ge(turned, 2 * v + s + 3)
                    dve.wait_ge(stored[s], 16 * v + 16)
                    nc.vector.tensor_copy(xtok[:, s], tp[:, s]).then_inc(copied, 1)

        @block.scalar
        def _(act):
            with act.Fori(0, tiles // 2) as v:
                for s in range(2):
                    act.wait_ge(copied, 2 * v + s + 3)
                    act.dma_start(g.out[0, bass.ds((2 * v + s) * P, P), :].rearrange("p (k q) -> p k q", q=P), xtok[:, s]).then_inc(stored[s], 16)
            for s in range(2):
                act.wait_ge(stored[s], 16 * (tiles // 2 + 1))


class Names:
    pass


def backbone(nc, x_in, c, c_ctx, w_ada, b_ada, norm_g, w_in, conv_w, conv_b, a_log, dt_bias, d_skip,
             ssd_norm_g, diff_lambda, subln_g, w_out, w_ffn_in, w_ffn_out, ident, masks, rope, reset, out):
    g = Names()
    g.x_in, g.c, g.c_ctx, g.w_ada, g.b_ada, g.norm_g, g.w_in = x_in, c, c_ctx, w_ada, b_ada, norm_g, w_in
    g.conv_w, g.conv_b, g.a_log, g.dt_bias_d, g.d_skip = conv_w, conv_b, a_log, dt_bias, d_skip
    g.ssd_g, g.lam_d, g.sub_g, g.w_out, g.w_ffn_in, g.w_ffn_out = ssd_norm_g, diff_lambda, subln_g, w_out, w_ffn_in, w_ffn_out
    g.ident_d, g.masks_d, g.rope_d, g.reset_d, g.out = ident, masks, rope, reset, out
    g.xT = nc.dram_tensor("xT", [D_MODEL, T], F32).ap()
    g.zx_d = nc.dram_tensor("zx_d", [12, P, T], F32).ap()
    g.qk_d = nc.dram_tensor("qk_d", [2, QK_TILES, P, T], F32).ap()
    g.v_d = nc.dram_tensor("v_d", [2, HEADS, T, P], F32).ap()
    g.cv_d = nc.dram_tensor("cv_d", [8, P, T], F32).ap()
    g.tok_d = nc.dram_tensor("tok_d", [NT, P, SW + NG * P], F32).ap()
    g.cum_d = nc.dram_tensor("cum_d", [2 * SH, T], F32).ap()
    g.h_d = nc.dram_tensor("h_d", [2, NT, P, SW], F32).ap()
    with ExitStack() as ctx:
        def sb(name, shape):
            return ctx.enter_context(nc.sbuf_tensor(name, shape, F32))
        g.ident, g.masks, g.ones = sb("ident", [P, P]), sb("masks", [P, 2, P]), sb("ones", [P, P])
        g.cols_a, g.cols_b = sb("cols_a", [P, P]), sb("cols_b", [P, 21])
        g.mod, g.pre, g.post = sb("mod", [P, 2, 48]), sb("pre", [P, 2, 2, KD]), sb("post", [P, 2, 2, KD])
        g.a_neg, g.dt_bias = sb("a_neg", [DTP, 1]), sb("dt_bias", [DTP, 1])
        g.neg_lam, g.sub_col = sb("neg_lam", [P, 1]), sb("sub_col", [P, 1])
        g.dskip_b = sb("dskip_b", [P, 4, P])
        setup_stage(nc, g)
        for layer in range(2):
            ada_stage(nc, g, layer)
            chunks = range(3) if layer == 0 else range(1, 3)
            with ExitStack() as mixer:
                m = Names()

                def keep(stack, name, shape):
                    return stack.enter_context(nc.sbuf_tensor(f"{name}{layer}", shape, F32))
                m.dt = keep(mixer, "dt", [DTP, T])
                m.att = keep(mixer, "att", [P, HEADS, T])
                for ci in range(3):
                    in_proj_stage(nc, g, m, layer, ci)
                attention_stage(nc, g, m, layer)
                m.ssd = keep(mixer, "ssd", [P, 4, T])
                with ExitStack() as scan:
                    m.dt_tok, m.cum_tok, m.w_tok, m.etot = (keep(scan, x, [P, NT, 2, SH]) for x in ("dt_tok", "cum_tok", "w_tok", "etot"))
                    scan_prep_stage(nc, g, layer, m)
                    scan_state_stage(nc, g, m, layer)
                    scan_out_stage(nc, g, m, layer)
                for ci in chunks:
                    out_proj_stage(nc, g, m, layer, ci)
            for ci in chunks:
                ffn_stage(nc, g, layer, ci)
        output_stage(nc, g)


_INS = ["c", "c_ctx", "w_ada", "b_ada", "norm_g", "w_in", "conv_w", "conv_b", "a_log", "dt_bias", "d_skip",
        "ssd_norm_g", "diff_lambda", "subln_g", "w_out", "w_ffn_in", "w_ffn_out"]


def _constants():
    import numpy as np
    f = np.float32
    ident = np.eye(P, dtype=f)
    upper = np.triu(np.ones((P, P), f))
    masks = np.stack([upper, np.ascontiguousarray(upper.T)])
    row = np.repeat(np.arange(LAT // 64, dtype=f), 64)
    col = np.tile(np.arange(64, dtype=f), LAT // 64)
    inv = (f(10000.0) ** (-np.arange(16, dtype=f) / f(16))).astype(f)
    ang = np.concatenate([row[:, None] * inv, col[:, None] * inv], axis=-1).T
    cos, sin = np.cos(ang).astype(f), np.sin(ang).astype(f)
    rope = np.zeros((2, P, T), f)
    rope[0, :, 0:CTX] = 1.0
    rope[0, :, CTX:] = np.tile(cos, (4, 1))
    rope[1, :, CTX:] = np.concatenate([-sin, sin, -sin, sin])
    reset = np.ones((DTP, T), f)
    reset[:, ::P] = 0.0
    return {"ident": ident, "masks": masks, "rope": rope, "reset": reset}


def kernel(**inputs):
    import numpy as _np
    import concourse.bacc as _bacc
    from concourse import mybir as _mybir
    from concourse.bass_utils import run_bass_kernel_spmd as _run

    nc = _bacc.Bacc("TRN2", target_bir_lowering=False, num_devices=1)
    given = {"x_in": _np.concatenate([inputs["ctx"][0], inputs["x"][0]], axis=0)}
    given.update({name: inputs[name] for name in _INS})
    given.update(_constants())
    arrays, args = {}, []
    for name, a in given.items():
        a = _np.ascontiguousarray(a)
        arrays[f"in_{name}_dram"] = a
        args.append(nc.dram_tensor(f"in_{name}_dram", a.shape, _mybir.dt.from_np(a.dtype), kind="ExternalInput").ap())
    args.append(nc.dram_tensor("out_0_dram", (1, LAT, D_MODEL), F32, kind="ExternalOutput").ap())
    backbone(nc, *args)
    r = _run(nc, [arrays], core_ids=[0])
    return r.results[0]["out_0_dram"]
```

```python
from contextlib import ExitStack, contextmanager

import concourse.bass as bass
from concourse import mybir

F32 = mybir.dt.float32
F32R = mybir.dt.float32r
ALU = mybir.AluOpType
ACT = mybir.ActivationFunctionType
AX = mybir.AxisListType

P = 128
D_MODEL = 1024
KD = D_MODEL // P
CTX, LAT = 256, 1024
T = CTX + LAT
NT = T // P
HEADS = 4
SH = 8
SW = 512
NG = 2
DFF = 2816
KF = DFF // P
QK_TILES = 8
V_END = 1536
XBC0 = 2048
DT0 = 3072
IN_COLS = 3088
DTP = 40
BWD = 32
EPS = 1e-6
CHUNKS = [(0, 256), (256, 512), (768, 512)]
LAM_INIT = [0.2, 0.8 - 0.6 * 0.7408182206817179]
ROW_ADA, ROW_NG, ROW_CW, ROW_CB = 0, 48, 80, 120
ROW_SG, ROW_SUB, ROW_C = 0, 4, 5
SH1, SC1, G1, SH2, SC2, G2 = range(6)


class Chain:

    def __init__(self, eng, sem):
        self.eng, self.sem, self.n, self.off = eng, sem, 0, 0

    def __call__(self, ins):
        self.n += 1
        ins.then_inc(self.sem, 1)
        self.eng.wait_ge(self.sem, self.off + self.n)

    @contextmanager
    def over(self, i, count, per):
        start, self.off = self.n, i * per
        yield
        assert self.n - start == per, (self.n - start, per)
        self.n, self.off = start + per * count, 0


class Stage:

    def __init__(self, nc, name):
        self.nc, self.name, self.ctx, self.sems = nc, name, ExitStack(), []

    def __enter__(self):
        self.ctx.__enter__()
        return self

    def __exit__(self, *a):
        done = self.ctx.__exit__(*a)
        if a[0] is None:
            self.nc.clear_and_free_semaphores(self.sems)
            self.nc.all_engine_barrier()
        return done

    def sb(self, name, shape, dt=F32):
        return self.ctx.enter_context(self.nc.sbuf_tensor(f"{self.name}_{name}", shape, dt))

    def ps(self, name, shape):
        return self.ctx.enter_context(self.nc.psum_tensor(f"{self.name}_{name}", shape, F32))

    def sem(self, name):
        self.sems.append(self.nc.alloc_semaphore(f"{self.name}_{name}"))
        return self.sems[-1]

    def block(self):
        return self.ctx.enter_context(self.nc.Block())


class WeightRing:

    def __init__(self, st, tiles=KD, width=P):
        self.raw = st.sb("w_raw", [P, 2, tiles, width])
        self.hi = st.sb("w_hi", [P, 2, tiles, width], F32R)
        self.lo = st.sb("w_lo", [P, 2, tiles, width], F32R)
        self.landed = [st.sem(f"w_landed{s}") for s in range(2)]
        self.rounded, self.split, self.used = st.sem("w_rounded"), st.sem("w_split"), st.sem("w_used")

    def start_vector(self, dve):
        dve.sem_inc(self.split, 2)

    def start_tensor(self, pe):
        pe.sem_inc(self.used, 2)

    def load(self, sp, v, s, src, tiles=KD):
        sp.wait_ge(self.split, 2 * v + s + 1)
        sp.dma_start(self.raw[:, s, 0:tiles], src).then_inc(self.landed[s], 16)

    def round(self, act, nc, v, s, tiles=KD):
        act.wait_ge(self.landed[s], 16 * v + 16)
        act.wait_ge(self.used, 2 * v + s + 1)
        nc.scalar.activation(self.hi[:, s, 0:tiles], self.raw[:, s, 0:tiles], ACT.Copy).then_inc(self.rounded, 1)

    def rest(self, dve, nc, v, s, tiles=KD):
        dve.wait_ge(self.rounded, 2 * v + s + 1)
        nc.vector.tensor_tensor(self.lo[:, s, 0:tiles], self.raw[:, s, 0:tiles], self.hi[:, s, 0:tiles],
                                ALU.subtract).then_inc(self.split, 1)

    def ready(self, pe, v, s):
        pe.wait_ge(self.split, 2 * v + s + 3)

    def count_used(self, v, s):
        return 2 * v + s + 3


def product3(nc, out, w_hi, w_lo, x_hi, x_lo, tiles, first=True, last=True):
    for k in range(tiles):
        a, b = first and k == 0, last and k == tiles - 1
        nc.tensor.matmul(out, w_hi[:, k], x_hi[:, k], start=a, stop=False)
        nc.tensor.matmul(out, w_hi[:, k], x_lo[:, k], start=False, stop=False)
        ins = nc.tensor.matmul(out, w_lo[:, k], x_hi[:, k], start=False, stop=b)
    return ins


class RowNorm:

    def __init__(self, st, name, n, features, psum, ones, bufs):
        self.n, self.features, self.psum, self.ones = n, features, psum, ones
        self.ss, self.m, self.r = (bufs[:, i, 0:n] for i in range(3))
        self.total, self.mean, self.guess = (st.sem(f"{name}_{x}") for x in ("total", "mean", "guess"))

    def add_partitions(self, nc):
        nc.tensor.matmul(self.psum[:, 0:self.n], self.ones[:], self.ss, start=True, stop=True).then_inc(self.total, 1)

    def mean_eps(self, dve, nc):
        dve.wait_ge(self.total, 1)
        nc.vector.tensor_scalar(self.m, self.psum[:, 0:self.n], 1.0 / self.features, EPS,
                                ALU.mult, ALU.add).then_inc(self.mean, 1)

    def root(self, act, nc, chain):
        act.wait_ge(self.mean, 1)
        chain(nc.scalar.activation(self.r, self.m, ACT.Ln))
        nc.scalar.activation(self.r, self.r, ACT.Exp, scale=-0.5).then_inc(self.guess, 1)

    def refine(self, dve, nc, chain):
        dve.wait_ge(self.guess, 1)
        chain(nc.vector.tensor_tensor(self.ss, self.r, self.r, ALU.mult))
        chain(nc.vector.scalar_tensor_tensor(self.ss, self.ss, -0.5, self.m, ALU.mult, ALU.mult))
        chain(nc.vector.scalar_tensor_tensor(self.r, self.ss, 1.5, self.r, ALU.add, ALU.mult))


def setup_stage(nc, g):
    with Stage(nc, "setup") as st:
        xtok = st.sb("xtok", [P, 2, D_MODEL])
        xt = st.sb("xt", [P, 2, KD, P])
        tp = st.ps("tp", [P, 2, KD, P])
        const_in = st.sem("const_in")
        x_in = [st.sem(f"x_in{s}") for s in range(2)]
        turned, copied = st.sem("turned"), st.sem("copied")
        stored = [st.sem(f"stored{s}") for s in range(2)]
        block = st.block()

        @block.sync
        def _(sp):
            sp.dma_start(g.ident[:], g.ident_d).then_inc(const_in, 16)
            sp.dma_start(g.masks[:], g.masks_d.rearrange("d j i -> j d i")).then_inc(const_in, 16)
            with sp.Fori(0, NT // 2) as v:
                for s in range(2):
                    sp.wait_ge(turned, 2 * v + s + 1)
                    sp.dma_start(xtok[:, s], g.x_in[bass.ds((2 * v + s) * P, P), :]).then_inc(x_in[s], 16)

        @block.tensor
        def _(pe):
            pe.sem_inc(turned, 2)
            pe.wait_ge(const_in, 32)
            with pe.Fori(0, NT // 2) as v:
                for s in range(2):
                    pe.wait_ge(x_in[s], 16 * v + 16)
                    pe.wait_ge(copied, 2 * v + s + 1)
                    for k in range(KD):
                        last = nc.tensor.transpose(tp[:, s, k], xtok[:, s, k * P:(k + 1) * P], g.ident[:])
                    last.then_inc(turned, 1)

        @block.vector
        def _(dve):
            dve.sem_inc(copied, 2)
            nc.vector.memset(g.ones[:], 1.0)
            for s in range(2):
                dve.sem_inc(stored[s], 16)
            with dve.Fori(0, NT // 2) as v:
                for s in range(2):
                    dve.wait_ge(turned, 2 * v + s + 3)
                    dve.wait_ge(stored[s], 16 * v + 16)
                    nc.vector.tensor_copy(xt[:, s], tp[:, s]).then_inc(copied, 1)

        @block.scalar
        def _(act):
            with act.Fori(0, NT // 2) as v:
                for s in range(2):
                    act.wait_ge(copied, 2 * v + s + 3)
                    act.dma_start(g.xT.rearrange("(k p) t -> p k t", p=P)[:, :, bass.ds((2 * v + s) * P, P)],
                                  xt[:, s]).then_inc(stored[s], 16)
            for s in range(2):
                act.wait_ge(stored[s], 16 * (NT // 2 + 1))


def ada_stage(nc, g, layer):
    STEP = 512
    steps = 6 * D_MODEL // STEP
    sub = STEP // P
    with Stage(nc, f"ada{layer}") as st:
        rows_a = st.sb("rows_a", [P, P])
        rows_b = st.sb("rows_b", [21, P])
        lam_in = st.sb("lam_in", [P, 4, 64])
        lam_t = st.sb("lam_t", [P, 2, 64])
        skip_in = st.sb("skip_in", [P, SH])
        lam_s = st.sb("lam_s", [P, 2])
        silu_c = st.sb("silu_c", [P, KD, 2])
        e_c = st.sb("e_c", [P, 2 * KD])
        wa = st.sb("wa", [P, 2, KD, STEP])
        psv = st.ps("psv", [P, 2, P])
        row = st.sb("row", [2, 2, STEP])
        psr = st.ps("psr", [2, 2, 512])
        psm = st.ps("psm", [P, 2, 512])
        vec_in, lam_land = st.sem("vec_in"), st.sem("lam_land")
        wa_in = [st.sem(f"wa_in{s}") for s in range(2)]
        turned, cols_done, c_exp, c_silu = st.sem("turned"), st.sem("cols_done"), st.sem("c_exp"), st.sem("c_silu")
        columns = st.sem("columns")
        done, mod_done, lam_sum, lam_exp = st.sem("done"), st.sem("mod_done"), st.sem("lam_sum"), st.sem("lam_exp")
        a_land, a_exp = st.sem("a_land"), st.sem("a_exp")
        a_zero, row_done = st.sem("a_zero"), st.sem("row_done")
        chain_v = st.sem("chain_v")
        block = st.block()

        @block.sync
        def _(sp):
            for row, src in ((ROW_ADA, g.b_ada[layer].rearrange("(r q) -> r q", q=P)),
                             (ROW_NG, g.norm_g[layer].rearrange("v (r q) -> (v r) q", q=P)),
                             (ROW_CW, g.conv_w[layer].rearrange("v (r q) -> (v r) q", q=P)),
                             (ROW_CB, g.conv_b[layer].rearrange("(r q) -> r q", q=P))):
                sp.dma_start(rows_a[row:row + src.shape[0]], src).then_inc(vec_in, 16)
            for row, src in ((ROW_SG, g.ssd_g[layer].rearrange("(r q) -> r q", q=P)),
                             (ROW_SUB, g.sub_g[layer].rearrange("(r q) -> r q", q=P)),
                             (ROW_C, g.c_ctx.rearrange("(r q) -> r q", q=P)),
                             (ROW_C + KD, g.c.rearrange("b (r q) -> (b r) q", q=P))):
                sp.dma_start(rows_b[row:row + src.shape[0]], src).then_inc(vec_in, 16)
            with sp.Fori(0, steps // 2) as v:
                for s in range(2):
                    sp.wait_ge(done, 2 * v + s + 1)
                    sp.dma_start(wa[:, s], g.w_ada[layer].rearrange("(k p) n -> p k n", p=P)[
                        :, :, bass.ds((2 * v + s) * STEP, STEP)]).then_inc(wa_in[s], 16)

        @block.gpsimd
        def _(pool):
            nc.gpsimd.memset(g.a_neg[:], 0.0).then_inc(a_zero, 1)
            nc.gpsimd.memset(g.dt_bias[:], 0.0).then_inc(a_zero, 1)
            pool.wait_ge(a_zero, 2)
            for d in range(2):
                pool.dma_start(g.a_neg[BWD * d:BWD * d + SH, :], g.a_log[layer, d].rearrange("(h o) -> h o", o=1)).then_inc(a_land, 16)
                pool.dma_start(g.dt_bias[BWD * d:BWD * d + SH, :], g.dt_bias_d[layer, d].rearrange("(h o) -> h o", o=1)).then_inc(a_land, 16)
            pool.dma_start(skip_in[:], g.d_skip[layer:layer + 1].to_broadcast([P, SH])).then_inc(a_land, 16)
            pool.dma_start(lam_in[:], g.lam_d[layer:layer + 1].to_broadcast([P, 4, 64])).then_inc(lam_land, 16)
            pool.wait_ge(lam_land, 16)
            pool.wait_ge(a_land, 16 * 5)

        @block.tensor
        def _(pe):
            pe.sem_inc(done, 2)
            pe.wait_ge(row_done, 2)
            pe.wait_ge(vec_in, 16 * 8)
            nc.tensor.transpose(psv[:, 0], rows_a[:], g.ident[:])
            nc.tensor.transpose(psv[:, 1, 0:21], rows_b[:], g.ident[0:21, 0:21]).then_inc(turned, 1)
            pe.wait_ge(c_silu, 1)
            with pe.Fori(0, steps // 2) as v:
                for s in range(2):
                    pe.wait_ge(wa_in[s], 16 * v + 16)
                    pe.wait_ge(row_done, 2 * v + s + 1)
                    for k in range(KD):
                        last = nc.tensor.matmul(psr[:, s, 0:STEP], silu_c[:, k], wa[:, s, k], start=k == 0, stop=k == KD - 1)
                    last.then_inc(done, 1)
                    pe.wait_ge(row_done, 2 * v + s + 3)
                    pe.wait_ge(mod_done, 2 * v + s + 1)
                    for j in range(sub):
                        last = nc.tensor.matmul(psm[:, s, 2 * j:2 * j + 2], row[:, s, j * P:(j + 1) * P], g.ident[0:2, 0:2],
                                                start=True, stop=True)
                    last.then_inc(columns, 1)

        @block.scalar
        def _(act):
            act.sem_inc(row_done, 2)
            act.wait_ge(cols_done, 1)
            nc.scalar.activation(e_c[:], g.cols_b[:, ROW_C:ROW_C + 2 * KD], ACT.Exp, scale=-1.0).then_inc(c_exp, 1)
            act.wait_ge(a_land, 16 * 5)
            nc.scalar.activation(g.a_neg[:], g.a_neg[:], ACT.Exp).then_inc(a_exp, 1)
            act.wait_ge(lam_sum, 1)
            nc.scalar.activation(lam_s[:], lam_s[:], ACT.Exp).then_inc(lam_exp, 1)
            with act.Fori(0, steps // 2) as v:
                for s in range(2):
                    act.wait_ge(done, 2 * v + s + 3)
                    nc.scalar.activation(row[:, s], psr[:, s, 0:STEP], ACT.Copy).then_inc(row_done, 1)

        @block.vector
        def _(dve):
            chain = Chain(dve, chain_v)
            dve.sem_inc(mod_done, 2)
            dve.wait_ge(turned, 1)
            nc.vector.tensor_copy(g.cols_a[:], psv[:, 0])
            nc.vector.tensor_copy(g.cols_b[:], psv[:, 1, 0:21]).then_inc(cols_done, 1)
            dve.wait_ge(c_exp, 1)
            chain(nc.vector.tensor_scalar_add(e_c[:], e_c[:], 1.0))
            chain(nc.vector.reciprocal(e_c[:], e_c[:]))
            nc.vector.tensor_tensor(silu_c.rearrange("p k v -> p v k"), g.cols_b[:, ROW_C:ROW_C + 2 * KD].rearrange("p (v k) -> p v k", v=2),
                                    e_c.rearrange("p (v k) -> p v k", v=2), ALU.mult).then_inc(c_silu, 1)
            dve.wait_ge(a_exp, 1)
            chain(nc.vector.tensor_scalar(g.a_neg[:], g.a_neg[:], -1.0, None, ALU.mult))
            dve.wait_ge(lam_land, 16)
            pairs = lam_in.rearrange("p (a b) d -> p a b d", b=2)
            chain(nc.vector.tensor_tensor(lam_t[:], pairs[:, :, 0], pairs[:, :, 1], ALU.mult))
            nc.vector.tensor_reduce(lam_s[:], lam_t[:], AX.X, ALU.add).then_inc(lam_sum, 1)
            dve.wait_ge(lam_exp, 1)
            chain(nc.vector.tensor_tensor(g.neg_lam[:], lam_s[:, 1:2], lam_s[:, 0:1], ALU.subtract))
            chain(nc.vector.tensor_scalar_add(g.neg_lam[:], g.neg_lam[:], -LAM_INIT[layer]))
            chain(nc.vector.tensor_scalar(g.sub_col[:], g.cols_b[:, ROW_SUB:ROW_SUB + 1], 1.0 - LAM_INIT[layer], None, ALU.mult))
            for e in range(2):
                half = slice(64 * e, 64 * e + 64)
                chain(nc.vector.tensor_copy(g.dskip_b[half], skip_in[half].rearrange("p (t e) -> p t e", e=2)[:, :, e:e + 1].broadcast_to([64, 4, P])))
            with dve.Fori(0, steps // 2) as v:
                for s in range(2):
                    dve.wait_ge(columns, 2 * v + s + 1)
                    cols = bass.ds((2 * v + s) * sub, sub)
                    nc.vector.tensor_tensor(g.mod[:, :, cols], psm[:, s, 0:2 * sub].rearrange("p (j v) -> p v j", v=2),
                                            g.cols_a[:, cols].unsqueeze(1).broadcast_to([P, 2, sub]), ALU.add).then_inc(mod_done, 1)
            dve.wait_ge(mod_done, steps + 2)
            for which, scale, norm in ((0, SC1, 0), (1, SC2, 2)):
                chain(nc.vector.scalar_tensor_tensor(
                    g.pre[:, which], g.mod[:, :, scale * KD:(scale + 1) * KD], 1.0,
                    g.cols_a[:, ROW_NG + norm * KD:ROW_NG + (norm + 1) * KD].unsqueeze(1).broadcast_to([P, 2, KD]), ALU.add, ALU.mult))
            for which, gate, norm in ((0, G1, 1), (1, G2, 3)):
                chain(nc.vector.tensor_tensor(
                    g.post[:, which], g.mod[:, :, gate * KD:(gate + 1) * KD],
                    g.cols_a[:, ROW_NG + norm * KD:ROW_NG + (norm + 1) * KD].unsqueeze(1).broadcast_to([P, 2, KD]), ALU.mult))


class Prenorm:

    def __init__(self, st, g, name, n, psum, x, sq, norm_bufs, hi, lo):
        self.g, self.n = g, n
        self.x, self.sq, self.hi, self.lo = x[:, :, 0:n], sq[:, :, 0:n], hi[:, :, 0:n], lo[:, :, 0:n]
        self.x_in, self.squared, self.added, self.scaled, self.rounded, self.ready = (st.sem(f"{name}_{x}") for x in (
            "x_in", "squared", "added", "scaled", "h_rounded", "h_ready"))
        self.norm = RowNorm(st, name, n, D_MODEL, psum, g.ones, norm_bufs)

    def load(self, eng, c0):
        eng.dma_start(self.x, self.g.xT.rearrange("(k p) t -> p k t", p=P)[:, :, c0:c0 + self.n]).then_inc(self.x_in, 16)

    def square(self, act, nc, k):
        if k == 0:
            act.wait_ge(self.x_in, 16)
        if k >= 3:
            act.wait_ge(self.added, k - 2)
        nc.scalar.activation(self.sq[:, k % 2] if k else self.norm.ss, self.x[:, k], ACT.Square).then_inc(self.squared, 1)

    def add(self, eng, ops, k):
        eng.wait_ge(self.squared, k + 1)
        if k > 1:
            eng.wait_ge(self.added, k - 1)
        ops.tensor_tensor(self.norm.ss, self.norm.ss, self.sq[:, k % 2], ALU.add).then_inc(self.added, 1)

    def total(self, pe, nc):
        pe.wait_ge(self.added, KD - 1)
        self.norm.add_partitions(nc)

    def high(self, act, nc, k, shift):
        act.wait_ge(self.scaled, k + 1)
        nc.scalar.activation(self.hi[:, k], self.x[:, k], ACT.Identity, bias=shift[:, k:k + 1]).then_inc(self.rounded, 1)

    def scale(self, nc, k, scale):
        nc.vector.scalar_tensor_tensor(self.x[:, k], self.x[:, k], scale[:, k:k + 1], self.norm.r,
                                       ALU.mult, ALU.mult).then_inc(self.scaled, 1)

    def low(self, dve, nc, k, shift):
        dve.wait_ge(self.scaled, k + 1)
        dve.wait_ge(self.rounded, k + 1)
        nc.vector.scalar_tensor_tensor(self.lo[:, k], self.x[:, k], shift[:, k:k + 1], self.hi[:, k],
                                       ALU.add, ALU.subtract).then_inc(self.ready, 1)

    SCALAR_STEPS, VECTOR_STEPS = 5 + KD, 3 + KD

    def scalar_step(self, act, nc, chain, shift, i):
        if i < 4:
            self.square(act, nc, 2 * i)
            self.square(act, nc, 2 * i + 1)
        elif i == 4:
            self.norm.root(act, nc, chain)
        else:
            self.high(act, nc, i - 5, shift)

    def vector_step(self, dve, nc, chain, scale, shift, i):
        if i == 0:
            self.norm.mean_eps(dve, nc)
        elif i == 1:
            self.norm.refine(dve, nc, chain)
        else:
            if i < KD + 2:
                self.scale(nc, i - 2, scale)
            if i > 2:
                self.low(dve, nc, i - 3, shift)

    def scalar(self, act, nc, chain, shift):
        for i in range(self.SCALAR_STEPS):
            self.scalar_step(act, nc, chain, shift, i)

    def vector(self, dve, nc, chain, scale, shift):
        for k in range(1, KD):
            self.add(dve, nc.vector, k)
        for i in range(self.VECTOR_STEPS):
            self.vector_step(dve, nc, chain, scale, shift, i)


class Residual:

    def __init__(self, st, g, name, n, psum, f, x, tmp, norm_bufs):
        self.g, self.n, self.f, self.x, self.tmp = g, n, f[:, :, 0:n], x[:, :, 0:n], tmp[:, :, 0:n]
        self.x_in, self.scaled, self.summed, self.out, self.zeroed, self.squared, self.added, self.copied = (
            st.sem(f"{name}_{x}") for x in ("in", "scaled", "summed", "out", "zeroed", "squared", "added", "copied"))
        self.drained = [st.sem(f"{name}_drained{s}") for s in range(2)]
        self.norm = RowNorm(st, name, n, D_MODEL, psum, g.ones, norm_bufs)

    def view(self, c0):
        return self.g.xT.rearrange("(k p) t -> p k t", p=P)[:, :, c0:c0 + self.n]

    def load(self, eng, c0):
        eng.dma_start(self.x, self.view(c0)).then_inc(self.x_in, 16)

    def start_vector(self, dve):
        for s in range(2):
            dve.sem_inc(self.drained[s], 1)

    def square_tile(self, act, nc, o, half):
        act.wait_ge(self.copied, 2 * o + (half + 1))
        act.wait_ge(self.added, 2 * o + (half + 1))
        nc.scalar.activation(self.tmp[:, half], self.f[:, bass.ds(2 * o + half, 1)].rearrange("p o t -> p (o t)"),
                             ACT.Square).then_inc(self.squared, 1)

    def copy_tile(self, dve, nc, o, half, src):
        nc.vector.tensor_copy(self.f[:, bass.ds(2 * o + half, 1)].rearrange("p o t -> p (o t)"), src).then_inc(self.copied, 1)
        dve.wait_ge(self.copied, 2 * o + (half + 1))
        dve.sem_inc(self.drained[half], 1)

    def bank_free(self, pe, o, half):
        pe.wait_ge(self.drained[half], o + 1)

    def sum_squares(self, pool, nc):
        pool.sem_inc(self.added, 2)
        nc.gpsimd.memset(self.norm.ss, 0.0).then_inc(self.zeroed, 1)
        pool.wait_ge(self.zeroed, 1)
        with pool.Fori(0, KD // 2) as o:
            for half in range(2):
                pool.wait_ge(self.squared, 2 * o + (half + 1))
                pool.wait_ge(self.added, 2 * o + (half + 2))
                nc.gpsimd.tensor_tensor(self.norm.ss, self.norm.ss, self.tmp[:, half], ALU.add).then_inc(self.added, 1)

    def add(self, pool, nc):
        pool.wait_ge(self.x_in, 16)
        for k in range(KD):
            pool.wait_ge(self.scaled, k + 1)
            nc.gpsimd.tensor_tensor(self.x[:, k], self.x[:, k], self.f[:, k], ALU.add).then_inc(self.summed, 1)

    def tensor(self, pe, nc):
        pe.wait_ge(self.added, KD + 2)
        self.norm.add_partitions(nc)

    def scale(self, nc, gate):
        for k in range(KD):
            nc.vector.scalar_tensor_tensor(self.f[:, k], self.f[:, k], gate[:, k:k + 1], self.norm.r,
                                           ALU.mult, ALU.mult).then_inc(self.scaled, 1)

    def vector(self, dve, nc, chain, gate):
        self.norm.mean_eps(dve, nc)
        self.norm.refine(dve, nc, chain)
        self.scale(nc, gate)

    def store(self, eng, c0):
        eng.wait_ge(self.summed, KD)
        eng.dma_start(self.view(c0), self.x).then_inc(self.out, 16)
        eng.wait_ge(self.out, 16)


def in_proj_stage(nc, g, m, layer):
    N = CHUNKS[-1][1]
    C = len(CHUNKS)
    w_view = g.w_in[layer].rearrange("(k p) n -> p k n", p=P)
    QK, QKV, ALL = 4, 6, 12
    SPLIT, ZX = 2 * QKV, 2 * (ALL - QKV)
    SCALAR_AT = {0: (0,), 1: (1,), 2: (2,), 3: (3,), 5: (4,), 6: (5, 6), 7: (7, 8), 8: (9, 10), 9: (11, 12)}
    VECTOR_AT = {4: (0,), 5: (1,), 6: (2, 3), 7: (4, 5), 8: (6, 7), 9: (8, 9), 10: (10,)}
    TOTAL_AT = 2
    with Stage(nc, f"in{layer}") as st:
        psn = st.ps("psn", [P, 512])
        psd = st.ps("psd", [P, 512])
        psu = st.ps("psu", [P, 2, 512])
        x, sq, pre_bufs = st.sb("x", [P, KD, N]), st.sb("sq", [P, 2, N]), st.sb("pre_bufs", [P, 3, N])
        h_hi, h_lo = st.sb("h_hi", [P, 2, KD, N], F32R), st.sb("h_lo", [P, 2, KD, N], F32R)
        pres = [Prenorm(st, g, f"pre{i}", n, psn, x, sq, pre_bufs, h_hi[:, i % 2], h_lo[:, i % 2]) for i, (_, n) in enumerate(CHUNKS)]
        ring = WeightRing(st)
        rope, swap, turn, stage = (st.sb(x, [P, 2, N]) for x in ("rope", "swap", "turn", "stage"))
        split_hi = st.sb("split_hi", [P, 2, N], F32R)
        split_lo = st.sb("split_lo", [P, 2, N])
        wdt = st.sb("wdt", [P, KD, P])
        wdt_hi = st.sb("wdt_hi", [P, KD, P], F32R)
        wdt_lo = st.sb("wdt_lo", [P, KD, P], F32R)
        rope_in, dt_in, dt_zero, dt_round, dt_split, dt_done, dt_out = (st.sem(x) for x in (
            "rope_in", "dt_in", "dt_zero", "dt_round", "dt_split", "dt_done", "dt_out"))
        drained = [st.sem(f"drained{s}") for s in range(2)]
        swapped, cos_made, sin_made, turned, hi_made, lo_made, v_hi, v_lo, staged = (st.sem(x) for x in (
            "swapped", "cos_made", "sin_made", "turned", "hi_made", "lo_made", "v_hi", "v_lo", "staged"))
        split_out = [st.sem(f"split_out{s}") for s in range(2)]
        stored = [st.sem(f"stored{s}") for s in range(2)]
        chain_v, chain_a = st.sem("chain_v"), st.sem("chain_a")
        streams = [0 if i == 0 else 1 for i in range(C)]
        shifts = [g.mod[:, s, SH1 * KD:(SH1 + 1) * KD] for s in streams]
        scales = [g.pre[:, 0, s] for s in streams]
        block = st.block()

        @block.sync
        def _(sp):
            sp.wait_ge(dt_zero, 1)
            for d in range(2):
                sp.dma_start(wdt[:, :, BWD * d:BWD * d + SH], w_view[:, :, DT0 + SH * d:DT0 + SH * (d + 1)]).then_inc(dt_in, 16)

            def load_rope(i):
                c0, n = CHUNKS[i]
                sp.dma_start(rope[:, :, 0:n], g.rope_d.rearrange("r p t -> p r t")[:, :, c0:c0 + n]).then_inc(rope_in, 16)
            for v in range(2):
                for s in range(2):
                    ring.load(sp, v, s, w_view[:, :, (2 * v + s) * P:(2 * v + s + 1) * P])
                if v == 0:
                    load_rope(0)
            for i, (c0, n) in enumerate(CHUNKS):
                with sp.Fori(0, QK) as v:
                    for s in range(2):
                        ring.load(sp, v + (ALL * i + 2), s, w_view[:, :, bass.ds((2 * v + (4 + s)) * P, P)])
                        sp.wait_ge(lo_made, 2 * v + (2 * QK * i + s + 1))
                        for part, src in enumerate((split_hi[:, s, 0:n].bitcast(F32), split_lo[:, s, 0:n])):
                            sp.dma_start(g.qk_d[part, bass.ds(2 * v + s, 1), :, c0:c0 + n].rearrange("o p t -> p (o t)"),
                                         src).then_inc(split_out[s], 16)
                for v in range(QK, QKV):
                    for s in range(2):
                        ring.load(sp, ALL * i + v + 2, s, w_view[:, :, (2 * v + 4 + s) * P:(2 * v + 5 + s) * P])
                        sp.wait_ge(v_lo, 2 * (QKV - QK) * i + 2 * (v - QK) + s + 1)
                        for part, src in enumerate((split_hi[:, s, 0:n].bitcast(F32), split_lo[:, s, 0:n])):
                            sp.dma_start(g.v_d[part, 2 * (v - QK) + s, c0:c0 + n].rearrange("(t p) e -> p t e", p=P),
                                         src.rearrange("p (t e) -> p t e", e=P)).then_inc(split_out[s], 16)
                if i + 1 < C:
                    load_rope(i + 1)

                def store(j, s):
                    sp.wait_ge(staged, 2 * j + (ZX * i + s + 1))
                    sp.dma_start(g.zx_d[bass.ds(2 * j + s, 1), :, c0:c0 + n].rearrange("o p t -> p (o t)"),
                                 stage[:, s, 0:n]).then_inc(stored[s], 16)
                with sp.Fori(0, ALL - QKV - 2) as j:
                    for s in range(2):
                        ring.load(sp, j + (ALL * i + QKV + 2), s, w_view[:, :, bass.ds((2 * j + (2 * QKV + 4 + s)) * P, P)])
                        store(j, s)
                for v in range(2):
                    for s in range(2):
                        if i + 1 < C:
                            ring.load(sp, ALL * (i + 1) + v, s, w_view[:, :, (2 * v + s) * P:(2 * v + s + 1) * P])
                        store(ALL - QKV - 2 + v, s)
            for s in range(2):
                sp.wait_ge(stored[s], 16 + 16 * C * ZX // 2)
                sp.wait_ge(split_out[s], 32 + 32 * C * SPLIT // 2)

        @block.gpsimd
        def _(pool):
            pres[0].load(pool, CHUNKS[0][0])
            nc.gpsimd.memset(wdt[:], 0.0).then_inc(dt_zero, 1)
            for i, (c0, n) in enumerate(CHUNKS):
                pool.wait_ge(pres[i].ready, KD)
                if i + 1 < C:
                    pres[i + 1].load(pool, CHUNKS[i + 1][0])
                pool.wait_ge(rope_in, 16 * i + 16)
                with pool.Fori(0, QK) as v:
                    for s in range(2):
                        pool.wait_ge(swapped, 2 * v + (2 * QK * i + s + 1))
                        nc.gpsimd.tensor_tensor(swap[:, s, 0:n], swap[:, s, 0:n], rope[:, 1, 0:n], ALU.mult).then_inc(sin_made, 1)
                        pool.wait_ge(hi_made, 2 * v + (2 * QK * i + s + 1))
                        nc.gpsimd.tensor_tensor(split_lo[:, s, 0:n], turn[:, s, 0:n], split_hi[:, s, 0:n], ALU.subtract).then_inc(lo_made, 1)
                if i + 1 < C:
                    for k in range(1, KD):
                        pres[i + 1].add(pool, nc.gpsimd, k)

        @block.scalar
        def _(act):
            chain = Chain(act, chain_a)
            for s in range(2):
                act.sem_inc(stored[s], 16)
                act.sem_inc(split_out[s], 32)
            pres[0].scalar(act, nc, chain, shifts[0])
            for s in range(2):
                ring.round(act, nc, 0, s)
            act.wait_ge(dt_in, 32)
            nc.scalar.activation(wdt_hi[:], wdt[:], ACT.Copy).then_inc(dt_round, 1)
            for i, (c0, n) in enumerate(CHUNKS):
                with act.Fori(0, QK) as v:
                    for s in range(2):
                        ring.round(act, nc, v + (ALL * i + 1), s)
                        act.wait_ge(turned, 2 * v + (2 * QK * i + s + 1))
                        for a in range(4):
                            b = a ^ 1
                            last = nc.scalar.activation(swap[32 * a:32 * a + 32, s, 0:n], psu[32 * b:32 * b + 32, s, 0:n], ACT.Copy)
                        last.then_inc(swapped, 1)
                for v in range(QK, QKV):
                    for s in range(2):
                        ring.round(act, nc, ALL * i + v + 1, s)
                        act.wait_ge(split_out[s], 32 * (SPLIT // 2 * i + v) + 32)
                        nc.scalar.activation(split_hi[:, s, 0:n], psu[:, s, 0:n], ACT.Copy).then_inc(v_hi, 1)

                def unit(j, s, func, more=True):
                    if more:
                        ring.round(act, nc, j + (ALL * i + QKV + 1), s)
                    act.wait_ge(ring.used, 2 * j + (2 * (ALL * i + QKV) + s + 3))
                    act.wait_ge(stored[s], 16 * j + (16 * ZX // 2 * i + 16))
                    nc.scalar.activation(stage[:, s, 0:n], psu[:, s, 0:n], func).then_inc(staged, 1)
                    act.wait_ge(staged, 2 * j + (ZX * i + s + 1))
                    act.sem_inc(drained[s], 1)
                if i + 1 < C:
                    for j in range(ALL - QKV):
                        for s in range(2):
                            unit(j, s, ACT.Silu if j < 2 else ACT.Copy)
                            for step in SCALAR_AT.get(2 * j + s, ()):
                                pres[i + 1].scalar_step(act, nc, chain, shifts[i + 1], step)
                else:
                    for start, end, func in ((0, 2, ACT.Silu), (2, ALL - QKV - 1, ACT.Copy)):
                        with act.Fori(start, end) as j:
                            for s in range(2):
                                unit(j, s, func)
                    for s in range(2):
                        unit(ALL - QKV - 1, s, ACT.Copy, False)
                act.wait_ge(dt_done, i + 1)
                nc.scalar.activation(m.dt[:, c0:c0 + n], psd[0:DTP, 0:n], ACT.Copy).then_inc(dt_out, 1)

        @block.vector
        def _(dve):
            chain = Chain(dve, chain_v)
            ring.start_vector(dve)
            dve.sem_inc(turned, 2)
            for s in range(2):
                dve.sem_inc(drained[s], 1)
            pres[0].vector(dve, nc, chain, scales[0], shifts[0])
            for s in range(2):
                ring.rest(dve, nc, 0, s)
            dve.wait_ge(dt_round, 1)
            nc.vector.tensor_tensor(wdt_lo[:], wdt[:], wdt_hi[:], ALU.subtract).then_inc(dt_split, 1)
            for i, (c0, n) in enumerate(CHUNKS):
                dve.wait_ge(rope_in, 16 * i + 16)
                with dve.Fori(0, QK) as v:
                    for s in range(2):
                        ring.rest(dve, nc, v + (ALL * i + 1), s)
                        dve.wait_ge(swapped, 2 * v + (2 * QK * i + s + 1))
                        dve.wait_ge(split_out[s], 32 * v + (32 * SPLIT // 2 * i + 32))
                        nc.vector.tensor_tensor(turn[:, s, 0:n], psu[:, s, 0:n], rope[:, 0, 0:n], ALU.mult).then_inc(cos_made, 1)
                        dve.wait_ge(cos_made, 2 * v + (2 * QK * i + s + 1))
                        dve.sem_inc(drained[s], 1)
                        dve.wait_ge(sin_made, 2 * v + (2 * QK * i + s + 1))
                        nc.vector.tensor_tensor(turn[:, s, 0:n], turn[:, s, 0:n], swap[:, s, 0:n], ALU.add).then_inc(turned, 1)
                        dve.wait_ge(turned, 2 * v + (2 * QK * i + s + 3))
                        nc.vector.tensor_copy(split_hi[:, s, 0:n], turn[:, s, 0:n]).then_inc(hi_made, 1)
                for v in range(QK, QKV):
                    for s in range(2):
                        ring.rest(dve, nc, ALL * i + v + 1, s)
                        dve.wait_ge(v_hi, 2 * (QKV - QK) * i + 2 * (v - QK) + s + 1)
                        nc.vector.tensor_tensor(split_lo[:, s, 0:n], psu[:, s, 0:n], split_hi[:, s, 0:n], ALU.subtract).then_inc(v_lo, 1)
                        dve.wait_ge(v_lo, 2 * (QKV - QK) * i + 2 * (v - QK) + s + 1)
                        dve.sem_inc(drained[s], 1)
                if i + 1 < C:
                    for j in range(ALL - QKV):
                        for s in range(2):
                            ring.rest(dve, nc, ALL * i + QKV + 1 + j, s)
                            for step in VECTOR_AT.get(2 * j + s, ()):
                                pres[i + 1].vector_step(dve, nc, chain, scales[i + 1], shifts[i + 1], step)
                else:
                    with dve.Fori(0, ALL - QKV - 1) as j:
                        for s in range(2):
                            ring.rest(dve, nc, j + (ALL * i + QKV + 1), s)

        @block.tensor
        def _(pe):
            ring.start_tensor(pe)
            pres[0].total(pe, nc)
            for i, (c0, n) in enumerate(CHUNKS):
                hi, lo = h_hi[:, i % 2, :, 0:n], h_lo[:, i % 2, :, 0:n]
                pe.wait_ge(pres[i].ready, KD)

                def unit(v, s):
                    ring.ready(pe, v + ALL * i, s)
                    pe.wait_ge(drained[s], v + (ALL * i + 1))

                def columns(v, s):
                    unit(v, s)
                    product3(nc, psu[:, s, 0:n], ring.hi[:, s], ring.lo[:, s], hi, lo, KD).then_inc(ring.used, 1)

                with pe.Fori(0, QK) as v:
                    for s in range(2):
                        columns(v, s)
                for v in range(QK, QKV):
                    for s in range(2):
                        unit(v, s)
                        for t in range(n // P):
                            tok = slice(t * P, (t + 1) * P)
                            last = product3(nc, psu[:, s, tok], hi[:, :, tok], lo[:, :, tok], ring.hi[:, s], ring.lo[:, s], KD)
                        last.then_inc(ring.used, 1)
                for start, end in ((QKV, QKV + TOTAL_AT), (QKV + TOTAL_AT, ALL)):
                    with pe.Fori(start, end) as v:
                        for s in range(2):
                            columns(v, s)
                    if end < ALL and i + 1 < C:
                        pres[i + 1].total(pe, nc)
                pe.wait_ge(dt_split, 1)
                if i:
                    pe.wait_ge(dt_out, i)
                product3(nc, psd[:, 0:n], wdt_hi, wdt_lo, hi, lo, KD).then_inc(dt_done, 1)


def out_proj_stage(nc, g, m, layer, ci):
    c0, n = CHUNKS[ci]
    stream = 0 if ci == 0 else 1
    w_view = g.w_out[layer].rearrange("(k p) n -> p k n", p=P)
    toks = slice(c0, c0 + n)
    with Stage(nc, f"out{layer}{ci}") as st:
        psn = st.ps("psn", [P, 4, 512])
        psq = st.ps("psq", [P, 512])
        psu = st.ps("psu", [P, 2, 512])
        ring = WeightRing(st)
        sq = st.sb("sq", [P, KD, n])
        hi = st.sb("hi", [P, KD, n], F32R)
        lo = st.sb("lo", [P, KD, n], F32R)
        f = st.sb("f", [P, KD, n])
        mean = st.sb("mean", [P, HEADS + 1, n])
        root = st.sb("root", [P, HEADS + 1, n])
        tmp = st.sb("tmp", [P, HEADS + 1, n])
        x = st.sb("x", [P, KD, n])
        res_tmp, post_bufs = st.sb("res_tmp", [P, 2, n]), st.sb("post_bufs", [P, 3, n])
        res = Residual(st, g, "res", n, psn[:, 0], f, x, res_tmp, post_bufs)
        squared, summed, totals, means, guesses = (st.sem(x) for x in ("squared", "summed", "totals", "means", "guesses"))
        scaled, rounded, ready = st.sem("scaled"), st.sem("rounded"), st.sem("ready")
        chain_v, chain_a = st.sem("chain_v"), st.sem("chain_a")
        block = st.block()

        def part(k):
            return m.att[:, k, toks] if k < HEADS else m.ssd[:, k - HEADS, toks]

        @block.sync
        def _(sp):
            res.load(sp, c0)
            with sp.Fori(0, KD // 2) as v:
                for s in range(2):
                    ring.load(sp, v, s, w_view[:, :, bass.ds((2 * v + s) * P, P)])
            res.store(sp, c0)

        @block.gpsimd
        def _(pool):
            res.sum_squares(pool, nc)
            res.add(pool, nc)

        @block.scalar
        def _(act):
            chain = Chain(act, chain_a)
            nc.scalar.activation(sq[:, 0:HEADS], m.att[:, :, toks], ACT.Square).then_inc(squared, 1)
            nc.scalar.activation(sq[:, HEADS:KD], m.ssd[:, :, toks], ACT.Square).then_inc(squared, 1)
            act.wait_ge(means, 1)
            chain(nc.scalar.activation(root[:], mean[:], ACT.Ln))
            nc.scalar.activation(root[:], root[:], ACT.Exp, scale=-0.5).then_inc(guesses, 1)
            for k in range(KD):
                act.wait_ge(scaled, k + 1)
                nc.scalar.activation(hi[:, k], sq[:, k], ACT.Copy).then_inc(rounded, 1)
            for s in range(2):
                ring.round(act, nc, 0, s)
            def square_out(v, s):
                res.square_tile(act, nc, v, s)
            with act.Fori(0, KD // 2 - 1) as v:
                for s in range(2):
                    square_out(v, s)
                    ring.round(act, nc, v + 1, s)
            for s in range(2):
                square_out(KD // 2 - 1, s)
            res.norm.root(act, nc, chain)

        @block.vector
        def _(dve):
            chain = Chain(dve, chain_v)
            ring.start_vector(dve)
            res.start_vector(dve)
            dve.wait_ge(squared, 2)
            nc.vector.tensor_reduce(tmp[:, HEADS], sq[:, HEADS:KD].rearrange("p k n -> p n k"), AX.X, ALU.add).then_inc(summed, 1)
            dve.wait_ge(totals, 1)
            nc.vector.tensor_scalar(mean[:, 0:HEADS], psn[:, :, 0:n], 1.0 / P, EPS, ALU.mult, ALU.add)
            nc.vector.tensor_scalar(mean[:, HEADS], psq[:, 0:n], 1.0 / SW, EPS, ALU.mult, ALU.add).then_inc(means, 1)
            dve.wait_ge(guesses, 1)
            chain(nc.vector.tensor_tensor(tmp[:], root[:], root[:], ALU.mult))
            chain(nc.vector.scalar_tensor_tensor(tmp[:], tmp[:], -0.5, mean[:], ALU.mult, ALU.mult))
            chain(nc.vector.scalar_tensor_tensor(root[:], tmp[:], 1.5, root[:], ALU.add, ALU.mult))

            def low(k):
                dve.wait_ge(scaled, k + 1)
                dve.wait_ge(rounded, k + 1)
                nc.vector.tensor_tensor(lo[:, k], sq[:, k], hi[:, k], ALU.subtract).then_inc(ready, 1)
            for k in range(KD):
                col = g.sub_col[:, 0:1] if k < HEADS else g.cols_b[:, ROW_SG + k - HEADS:ROW_SG + k - HEADS + 1]
                nc.vector.scalar_tensor_tensor(sq[:, k], part(k), col, root[:, min(k, HEADS)],
                                               ALU.mult, ALU.mult).then_inc(scaled, 1)
                if k:
                    low(k - 1)
            low(KD - 1)
            for s in range(2):
                ring.rest(dve, nc, 0, s)

            def copy_out(v, s):
                dve.wait_ge(ring.used, 2 * v + (s + 3))
                res.copy_tile(dve, nc, v, s, psu[:, s, 0:n])
            with dve.Fori(0, KD // 2 - 1) as v:
                for s in range(2):
                    copy_out(v, s)
                    ring.rest(dve, nc, v + 1, s)
            for s in range(2):
                copy_out(KD // 2 - 1, s)
            res.vector(dve, nc, chain, g.post[:, 0, stream])

        @block.tensor
        def _(pe):
            ring.start_tensor(pe)
            pe.wait_ge(squared, 2)
            for h in range(HEADS):
                nc.tensor.matmul(psn[:, h, 0:n], g.ones[:], sq[:, h], start=True, stop=True)
            pe.wait_ge(summed, 1)
            nc.tensor.matmul(psq[:, 0:n], g.ones[:], tmp[:, HEADS], start=True, stop=True).then_inc(totals, 1)
            pe.wait_ge(ready, KD)
            with pe.Fori(0, KD // 2) as v:
                for s in range(2):
                    ring.ready(pe, v, s)
                    res.bank_free(pe, v, s)
                    product3(nc, psu[:, s, 0:n], ring.hi[:, s], ring.lo[:, s], hi, lo, KD).then_inc(ring.used, 1)
            res.tensor(pe, nc)


def ffn_stage(nc, g, layer, chunks):
    N = CHUNKS[-1][1]
    C = len(chunks)
    w1 = g.w_ffn_in[layer].rearrange("(k p) n -> p k n", p=P)
    w2 = g.w_ffn_out[layer].rearrange("(k p) n -> p k n", p=P)
    KS = [(0, 8), (8, 8), (16, 6)]
    DOWN = [(i // 3, KS[i % 3]) for i in range(6)]
    PASSES = KD // 2
    PER = KF + 3 * PASSES
    SCALAR_AT = {2: 0, 3: 1, 4: 2, 5: 3, 8: 4, **{10 + k: 5 + k for k in range(KD)}}
    VECTOR_AT = {7: 0, 9: 1, **{10 + k: 2 + k for k in range(KD + 1)}}
    with Stage(nc, f"ffn{layer}") as st:
        psn = st.ps("psn", [P, 512])
        psu = st.ps("psu", [P, 2, 2, 512])
        psf = st.ps("psf", [P, 2, 512])
        x = st.sb("x", [P, KD, N])
        f = st.sb("f", [P, KD, N])
        h_hi = st.sb("h_hi", [P, KD, N], F32R)
        h_lo = st.sb("h_lo", [P, KD, N], F32R)
        sq = st.sb("sq", [P, 2, N])
        pre_bufs, post_bufs = st.sb("pre_bufs", [P, 3, N]), st.sb("post_bufs", [P, 3, N])
        ring = WeightRing(st)
        a_hi = st.sb("a_hi", [P, KF, N], F32R)
        a_lo = st.sb("a_lo", [P, KF, N], F32R)
        sig = st.sb("sig", [P, 2, N])
        act_t = st.sb("act_t", [P, 2, N])
        sizes = [CHUNKS[ci] for ci in chunks]
        pres = [Prenorm(st, g, f"pre{i}", n, psn, x, sq, pre_bufs, h_hi, h_lo) for i, (_, n) in enumerate(sizes)]
        ress = [Residual(st, g, f"post{i}", n, psn, f, x, sq, post_bufs) for i, (_, n) in enumerate(sizes)]
        streams = [0 if ci == 0 else 1 for ci in chunks]
        shifts = [g.mod[:, s, SH2 * KD:(SH2 + 1) * KD] for s in streams]
        scales = [g.pre[:, 1, s] for s in streams]
        gates = [g.post[:, 1, s] for s in streams]
        chain_v, chain_a = st.sem("chain_v"), st.sem("chain_a")
        gated, multiplied, a_rounded, a_ready = st.sem("gated"), st.sem("multiplied"), st.sem("a_rounded"), st.sem("a_ready")
        block = st.block()

        @block.sync
        def _(sp):
            for i in range(C):
                with sp.Fori(0, KF) as v:
                    for s in range(2):
                        ring.load(sp, v + PER * i, s, w1[:, :, bass.ds(v * P + s * DFF, P)])
                with sp.Fori(0, PASSES) as o:
                    for u, (half, (k0, nk)) in enumerate(DOWN):
                        ring.load(sp, 3 * o + (PER * i + KF + u // 2), u % 2, w2[:, k0:k0 + nk, bass.ds((2 * o + half) * P, P)], nk)

        @block.gpsimd
        def _(pool):
            pres[0].load(pool, sizes[0][0])
            for i in range(C):
                pool.wait_ge(pres[i].ready, KD)
                if i:
                    ress[i - 1].load(pool, sizes[i - 1][0])
                    ress[i - 1].add(pool, nc)
                    ress[i - 1].store(pool, sizes[i - 1][0])
                if i + 1 < C:
                    pres[i + 1].load(pool, sizes[i + 1][0])
                    for k in range(1, KD):
                        pres[i + 1].add(pool, nc.gpsimd, k)
                    pool.wait_ge(pres[i + 1].added, KD - 1)
                ress[i].sum_squares(pool, nc)
            ress[-1].load(pool, sizes[-1][0])
            ress[-1].add(pool, nc)
            ress[-1].store(pool, sizes[-1][0])

        @block.scalar
        def _(act):
            chain = Chain(act, chain_a)
            pres[0].scalar(act, nc, chain, shifts[0])
            for s in range(2):
                ring.round(act, nc, 0, s)
            for i in range(C):
                n, base, hidden0 = sizes[i][1], PER * i, KF * i

                def gate(t, e):
                    act.wait_ge(ring.used, 2 * t + (2 * base + 3))
                    act.wait_ge(multiplied, t + (hidden0 + 1))
                    nc.scalar.activation(sig[:, e, 0:n], psu[:, e, 0, 0:n], ACT.Silu).then_inc(gated, 1)

                def hidden_hi(t, e):
                    act.wait_ge(multiplied, t + (hidden0 + 3))
                    nc.scalar.activation(a_hi[:, bass.ds(t, 1), 0:n].rearrange("p o t -> p (o t)"), act_t[:, e, 0:n],
                                         ACT.Copy).then_inc(a_rounded, 1)

                def gate_up(t, e):
                    gate(t, e)
                    ring.round(act, nc, t + (base + 1), 0)
                    hidden_hi(t, e)
                    ring.round(act, nc, t + (base + 1), 1)
                for e in range(2):
                    gate_up(e, e)
                    if i and e == 0:
                        ress[i - 1].norm.root(act, nc, chain)
                with act.Fori(1, KF // 2) as w:
                    for e in range(2):
                        gate_up(2 * w + e, e)

                def round_(o, u):
                    ring.round(act, nc, 3 * o + (base + KF + u // 2), u % 2, DOWN[u % 6][1][1])
                    if i + 1 < C and 6 * o + u in SCALAR_AT:
                        pres[i + 1].scalar_step(act, nc, chain, shifts[i + 1], SCALAR_AT[6 * o + u])

                def down(o, more=True):
                    for u in (2, 3, 4, 5):
                        round_(o, u)
                    ress[i].square_tile(act, nc, o, 0)
                    if more:
                        round_(o, 6)
                        round_(o, 7)
                    ress[i].square_tile(act, nc, o, 1)
                if i + 1 < C:
                    for o in range(PASSES):
                        down(o)
                else:
                    with act.Fori(0, PASSES - 1) as o:
                        down(o)
                    down(PASSES - 1, False)
            ress[-1].norm.root(act, nc, chain)

        @block.vector
        def _(dve):
            chain = Chain(dve, chain_v)
            ring.start_vector(dve)
            dve.sem_inc(multiplied, 2)
            pres[0].vector(dve, nc, chain, scales[0], shifts[0])
            for s in range(2):
                ring.rest(dve, nc, 0, s)
            for i in range(C):
                n, base, hidden0 = sizes[i][1], PER * i, KF * i

                def hidden(t, e):
                    dve.wait_ge(gated, t + (hidden0 + 1))
                    dve.wait_ge(ring.used, 2 * t + (2 * base + 4))
                    nc.vector.tensor_tensor(act_t[:, e, 0:n], sig[:, e, 0:n], psu[:, e, 1, 0:n], ALU.mult).then_inc(multiplied, 1)

                def hidden_lo(t, e):
                    dve.wait_ge(a_rounded, t + (hidden0 + 1))
                    nc.vector.tensor_tensor(a_lo[:, bass.ds(t, 1), 0:n].rearrange("p o t -> p (o t)"), act_t[:, e, 0:n],
                                            a_hi[:, bass.ds(t, 1), 0:n].rearrange("p o t -> p (o t)"), ALU.subtract).then_inc(a_ready, 1)
                    dve.wait_ge(a_ready, t + (hidden0 + 1))

                def gate_up(t, e):
                    ring.rest(dve, nc, t + (base + 1), 0)
                    hidden(t, e)
                    hidden_lo(t, e)
                    ring.rest(dve, nc, t + (base + 1), 1)
                gate_up(0, 0)
                if i:
                    ress[i - 1].norm.mean_eps(dve, nc)
                gate_up(1, 1)
                if i:
                    ress[i - 1].norm.refine(dve, nc, chain)
                    ress[i - 1].scale(nc, gates[i - 1])
                with dve.Fori(1, KF // 2) as w:
                    for e in range(2):
                        gate_up(2 * w + e, e)
                if i:
                    dve.wait_ge(ress[i - 1].summed, KD)
                ress[i].start_vector(dve)

                def copy_out(o, half):
                    dve.wait_ge(ring.used, 6 * o + (2 * (base + KF) + 3 * half + 5))
                    ress[i].copy_tile(dve, nc, o, half, psf[:, half, 0:n])

                def rest(o, u):
                    ring.rest(dve, nc, 3 * o + (base + KF + u // 2), u % 2, DOWN[u % 6][1][1])
                    if i + 1 < C and 6 * o + u in VECTOR_AT:
                        pres[i + 1].vector_step(dve, nc, chain, scales[i + 1], shifts[i + 1], VECTOR_AT[6 * o + u])

                def down(o, more=True):
                    for u in (2, 3, 4):
                        rest(o, u)
                    copy_out(o, 0)
                    rest(o, 5)
                    if more:
                        rest(o, 6)
                        rest(o, 7)
                    copy_out(o, 1)
                if i + 1 < C:
                    for o in range(PASSES):
                        down(o)
                else:
                    with dve.Fori(0, PASSES - 1) as o:
                        down(o)
                    down(PASSES - 1, False)
            ress[-1].vector(dve, nc, chain, gates[-1])

        @block.tensor
        def _(pe):
            ring.start_tensor(pe)
            pres[0].total(pe, nc)
            for i in range(C):
                n, base, hidden0 = sizes[i][1], PER * i, KF * i
                hi, lo = h_hi[:, :, 0:n], h_lo[:, :, 0:n]

                def gate_up(t, e):
                    pe.wait_ge(multiplied, t + (hidden0 + 1))
                    for s in range(2):
                        ring.ready(pe, t + base, s)
                        product3(nc, psu[:, e, s, 0:n], ring.hi[:, s], ring.lo[:, s], hi, lo, KD).then_inc(ring.used, 1)

                def down(o):
                    for u, (half, (k0, nk)) in enumerate(DOWN):
                        pe.wait_ge(ring.split, 6 * o + (2 * (base + KF) + u + 3))
                        if u % 3 == 0:
                            ress[i].bank_free(pe, o, half)
                        last = product3(nc, psf[:, half, 0:n], ring.hi[:, u % 2], ring.lo[:, u % 2],
                                        a_hi[:, k0:k0 + nk, 0:n], a_lo[:, k0:k0 + nk, 0:n], nk, u % 3 == 0, u % 3 == 2)
                        last.then_inc(ring.used, 1)
                pe.wait_ge(pres[i].ready, KD)
                gate_up(0, 0)
                if i:
                    ress[i - 1].tensor(pe, nc)
                gate_up(1, 1)
                with pe.Fori(1, KF // 2) as w:
                    for e in range(2):
                        gate_up(2 * w + e, e)
                pe.wait_ge(a_ready, hidden0 + KF)
                if i + 1 < C:
                    down(0)
                    pres[i + 1].total(pe, nc)
                    with pe.Fori(1, PASSES) as o:
                        down(o)
                else:
                    with pe.Fori(0, PASSES) as o:
                        down(o)
            ress[-1].tensor(pe, nc)


def attention_stage(nc, g, m, layer):
    tiles = [(t, CTX) for t in range(CTX // P)] if layer == 0 else []
    tiles += [(t, T) for t in range(CTX // P, NT)]
    n_tiles = len(tiles)
    groups = [(i, k, min(4, keys // P - k)) for i, (_, keys) in enumerate(tiles) for k in range(0, keys // P, 4)]
    of_tile = [[j for j, x in enumerate(groups) if x[0] == i] for i in range(n_tiles)]
    n_groups = len(groups)
    ES, GS = 3, 6
    with Stage(nc, f"att{layer}") as st:
        q = st.sb("q", [P, 2, T], F32R)
        k_hi = st.sb("k_hi", [P, 2, T], F32R)
        k_lo = st.sb("k_lo", [P, 2, T], F32R)
        v_hi = st.sb("v_hi", [P, NT, P], F32R)
        v_lo = st.sb("v_lo", [P, NT, P], F32R)
        e = st.sb("e", [P, ES, 2, T])
        pt = st.sb("pt", [P, GS, 4, P])
        pt_hi = st.sb("pt_hi", [P, GS, 4, P], F32R)
        pt_lo = st.sb("pt_lo", [P, GS, 4, P], F32R)
        diag = st.sb("diag", [P, ES, P])
        top = st.sb("top", [P, ES, 2])
        shift = st.sb("shift", [P, ES, 2])
        total = st.sb("total", [P, ES, 2])
        inv = st.sb("inv", [P, ES, 2])
        coef = st.sb("coef", [P, ES])
        ps_s = st.ps("ps_s", [P, 2, 3, 512])
        ps_t = st.ps("ps_t", [P, 4, P])
        ps_o = st.ps("ps_o", [P, 4, P])
        q_in, k_in, v_in = st.sem("q_in"), st.sem("k_in"), st.sem("v_in")
        scored, topped, shifted, exped, mixed, turned, copied, hi_made, lo_made, summed, out = (st.sem(x) for x in (
            "scored", "topped", "shifted", "exped", "mixed", "turned", "copied", "hi_made", "lo_made", "summed", "out"))
        chain_v = st.sem("chain_v")
        block = st.block()

        @block.sync
        def _(sp):
            def load_qk(h):
                for a in range(2):
                    rows = slice(64 * a, 64 * a + 64)
                    for part in range(2):
                        half = slice(64 * part, 64 * part + 64)
                        sp.dma_start(q[half, a].bitcast(F32), g.qk_d[part, bass.ds(h, 1), rows].rearrange("o p t -> p (o t)")).then_inc(q_in, 16)
                        for dst, which in ((k_hi, 0), (k_lo, 1)):
                            sp.dma_start(dst[half, a].bitcast(F32), g.qk_d[which, bass.ds(h + HEADS, 1), rows].rearrange("o p t -> p (o t)")).then_inc(k_in, 16)

            def load_v(h):
                for dst, part in ((v_hi, 0), (v_lo, 1)):
                    sp.dma_start(dst[:].bitcast(F32), g.v_d[part, bass.ds(h, 1)].rearrange("o (t p) e -> p (o t) e", p=P)).then_inc(v_in, 16)
            load_qk(0)
            load_v(0)
            with sp.Fori(1, HEADS) as h:
                sp.wait_ge(scored, 2 * n_tiles * h)
                load_qk(h)
                sp.wait_ge(summed, n_groups * h)
                load_v(h)

        @block.tensor
        def _(pe):
            with pe.Fori(0, HEADS) as h:
                pe.wait_ge(q_in, 64 * h + 64)
                pe.wait_ge(k_in, 128 * h + 128)

                def scores(i, a):
                    if i >= n_tiles:
                        return
                    t, keys = tiles[i]
                    pe.wait_ge(exped, 2 * n_tiles * h + (2 * i + a + 1))
                    for c in range(0, keys, 512):
                        w = min(512, keys - c)
                        nc.tensor.matmul(ps_s[:, a, c // 512, 0:w], q[:, a, t * P:(t + 1) * P], k_hi[:, a, c:c + w], start=True, stop=False)
                        last = nc.tensor.matmul(ps_s[:, a, c // 512, 0:w], q[:, a, t * P:(t + 1) * P], k_lo[:, a, c:c + w], start=False, stop=True)
                    last.then_inc(scored, 1)

                def transposes(j):
                    i, k0, nk = groups[j]
                    pe.wait_ge(mixed, n_tiles * h + (i + 1))
                    pe.wait_ge(copied, n_groups * h + (j + 1))
                    for x in range(nk):
                        last = nc.tensor.matmul(ps_t[:, x], e[:, i % ES, 1, (k0 + x) * P:(k0 + x + 1) * P], diag[:, i % ES], start=True, stop=True)
                    last.then_inc(turned, 1)

                def products(j):
                    i, k0, nk = groups[j]
                    pe.wait_ge(lo_made, n_groups * h + (j + 1))
                    if k0 == 0:
                        pe.wait_ge(out, n_tiles * h + (i + 1))
                    last = product3(nc, ps_o[:, 0], v_hi[:, k0:k0 + nk], v_lo[:, k0:k0 + nk], pt_hi[:, j % GS], pt_lo[:, j % GS], nk,
                                    k0 == 0, (k0 + nk) * P == tiles[i][1])
                    last.then_inc(summed, 1)

                scores(0, 0)
                scores(0, 1)
                pe.wait_ge(v_in, 32 * h + 32)
                for i in range(n_tiles):
                    scores(i + 1, 0)
                    scores(i + 1, 1)
                    late = list(of_tile[i - 1]) if i else []
                    for j in of_tile[i]:
                        transposes(j)
                        if late:
                            products(late.pop(0))
                    for j in late:
                        products(j)
                for j in of_tile[-1]:
                    products(j)

        @block.vector
        def _(dve):
            chain = Chain(dve, chain_v)
            with dve.Fori(0, HEADS) as h, chain.over(h, HEADS, 2 * n_tiles):
                def maximum(i, a):
                    if i >= n_tiles:
                        return
                    dve.wait_ge(scored, 2 * n_tiles * h + (2 * i + a + 1))
                    nc.vector.tensor_reduce(top[:, i % ES, a:a + 1], ps_s[:, a].rearrange("p c w -> p (c w)")[:, 0:tiles[i][1]],
                                            AX.X, ALU.max).then_inc(topped, 1)
                    dve.wait_ge(topped, 2 * n_tiles * h + (2 * i + a + 1))
                    nc.vector.tensor_scalar(shift[:, i % ES, a:a + 1], top[:, i % ES, a:a + 1], -0.125, None,
                                            ALU.mult).then_inc(shifted, 1)

                def mix(i):
                    keys, x = tiles[i][1], i % ES
                    dve.wait_ge(exped, 2 * n_tiles * h + (2 * i + 4))
                    chain(nc.vector.reciprocal(inv[:, x], total[:, x]))
                    chain(nc.vector.scalar_tensor_tensor(coef[:, x:x + 1], inv[:, x, 1:2], g.neg_lam[:], total[:, x, 0:1], ALU.mult, ALU.mult))
                    nc.vector.tensor_scalar(diag[:, x], g.ident[:], inv[:, x, 0:1], None, ALU.mult)
                    nc.vector.scalar_tensor_tensor(e[:, x, 1, 0:keys], e[:, x, 1, 0:keys], coef[:, x:x + 1],
                                                   e[:, x, 0, 0:keys], ALU.mult, ALU.add).then_inc(mixed, 1)

                def high(j):
                    dve.wait_ge(copied, n_groups * h + (j + 2))
                    nk = groups[j][2]
                    nc.vector.tensor_copy(pt_hi[:, j % GS, 0:nk], pt[:, j % GS, 0:nk]).then_inc(hi_made, 1)
                maximum(0, 0)
                maximum(0, 1)
                for i in range(n_tiles):
                    js = of_tile[i]
                    mix(i)
                    maximum(i + 1, 0)
                    maximum(i + 1, 1)
                    for j in js:
                        high(j)

        @block.gpsimd
        def _(pool):
            with pool.Fori(0, HEADS) as h:
                for j, (_, _, nk) in enumerate(groups):
                    pool.wait_ge(hi_made, n_groups * h + (j + 1))
                    nc.gpsimd.tensor_tensor(pt_lo[:, j % GS, 0:nk], pt[:, j % GS, 0:nk], pt_hi[:, j % GS, 0:nk], ALU.subtract).then_inc(lo_made, 1)

        @block.scalar
        def _(act):
            act.sem_inc(exped, 2)
            act.sem_inc(copied, 1)
            act.sem_inc(out, 1)
            with act.Fori(0, HEADS) as h:
                def exps(i, a):
                    if i >= n_tiles:
                        return
                    keys = tiles[i][1]
                    if i >= ES:
                        act.wait_ge(turned, n_groups * h + (of_tile[i - ES][-1] + 1))
                    act.wait_ge(shifted, 2 * n_tiles * h + (2 * i + a + 1))
                    nc.scalar.activation(e[:, i % ES, a, 0:keys], ps_s[:, a].rearrange("p c w -> p (c w)")[:, 0:keys], ACT.Exp,
                                         bias=shift[:, i % ES, a:a + 1], scale=0.125,
                                         accum_out=total[:, i % ES, a:a + 1]).then_inc(exped, 1)

                def copy_group(j):
                    nk = groups[j][2]
                    act.wait_ge(turned, n_groups * h + (j + 1))
                    if j >= GS:
                        act.wait_ge(summed, n_groups * h + (j - GS + 1))
                    nc.scalar.activation(pt[:, j % GS, 0:nk], ps_t[:, 0:nk], ACT.Copy).then_inc(copied, 1)

                def copy_out(i):
                    act.wait_ge(summed, n_groups * h + (of_tile[i][-1] + 1))
                    t = tiles[i][0]
                    nc.scalar.activation(m.att[:, bass.ds(h, 1), t * P:(t + 1) * P].rearrange("p o t -> p (o t)"), ps_o[:, 0],
                                         ACT.Copy).then_inc(out, 1)
                exps(0, 0)
                exps(0, 1)
                for i in range(n_tiles):
                    js = of_tile[i]
                    copy_group(js[0])
                    exps(i + 1, 0)
                    for j in js[1:2]:
                        copy_group(j)
                    exps(i + 1, 1)
                    for j in js[2:]:
                        copy_group(j)
                    if i:
                        copy_out(i - 1)
                copy_out(n_tiles - 1)


def scan_prep_stage(nc, g, layer, m):
    PAD = T + 6
    CONV_T = 8
    with Stage(nc, f"prep{layer}") as st:
        pad = st.sb("pad", [P, 2, PAD])
        taps = st.sb("taps", [P, 2, 6])
        acc = st.sb("acc", [P, 2, PAD - 4])
        cv = st.sb("cv", [P, 2, T])
        tok = st.sb("tok", [P, 2, NT, P])
        ps = st.ps("ps", [P, 2, 3, 4, P])
        psd = st.ps("psd", [P, 512])
        dt_t = st.sb("dt_t", [DTP, T])
        dta = st.sb("dta", [DTP, T])
        cum = st.sb("cum", [DTP, T])
        s1 = st.sb("s1", [DTP, T])
        s2 = st.sb("s2", [DTP, T])
        s3 = st.sb("s3", [DTP, T])
        reset = st.sb("reset", [DTP, T])
        dta_tok = st.sb("dta_tok", [P, NT, 2, SH])
        w_tok = st.sb("w_tok", [P, NT, 2, SH])
        pad_in = [st.sem(f"pad_in{s}") for s in range(2)]
        zeroed, tapped, first, summed, sig, done, turned, tok_done = (st.sem(x) for x in (
            "zeroed", "tapped", "first", "summed", "sig", "done", "turned", "tok_done"))
        cv_out = [st.sem(f"cv_out{s}") for s in range(2)]
        tok_out = [st.sem(f"tok_out{s}") for s in range(2)]
        reset_in, a_exp, dt_ready, dt_turned, dt_copied, tot, tot_copied, cum_out, acc_free = (st.sem(x) for x in (
            "reset_in", "a_exp", "dt_ready", "dt_turned", "dt_copied", "tot", "tot_copied", "cum_out", "acc_free"))
        chain_v, chain_a = st.sem("chain_v"), st.sem("chain_a")
        block = st.block()
        PAIRS = CONV_T // 2
        TURNED = 3

        @block.sync
        def _(sp):
            sp.dma_start(reset[:], g.reset_d).then_inc(reset_in, 16)
            sp.wait_ge(zeroed, 3)

            def load(v, s):
                sp.wait_ge(summed, 2 * v + (s + 1))
                src = g.zx_d[bass.ds(2 * v + (s + 4), 1)].rearrange("o p t -> p (o t)")
                sp.dma_start(pad[:, s, 2:2 + CTX], src[:, 0:CTX]).then_inc(pad_in[s], 16)
                sp.dma_start(pad[:, s, 4 + CTX:4 + T], src[:, CTX:T]).then_inc(pad_in[s], 16)
            for s in range(2):
                load(0, s)
            with sp.Fori(0, TURNED) as v:
                for s in range(2):
                    load(v + 1, s)
                for s in range(2):
                    sp.wait_ge(done, 2 * v + s + 1)
                    sp.dma_start(g.cv_d[bass.ds(2 * v + s, 1)].rearrange("o p t -> p (o t)"), cv[:, s]).then_inc(cv_out[s], 16)
                    sp.wait_ge(tok_done, 6 * v + (3 * s + 7))
                    sp.dma_start(g.tok_d.rearrange("c p f -> p c f")[:, :, bass.ds((2 * v + s) * P, P)], tok[:, s]).then_inc(tok_out[s], 16)
            for s in range(2):
                sp.wait_ge(done, 2 * TURNED + s + 1)
                sp.dma_start(g.cv_d[2 * TURNED + s], cv[:, s]).then_inc(cv_out[s], 16)
            sp.wait_ge(dt_ready, 1)
            for d in range(2):
                sp.dma_start(g.cum_d[SH * d:SH * d + SH, :], cum[BWD * d:BWD * d + SH, :]).then_inc(cum_out, 16)
            sp.wait_ge(cum_out, 32)
            for s in range(2):
                sp.wait_ge(cv_out[s], 16 * PAIRS + 16)
                sp.wait_ge(tok_out[s], 16 * TURNED + 16)

        @block.gpsimd
        def _(pool):
            for a, b in ((0, 2), (2 + CTX, 4 + CTX), (4 + T, 6 + T)):
                nc.gpsimd.memset(pad[:, :, a:b], 0.0).then_inc(zeroed, 1)

        @block.scalar
        def _(act):
            chain = Chain(act, chain_a)
            for s in range(2):
                act.sem_inc(cv_out[s], 16)
            act.wait_ge(acc_free, 1)
            nc.scalar.activation(s1[:], s1[:], ACT.Exp, scale=-1.0).then_inc(a_exp, 1)
            with act.Fori(0, PAIRS) as v:
                for s in range(2):
                    act.wait_ge(pad_in[s], 32 * v + 32)
                    act.wait_ge(tapped, 2 * v + s + 1)
                    nc.scalar.activation(acc[:, s], pad[:, s, 0:PAD - 4], ACT.Identity, bias=taps[:, s, 5:6],
                                         scale=taps[:, s, 0:1]).then_inc(first, 1)
                    act.wait_ge(summed, 2 * v + (s + 3))
                    act.wait_ge(cv_out[s], 16 * v + 16)
                    act.wait_ge(turned, 6 * v + (3 * s + 1))
                    nc.scalar.activation(cv[:, s, 0:CTX], acc[:, s, 0:CTX], ACT.Silu)
                    nc.scalar.activation(cv[:, s, CTX:T], acc[:, s, CTX + 2:T + 2], ACT.Silu).then_inc(done, 1)
            act.wait_ge(tot_copied, 1)
            chain(nc.scalar.activation(w_tok[:], w_tok[:], ACT.Exp))
            nc.scalar.activation(m.etot[:], m.etot[:], ACT.Exp).then_inc(a_exp, 1)

        @block.vector
        def _(dve):
            chain = Chain(dve, chain_v)
            dve.sem_inc(summed, 2)
            dve.sem_inc(tok_done, 4)
            for s in range(2):
                dve.sem_inc(tok_out[s], 16)
            chain(nc.vector.tensor_scalar(m.dt[:], m.dt[:], g.dt_bias[:], None, ALU.add))
            chain(nc.vector.tensor_scalar(s2[:], m.dt[:], -1.0, None, ALU.mult))
            nc.vector.tensor_tensor(s1[:], m.dt[:], s2[:], ALU.max).then_inc(acc_free, 1)
            dve.wait_ge(a_exp, 1)
            chain(nc.vector.tensor_scalar_add(s2[:], s1[:], 2.0))
            chain(nc.vector.reciprocal(s2[:], s2[:]))
            chain(nc.vector.tensor_tensor(s1[:], s1[:], s2[:], ALU.mult))
            chain(nc.vector.tensor_tensor(s2[:], s1[:], s1[:], ALU.mult))
            chain(nc.vector.tensor_scalar(s3[:], s2[:], 2.0 / 17, None, ALU.mult))
            for odd in (15, 13, 11, 9, 7, 5, 3):
                chain(nc.vector.scalar_tensor_tensor(s3[:], s3[:], 2.0 / odd, s2[:], ALU.add, ALU.mult))
            chain(nc.vector.scalar_tensor_tensor(s3[:], s3[:], 2.0, s1[:], ALU.add, ALU.mult))
            chain(nc.vector.scalar_tensor_tensor(dt_t[:], m.dt[:], 0.0, s3[:], ALU.max, ALU.add))
            chain(nc.vector.tensor_scalar(dta[:], dt_t[:], g.a_neg[:], None, ALU.mult))
            dve.wait_ge(reset_in, 16)
            chain(nc.vector.tensor_tensor_scan(cum[:], reset[:], dta[:], 0.0, ALU.mult, ALU.add))
            back = slice(BWD, DTP)
            ends = cum[back].rearrange("h (c t) -> h c t", t=P)[:, :, P - 1:P].broadcast_to([SH, NT, P])
            chain(nc.vector.tensor_tensor(s1[back].rearrange("h (c t) -> h c t", t=P), ends,
                                          dta[back].rearrange("h (c t) -> h c t", t=P), ALU.add))
            nc.vector.tensor_tensor(cum[back], s1[back], cum[back], ALU.subtract).then_inc(dt_ready, 1)
            for i, dst in ((0, m.dt_tok), (1, dta_tok), (2, m.cum_tok)):
                dve.wait_ge(dt_turned, i + 1)
                for d in range(2):
                    ins = nc.vector.tensor_copy(dst[:, :, d], psd[:, 0:NT * DTP].rearrange("p (c h) -> p c h", h=DTP)[
                        :, :, BWD * d:BWD * d + SH])
                ins.then_inc(dt_copied, 1)
            dve.wait_ge(tot, 1)
            totals = psd[:, 0:NT * 2 * SH].rearrange("p (c d h) -> p c d h", d=2, h=SH)
            nc.vector.tensor_copy(m.etot[:], totals)
            dve.wait_ge(dt_copied, 3)
            nc.vector.tensor_tensor(w_tok[:], totals, m.cum_tok[:], ALU.subtract).then_inc(tot_copied, 1)

            def tile(v, s):
                dve.wait_ge(first, 2 * v + (s + 1))
                for tap in range(1, 5):
                    ins = nc.vector.scalar_tensor_tensor(acc[:, s], pad[:, s, tap:tap + PAD - 4], taps[:, s, tap:tap + 1], acc[:, s],
                                                         ALU.mult, ALU.add)
                    if tap < 4:
                        chain(ins)
                    else:
                        ins.then_inc(summed, 1)

            def get_taps(v, s):
                col = bass.ds(2 * v + s, 1)
                chain(nc.vector.tensor_copy(taps[:, s, 0:5], g.cols_a[:, ROW_CW:ROW_CW + 40].rearrange("p (a t) -> p a t", t=CONV_T)[:, :, col].rearrange("p a o -> p (a o)")))
                nc.vector.tensor_copy(taps[:, s, 5:6], g.cols_a[:, ROW_CB:ROW_CB + CONV_T][:, col]).then_inc(tapped, 1)

            def copies(v, s):
                dve.wait_ge(tok_out[s], 16 * v + 16)
                for i in range(3):
                    k0, nk = 4 * i, min(4, NT - 4 * i)
                    dve.wait_ge(turned, 6 * v + (3 * s + i + 5))
                    nc.vector.tensor_copy(tok[:, s, k0:k0 + nk], ps[:, s, i, 0:nk]).then_inc(tok_done, 1)
            with dve.Fori(0, TURNED) as v, chain.over(v, TURNED, 8):
                for s in range(2):
                    get_taps(v, s)
                    tile(v, s)
                for s in range(2):
                    copies(v, s)
            for s in range(2):
                get_taps(TURNED, s)
                tile(TURNED, s)
            dve.wait_ge(a_exp, 2)
            nc.vector.tensor_tensor(m.w_tok[:], w_tok[:], m.dt_tok[:], ALU.mult)

        @block.tensor
        def _(pe):
            pe.sem_inc(turned, 4)
            pe.wait_ge(dt_ready, 1)
            for i, src in enumerate((dt_t, dta, cum)):
                pe.wait_ge(dt_copied, i) if i else None
                for c in range(NT):
                    last = nc.tensor.transpose(psd[:, c * DTP:(c + 1) * DTP], src[:, c * P:(c + 1) * P], g.ident[0:DTP, 0:DTP])
                last.then_inc(dt_turned, 1)
            pe.wait_ge(dt_copied, 3)
            nc.tensor.matmul(psd[:, 0:NT * 2 * SH], g.ones[:], dta_tok.rearrange("p c d h -> p (c d h)"), start=True, stop=True).then_inc(tot, 1)
            with pe.Fori(0, TURNED) as v:
                for s in range(2):
                    pe.wait_ge(done, 2 * v + s + 1)
                    pe.wait_ge(tok_done, 6 * v + (3 * s + 1))
                    for i in range(3):
                        for x in range(min(4, NT - 4 * i)):
                            c = 4 * i + x
                            last = nc.tensor.transpose(ps[:, s, i, x], cv[:, s, c * P:(c + 1) * P], g.ident[:])
                        last.then_inc(turned, 1)


def wait_if(eng, sem, value):
    if not isinstance(value, int) or value > 0:
        eng.wait_ge(sem, value)


def scan_state_stage(nc, g, m, layer):
    XB = SW + NG * P
    with Stage(nc, f"state{layer}") as st:
        tok = st.sb("tok", [P, 2, 2, XB])
        xw = st.sb("xw", [P, 2, 2, SW])
        h = st.sb("h", [P, 2, 2, SW])
        hd = st.sb("hd", [P, 2, 2, SW])
        ps = st.ps("ps", [P, 2, 2, SW])
        tok_in = [[st.sem(f"tok_in{d}{s}") for s in range(2)] for d in range(2)]
        weighted, pushed, updated, decayed = ([st.sem(f"{x}{d}") for d in range(2)] for x in ("weighted", "pushed", "updated", "decayed"))
        stored = [[st.sem(f"stored{d}{s}") for s in range(2)] for d in range(2)]
        zeroed = st.sem("zeroed")
        block = st.block()

        def steps(body, eng):
            for s in range(2):
                body(0, s, (s, 1 - s))
            down = eng.alloc_register(f"backward_chunk{layer}")
            eng.reg_mov(down, NT + 1)
            with eng.Fori(1, NT // 2) as v:
                eng.reg_sub(down, down, 2)
                back = eng.snap(down, min_val=3, max_val=NT - 1)
                for s in range(2):
                    body(v, s, (2 * v + s, back - s if s else back))

        @block.sync
        def _(sp):
            def body(v, s, c):
                for d in range(2):
                    wait_if(sp, pushed[d], 2 * v + (s - 1))
                    sp.dma_start(tok[:, d, s], g.tok_d[bass.ds(c[d], 1)].rearrange("o p f -> p (o f)")).then_inc(tok_in[d][s], 16)
                for d in range(2):
                    wait_if(sp, updated[d], 2 * v + s)
                    if isinstance(v, int) and s == 0:
                        sp.wait_ge(zeroed, 2)
                    sp.dma_start(g.h_d[d, bass.ds(c[d], 1)].rearrange("o p f -> p (o f)"), h[:, d, s]).then_inc(stored[d][s], 16)
            steps(body, sp)
            for d in range(2):
                for s in range(2):
                    sp.wait_ge(stored[d][s], 16 * (NT // 2))

        @block.gpsimd
        def _(pool):
            for d in range(2):
                nc.gpsimd.memset(h[:, d, 0], 0.0).then_inc(zeroed, 1)

            def body(v, s, c):
                for d in range(2):
                    pool.wait_ge(tok_in[d][s], 16 * v + 16)
                    wait_if(pool, pushed[d], 2 * v + (s - 1))
                    nc.gpsimd.tensor_tensor(xw[:, d, s].rearrange("p (h e) -> p h e", h=SH), tok[:, d, s, 0:SW].rearrange("p (h e) -> p h e", h=SH),
                                            m.w_tok[:, bass.ds(c[d], 1), d].rearrange("p o h -> p (o h)").unsqueeze(2).broadcast_to([P, SH, 64]),
                                            ALU.mult).then_inc(weighted[d], 1)
            steps(body, pool)

        @block.tensor
        def _(pe):
            def body(v, s, c):
                for d in range(2):
                    pe.wait_ge(weighted[d], 2 * v + (s + 1))
                    wait_if(pe, updated[d], 2 * v + (s - 1))
                    for q in range(NG):
                        w = SW // NG
                        last = nc.tensor.matmul(ps[:, d, s, q * w:(q + 1) * w], tok[:, d, s, SW + q * P:SW + (q + 1) * P],
                                                xw[:, d, s, q * w:(q + 1) * w], start=True, stop=True)
                    last.then_inc(pushed[d], 1)
            steps(body, pe)

        @block.vector
        def _(dve):
            def body(v, s, c):
                for d in range(2):
                    if isinstance(v, int) and s == 0:
                        dve.wait_ge(zeroed, 2)
                    wait_if(dve, updated[d], 2 * v + s)
                    nc.vector.tensor_tensor(hd[:, d, s].rearrange("p (h e) -> p h e", h=SH), h[:, d, s].rearrange("p (h e) -> p h e", h=SH),
                                            m.etot[:, bass.ds(c[d], 1), d].rearrange("p o h -> p (o h)").unsqueeze(2).broadcast_to([P, SH, 64]),
                                            ALU.mult).then_inc(decayed[d], 1)
                for d in range(2):
                    dve.wait_ge(decayed[d], 2 * v + (s + 1))
                    dve.wait_ge(pushed[d], 2 * v + (s + 1))
                    wait_if(dve, stored[d][1 - s], 16 * v + 16 * s)
                    nc.vector.tensor_tensor(h[:, d, 1 - s], hd[:, d, s], ps[:, d, s], ALU.add).then_inc(updated[d], 1)
            steps(body, dve)


def scan_out_stage(nc, g, m, layer):
    v0 = 0 if layer == 0 else 1
    n_v = NT // 2 - v0
    DH = 2 * SH
    with Stage(nc, f"scan{layer}") as st:
        cv = st.sb("cv", [P, 2, 8, P])
        z = st.sb("z", [P, 2, 4, P])
        xt = st.sb("xt", [P, 2, SW])
        h = st.sb("h", [P, 2, 2, SW])
        rows = st.sb("rows", [P, 2, DH, P])
        seg = st.sb("seg", [P, 2, DH, P])
        er = st.sb("er", [P, 2, DH, P])
        xdt = st.sb("xdt", [P, 2, 2, SW])
        cbm = st.sb("cbm", [P, 2, 2, NG, P])
        skip = st.sb("skip", [P, 2, 4, P])
        ps_c = st.ps("ps_c", [P, 2, 4, P])
        ps_y = st.ps("ps_y", [P, 2, 4, P])
        loaded = [st.sem(f"loaded{s}") for s in range(2)]
        rows_in = [st.sem(f"rows_in{s}") for s in range(2)]
        crossed, masked, clipped, diffed, decays, row_decays, c_scaled, x_scaled, intra, summed, skipped, added, gated = (st.sem(x) for x in (
            "crossed", "masked", "clipped", "diffed", "decays", "row_decays", "c_scaled", "x_scaled", "intra", "summed", "skipped", "added", "gated"))
        LOADS = 4
        block = st.block()

        def steps(body, eng):
            for s in range(2):
                body(0, s)
            with eng.Fori(1, n_v) as w:
                for s in range(2):
                    body(w, s)

        @block.sync
        def _(sp):
            def body(w, s):
                c = 2 * w + (2 * v0 + s)
                wait_if(sp, gated, 2 * w + (s - 1))
                toks = bass.ds(c * P, P)
                sp.dma_start(rows[:, s], g.cum_d[:, toks].unsqueeze(0).broadcast_to([P, DH, P])).then_inc(rows_in[s], 16)
                sp.dma_start(cv[:, s], g.cv_d.rearrange("t p k -> p t k")[:, :, toks]).then_inc(loaded[s], 16)
                sp.dma_start(xt[:, s], g.tok_d[bass.ds(c, 1), :, 0:SW].rearrange("o p f -> p (o f)")).then_inc(loaded[s], 16)
                sp.dma_start(h[:, s], g.h_d[:, bass.ds(c, 1)].rearrange("d o p f -> p d (o f)")).then_inc(loaded[s], 16)
                sp.dma_start(z[:, s], g.zx_d[0:4].rearrange("t p k -> p t k")[:, :, toks]).then_inc(loaded[s], 16)
            steps(body, sp)

        @block.tensor
        def _(pe):
            def body(w, s):
                pe.wait_ge(loaded[s], 16 * LOADS * w + 16 * LOADS)
                wait_if(pe, masked, 2 * w + (s - 1))
                for q in range(NG):
                    last = nc.tensor.matmul(ps_c[:, s, q], cv[:, s, 4 + q], cv[:, s, 6 + q], start=True, stop=True)
                last.then_inc(crossed, 1)
                pe.wait_ge(x_scaled, 2 * w + (s + 1))
                pe.wait_ge(c_scaled, 2 * w + (s + 1))
                pe.wait_ge(intra, 2 * w + (s + 1))
                wait_if(pe, added, 2 * w + (s - 1))
                for t in range(4):
                    for e in range(2):
                        hd = 2 * t + e
                        out = ps_y[64 * e:64 * e + 64, s, t]
                        cols = slice(64 * hd, 64 * hd + 64)
                        for d in range(2):
                            nc.tensor.matmul(out, xdt[:, s, d, cols], seg[:, s, SH * d + hd], start=d == 0, stop=False)
                            last = nc.tensor.matmul(out, h[:, s, d, cols], er[:, s, SH * d + hd], start=False, stop=d == 1)
                last.then_inc(summed, 1)
            steps(body, pe)

        @block.scalar
        def _(act):
            def body(w, s):
                act.wait_ge(rows_in[s], 16 * w + 16)
                wait_if(act, summed, 2 * w + (s - 1))
                nc.scalar.activation(er[:, s], rows[:, s], ACT.Exp).then_inc(row_decays, 1)
                act.wait_ge(diffed, 2 * w + (s + 1))
                nc.scalar.activation(seg[:, s], seg[:, s], ACT.Exp).then_inc(decays, 1)
            steps(body, act)

        @block.gpsimd
        def _(pool):
            def body(w, s):
                c = bass.ds(2 * w + (2 * v0 + s), 1)
                pool.wait_ge(loaded[s], 16 * LOADS * w + 16 * LOADS)
                wait_if(pool, summed, 2 * w + (s - 1))
                for d in range(2):
                    last = nc.gpsimd.tensor_tensor(xdt[:, s, d].rearrange("p (h e) -> p h e", h=SH), xt[:, s].rearrange("p (h e) -> p h e", h=SH),
                                                   m.dt_tok[:, c, d].rearrange("p o h -> p (o h)").unsqueeze(2).broadcast_to([P, SH, 64]), ALU.mult)
                last.then_inc(x_scaled, 1)
                pool.wait_ge(row_decays, 2 * w + (s + 1))
                for d in range(2):
                    view = er[:, s, SH * d:SH * d + SH].rearrange("p (q r) i -> p q r i", q=NG)
                    last = nc.gpsimd.tensor_tensor(view, view, cv[:, s, 6:8].unsqueeze(2).broadcast_to([P, NG, SH // NG, P]), ALU.mult)
                last.then_inc(c_scaled, 1)
            steps(body, pool)

        @block.vector
        def _(dve):
            def body(w, s):
                c = bass.ds(2 * w + (2 * v0 + s), 1)
                cum = m.cum_tok[:, c].rearrange("p o d h -> p (o d h)").unsqueeze(2).broadcast_to([P, DH, P])
                dve.wait_ge(rows_in[s], 16 * w + 16)
                wait_if(dve, summed, 2 * w + (s - 1))
                nc.vector.tensor_tensor(seg[:, s], rows[:, s], cum, ALU.min).then_inc(clipped, 1)
                dve.wait_ge(clipped, 2 * w + (s + 1))
                nc.vector.tensor_tensor(seg[:, s], seg[:, s], cum, ALU.subtract).then_inc(diffed, 1)
                dve.wait_ge(crossed, 2 * w + (s + 1))
                for d in range(2):
                    last = nc.vector.tensor_tensor(cbm[:, s, d], ps_c[:, s, 0:NG], g.masks[:, d].unsqueeze(1).broadcast_to([P, NG, P]), ALU.mult)
                last.then_inc(masked, 1)
                nc.vector.tensor_tensor(skip[:, s], cv[:, s, 0:4], g.dskip_b[:], ALU.mult).then_inc(skipped, 1)
                dve.wait_ge(masked, 2 * w + (s + 1))
                dve.wait_ge(decays, 2 * w + (s + 1))
                view = seg[:, s].rearrange("p (a r) i -> p a r i", r=SH // NG)
                nc.vector.tensor_tensor(view, view, cbm[:, s].rearrange("p d q i -> p (d q) i").unsqueeze(2).broadcast_to([P, 4, SH // NG, P]),
                                        ALU.mult).then_inc(intra, 1)
                dve.wait_ge(summed, 2 * w + (s + 1))
                dve.wait_ge(skipped, 2 * w + (s + 1))
                nc.vector.tensor_tensor(skip[:, s], skip[:, s], ps_y[:, s], ALU.add).then_inc(added, 1)
                dve.wait_ge(added, 2 * w + (s + 1))
                out = m.ssd[:, :, bass.ds((2 * w + (2 * v0 + s)) * P, P)]
                nc.vector.tensor_tensor(out, skip[:, s], z[:, s], ALU.mult).then_inc(gated, 1)
            steps(body, dve)


def output_stage(nc, g):
    tiles = LAT // P
    with Stage(nc, "output") as st:
        xt = st.sb("xt", [P, 2, KD, P])
        xtok = st.sb("xtok", [P, 2, KD, P])
        tp = st.ps("tp", [P, 2, KD, P])
        x_in = [st.sem(f"x_in{s}") for s in range(2)]
        stored = [st.sem(f"stored{s}") for s in range(2)]
        turned, copied = st.sem("turned"), st.sem("copied")
        block = st.block()

        @block.sync
        def _(sp):
            with sp.Fori(0, tiles // 2) as v:
                for s in range(2):
                    sp.wait_ge(turned, 2 * v + s + 1)
                    sp.dma_start(xt[:, s], g.xT.rearrange("(k p) t -> p k t", p=P)[:, :, bass.ds((2 * v + s) * P + CTX, P)]).then_inc(x_in[s], 16)

        @block.tensor
        def _(pe):
            pe.sem_inc(turned, 2)
            with pe.Fori(0, tiles // 2) as v:
                for s in range(2):
                    pe.wait_ge(x_in[s], 16 * v + 16)
                    pe.wait_ge(copied, 2 * v + s + 1)
                    for k in range(KD):
                        last = nc.tensor.transpose(tp[:, s, k], xt[:, s, k], g.ident[:])
                    last.then_inc(turned, 1)

        @block.vector
        def _(dve):
            dve.sem_inc(copied, 2)
            for s in range(2):
                dve.sem_inc(stored[s], 16)
            with dve.Fori(0, tiles // 2) as v:
                for s in range(2):
                    dve.wait_ge(turned, 2 * v + s + 3)
                    dve.wait_ge(stored[s], 16 * v + 16)
                    nc.vector.tensor_copy(xtok[:, s], tp[:, s]).then_inc(copied, 1)

        @block.scalar
        def _(act):
            with act.Fori(0, tiles // 2) as v:
                for s in range(2):
                    act.wait_ge(copied, 2 * v + s + 3)
                    act.dma_start(g.out[0, bass.ds((2 * v + s) * P, P), :].rearrange("p (k q) -> p k q", q=P), xtok[:, s]).then_inc(stored[s], 16)
            for s in range(2):
                act.wait_ge(stored[s], 16 * (tiles // 2 + 1))


class Names:
    pass


def backbone(nc, x_in, c, c_ctx, w_ada, b_ada, norm_g, w_in, conv_w, conv_b, a_log, dt_bias, d_skip,
             ssd_norm_g, diff_lambda, subln_g, w_out, w_ffn_in, w_ffn_out, ident, masks, rope, reset, out):
    g = Names()
    g.x_in, g.c, g.c_ctx, g.w_ada, g.b_ada, g.norm_g, g.w_in = x_in, c, c_ctx, w_ada, b_ada, norm_g, w_in
    g.conv_w, g.conv_b, g.a_log, g.dt_bias_d, g.d_skip = conv_w, conv_b, a_log, dt_bias, d_skip
    g.ssd_g, g.lam_d, g.sub_g, g.w_out, g.w_ffn_in, g.w_ffn_out = ssd_norm_g, diff_lambda, subln_g, w_out, w_ffn_in, w_ffn_out
    g.ident_d, g.masks_d, g.rope_d, g.reset_d, g.out = ident, masks, rope, reset, out
    g.xT = nc.dram_tensor("xT", [D_MODEL, T], F32).ap()
    g.zx_d = nc.dram_tensor("zx_d", [12, P, T], F32).ap()
    g.qk_d = nc.dram_tensor("qk_d", [2, QK_TILES, P, T], F32).ap()
    g.v_d = nc.dram_tensor("v_d", [2, HEADS, T, P], F32).ap()
    g.cv_d = nc.dram_tensor("cv_d", [8, P, T], F32).ap()
    g.tok_d = nc.dram_tensor("tok_d", [NT, P, SW + NG * P], F32).ap()
    g.cum_d = nc.dram_tensor("cum_d", [2 * SH, T], F32).ap()
    g.h_d = nc.dram_tensor("h_d", [2, NT, P, SW], F32).ap()
    with ExitStack() as ctx:
        def sb(name, shape):
            return ctx.enter_context(nc.sbuf_tensor(name, shape, F32))
        g.ident, g.masks, g.ones = sb("ident", [P, P]), sb("masks", [P, 2, P]), sb("ones", [P, P])
        g.cols_a, g.cols_b = sb("cols_a", [P, P]), sb("cols_b", [P, 21])
        g.mod, g.pre, g.post = sb("mod", [P, 2, 48]), sb("pre", [P, 2, 2, KD]), sb("post", [P, 2, 2, KD])
        g.a_neg, g.dt_bias = sb("a_neg", [DTP, 1]), sb("dt_bias", [DTP, 1])
        g.neg_lam, g.sub_col = sb("neg_lam", [P, 1]), sb("sub_col", [P, 1])
        g.dskip_b = sb("dskip_b", [P, 4, P])
        setup_stage(nc, g)
        for layer in range(2):
            ada_stage(nc, g, layer)
            chunks = range(3) if layer == 0 else range(1, 3)
            with ExitStack() as mixer:
                m = Names()

                def keep(stack, name, shape):
                    return stack.enter_context(nc.sbuf_tensor(f"{name}{layer}", shape, F32))
                m.dt = keep(mixer, "dt", [DTP, T])
                m.att = keep(mixer, "att", [P, HEADS, T])
                in_proj_stage(nc, g, m, layer)
                attention_stage(nc, g, m, layer)
                m.ssd = keep(mixer, "ssd", [P, 4, T])
                with ExitStack() as scan:
                    m.dt_tok, m.cum_tok, m.w_tok, m.etot = (keep(scan, x, [P, NT, 2, SH]) for x in ("dt_tok", "cum_tok", "w_tok", "etot"))
                    scan_prep_stage(nc, g, layer, m)
                    scan_state_stage(nc, g, m, layer)
                    scan_out_stage(nc, g, m, layer)
                for ci in chunks:
                    out_proj_stage(nc, g, m, layer, ci)
            ffn_stage(nc, g, layer, chunks)
        output_stage(nc, g)


_INS = ["c", "c_ctx", "w_ada", "b_ada", "norm_g", "w_in", "conv_w", "conv_b", "a_log", "dt_bias", "d_skip",
        "ssd_norm_g", "diff_lambda", "subln_g", "w_out", "w_ffn_in", "w_ffn_out"]


def _constants():
    import numpy as np
    f = np.float32
    ident = np.eye(P, dtype=f)
    upper = np.triu(np.ones((P, P), f))
    masks = np.stack([upper, np.ascontiguousarray(upper.T)])
    row = np.repeat(np.arange(LAT // 64, dtype=f), 64)
    col = np.tile(np.arange(64, dtype=f), LAT // 64)
    inv = (f(10000.0) ** (-np.arange(16, dtype=f) / f(16))).astype(f)
    ang = np.concatenate([row[:, None] * inv, col[:, None] * inv], axis=-1).T
    cos, sin = np.cos(ang).astype(f), np.sin(ang).astype(f)
    rope = np.zeros((2, P, T), f)
    rope[0, :, 0:CTX] = 1.0
    rope[0, :, CTX:] = np.tile(cos, (4, 1))
    rope[1, :, CTX:] = np.concatenate([-sin, sin, -sin, sin])
    reset = np.ones((DTP, T), f)
    reset[:, ::P] = 0.0
    return {"ident": ident, "masks": masks, "rope": rope, "reset": reset}


def kernel(**inputs):
    import numpy as _np
    import concourse.bacc as _bacc
    from concourse import mybir as _mybir
    from concourse.bass_utils import run_bass_kernel_spmd as _run

    nc = _bacc.Bacc("TRN2", target_bir_lowering=False, num_devices=1)
    given = {"x_in": _np.concatenate([inputs["ctx"][0], inputs["x"][0]], axis=0)}
    given.update({name: inputs[name] for name in _INS})
    given.update(_constants())
    arrays, args = {}, []
    for name, a in given.items():
        a = _np.ascontiguousarray(a)
        arrays[f"in_{name}_dram"] = a
        args.append(nc.dram_tensor(f"in_{name}_dram", a.shape, _mybir.dt.from_np(a.dtype), kind="ExternalInput").ap())
    args.append(nc.dram_tensor("out_0_dram", (1, LAT, D_MODEL), F32, kind="ExternalOutput").ap())
    backbone(nc, *args)
    r = _run(nc, [arrays], core_ids=[0])
    return r.results[0]["out_0_dram"]
```

```python
from contextlib import ExitStack, contextmanager

import concourse.bass as bass
from concourse import mybir

F32 = mybir.dt.float32
F32R = mybir.dt.float32r
ALU = mybir.AluOpType
ACT = mybir.ActivationFunctionType
AX = mybir.AxisListType

P = 128
D_MODEL = 1024
KD = D_MODEL // P
CTX, LAT = 256, 1024
T = CTX + LAT
NT = T // P
HEADS = 4
SH = 8
SW = 512
NG = 2
DFF = 2816
KF = DFF // P
QK_TILES = 8
V_END = 1536
XBC0 = 2048
DT0 = 3072
IN_COLS = 3088
DTP = 40
BWD = 32
EPS = 1e-6
CHUNKS = [(0, 256), (256, 512), (768, 512)]
LAM_INIT = [0.2, 0.8 - 0.6 * 0.7408182206817179]
ROW_ADA, ROW_NG, ROW_CW, ROW_CB = 0, 48, 80, 120
ROW_SG, ROW_SUB, ROW_C = 0, 4, 5
SH1, SC1, G1, SH2, SC2, G2 = range(6)


class Chain:

    def __init__(self, eng, sem):
        self.eng, self.sem, self.n, self.off = eng, sem, 0, 0

    def __call__(self, ins):
        self.n += 1
        ins.then_inc(self.sem, 1)
        self.eng.wait_ge(self.sem, self.off + self.n)

    @contextmanager
    def over(self, i, count, per):
        start, self.off = self.n, i * per
        yield
        assert self.n - start == per, (self.n - start, per)
        self.n, self.off = start + per * count, 0


class Stage:

    def __init__(self, nc, name):
        self.nc, self.name, self.ctx, self.sems = nc, name, ExitStack(), []

    def __enter__(self):
        self.ctx.__enter__()
        return self

    def __exit__(self, *a):
        done = self.ctx.__exit__(*a)
        if a[0] is None:
            self.nc.clear_and_free_semaphores(self.sems)
            self.nc.all_engine_barrier()
        return done

    def sb(self, name, shape, dt=F32):
        return self.ctx.enter_context(self.nc.sbuf_tensor(f"{self.name}_{name}", shape, dt))

    def ps(self, name, shape):
        return self.ctx.enter_context(self.nc.psum_tensor(f"{self.name}_{name}", shape, F32))

    def sem(self, name):
        self.sems.append(self.nc.alloc_semaphore(f"{self.name}_{name}"))
        return self.sems[-1]

    def block(self):
        return self.ctx.enter_context(self.nc.Block())


class WeightRing:

    def __init__(self, st, tiles=KD, width=P):
        self.raw = st.sb("w_raw", [P, 2, tiles, width])
        self.hi = st.sb("w_hi", [P, 2, tiles, width], F32R)
        self.lo = st.sb("w_lo", [P, 2, tiles, width], F32R)
        self.landed = [st.sem(f"w_landed{s}") for s in range(2)]
        self.rounded, self.split, self.used = st.sem("w_rounded"), st.sem("w_split"), st.sem("w_used")

    def start_vector(self, dve):
        dve.sem_inc(self.split, 2)

    def start_tensor(self, pe):
        pe.sem_inc(self.used, 2)

    def load(self, sp, v, s, src, tiles=KD):
        sp.wait_ge(self.split, 2 * v + s + 1)
        sp.dma_start(self.raw[:, s, 0:tiles], src).then_inc(self.landed[s], 16)

    def round(self, act, nc, v, s, tiles=KD):
        act.wait_ge(self.landed[s], 16 * v + 16)
        act.wait_ge(self.used, 2 * v + s + 1)
        nc.scalar.activation(self.hi[:, s, 0:tiles], self.raw[:, s, 0:tiles], ACT.Copy).then_inc(self.rounded, 1)

    def rest(self, dve, nc, v, s, tiles=KD):
        dve.wait_ge(self.rounded, 2 * v + s + 1)
        nc.vector.tensor_tensor(self.lo[:, s, 0:tiles], self.raw[:, s, 0:tiles], self.hi[:, s, 0:tiles],
                                ALU.subtract).then_inc(self.split, 1)

    def ready(self, pe, v, s):
        pe.wait_ge(self.split, 2 * v + s + 3)

    def count_used(self, v, s):
        return 2 * v + s + 3


def product3(nc, out, w_hi, w_lo, x_hi, x_lo, tiles, first=True, last=True, each=lambda k: None):
    for k in range(tiles):
        each(k)
        a, b = first and k == 0, last and k == tiles - 1
        nc.tensor.matmul(out, w_hi[:, k], x_hi[:, k], start=a, stop=False)
        nc.tensor.matmul(out, w_hi[:, k], x_lo[:, k], start=False, stop=False)
        ins = nc.tensor.matmul(out, w_lo[:, k], x_hi[:, k], start=False, stop=b)
    return ins


class RowNorm:

    def __init__(self, st, name, n, features, psum, ones, bufs, sum_at=0):
        self.n, self.features, self.psum, self.ones = n, features, psum, ones
        self.ss, self.m, self.r = (bufs[:, i, 0:n] for i in (sum_at, 1, 2))
        self.total, self.mean, self.guess = (st.sem(f"{name}_{x}") for x in ("total", "mean", "guess"))

    def add_partitions(self, nc):
        nc.tensor.matmul(self.psum[:, 0:self.n], self.ones[:], self.ss, start=True, stop=True).then_inc(self.total, 1)

    def mean_eps(self, dve, nc):
        dve.wait_ge(self.total, 1)
        nc.vector.tensor_scalar(self.m, self.psum[:, 0:self.n], 1.0 / self.features, EPS,
                                ALU.mult, ALU.add).then_inc(self.mean, 1)

    def root(self, act, nc, chain):
        act.wait_ge(self.mean, 1)
        chain(nc.scalar.activation(self.r, self.m, ACT.Ln))
        nc.scalar.activation(self.r, self.r, ACT.Exp, scale=-0.5).then_inc(self.guess, 1)

    def refine(self, dve, nc, chain):
        dve.wait_ge(self.guess, 1)
        chain(nc.vector.tensor_tensor(self.ss, self.r, self.r, ALU.mult))
        chain(nc.vector.scalar_tensor_tensor(self.ss, self.ss, -0.5, self.m, ALU.mult, ALU.mult))
        chain(nc.vector.scalar_tensor_tensor(self.r, self.ss, 1.5, self.r, ALU.add, ALU.mult))


def setup_stage(nc, g):
    with Stage(nc, "setup") as st:
        xtok = st.sb("xtok", [P, 2, D_MODEL])
        xt = st.sb("xt", [P, 2, KD, P])
        tp = st.ps("tp", [P, 2, KD, P])
        const_in = st.sem("const_in")
        x_in = [st.sem(f"x_in{s}") for s in range(2)]
        turned, copied = st.sem("turned"), st.sem("copied")
        stored = [st.sem(f"stored{s}") for s in range(2)]
        block = st.block()

        @block.sync
        def _(sp):
            sp.dma_start(g.ident[:], g.ident_d).then_inc(const_in, 16)
            sp.dma_start(g.masks[:], g.masks_d.rearrange("d j i -> j d i")).then_inc(const_in, 16)
            with sp.Fori(0, NT // 2) as v:
                for s in range(2):
                    sp.wait_ge(turned, 2 * v + s + 1)
                    sp.dma_start(xtok[:, s], g.x_in[bass.ds((2 * v + s) * P, P), :]).then_inc(x_in[s], 16)

        @block.tensor
        def _(pe):
            pe.sem_inc(turned, 2)
            pe.wait_ge(const_in, 32)
            with pe.Fori(0, NT // 2) as v:
                for s in range(2):
                    pe.wait_ge(x_in[s], 16 * v + 16)
                    pe.wait_ge(copied, 2 * v + s + 1)
                    for k in range(KD):
                        last = nc.tensor.transpose(tp[:, s, k], xtok[:, s, k * P:(k + 1) * P], g.ident[:])
                    last.then_inc(turned, 1)

        @block.vector
        def _(dve):
            dve.sem_inc(copied, 2)
            nc.vector.memset(g.ones[:], 1.0)
            for s in range(2):
                dve.sem_inc(stored[s], 16)
            with dve.Fori(0, NT // 2) as v:
                for s in range(2):
                    dve.wait_ge(turned, 2 * v + s + 3)
                    dve.wait_ge(stored[s], 16 * v + 16)
                    nc.vector.tensor_copy(xt[:, s], tp[:, s]).then_inc(copied, 1)

        @block.scalar
        def _(act):
            with act.Fori(0, NT // 2) as v:
                for s in range(2):
                    act.wait_ge(copied, 2 * v + s + 3)
                    act.dma_start(g.xT.rearrange("(k p) t -> p k t", p=P)[:, :, bass.ds((2 * v + s) * P, P)],
                                  xt[:, s]).then_inc(stored[s], 16)
            for s in range(2):
                act.wait_ge(stored[s], 16 * (NT // 2 + 1))


def ada_stage(nc, g, layer):
    STEP = 512
    steps = 6 * D_MODEL // STEP
    sub = STEP // P
    with Stage(nc, f"ada{layer}") as st:
        rows_a = st.sb("rows_a", [P, P])
        rows_b = st.sb("rows_b", [21, P])
        lam_in = st.sb("lam_in", [P, 4, 64])
        lam_t = st.sb("lam_t", [P, 2, 64])
        skip_in = st.sb("skip_in", [P, SH])
        lam_s = st.sb("lam_s", [P, 2])
        silu_c = st.sb("silu_c", [P, KD, 2])
        e_c = st.sb("e_c", [P, 2 * KD])
        wa = st.sb("wa", [P, 2, KD, STEP])
        psv = st.ps("psv", [P, 2, P])
        row = st.sb("row", [2, 2, STEP])
        psr = st.ps("psr", [2, 2, 512])
        psm = st.ps("psm", [P, 2, 512])
        vec_in, lam_land = st.sem("vec_in"), st.sem("lam_land")
        wa_in = [st.sem(f"wa_in{s}") for s in range(2)]
        turned, cols_done, c_exp, c_silu = st.sem("turned"), st.sem("cols_done"), st.sem("c_exp"), st.sem("c_silu")
        columns = st.sem("columns")
        done, mod_done, lam_sum, lam_exp = st.sem("done"), st.sem("mod_done"), st.sem("lam_sum"), st.sem("lam_exp")
        a_land, a_exp = st.sem("a_land"), st.sem("a_exp")
        row_done = st.sem("row_done")
        chain_v = st.sem("chain_v")
        block = st.block()

        @block.sync
        def _(sp):
            for row, src in ((ROW_ADA, g.b_ada[layer].rearrange("(r q) -> r q", q=P)),
                             (ROW_NG, g.norm_g[layer].rearrange("v (r q) -> (v r) q", q=P)),
                             (ROW_CW, g.conv_w[layer].rearrange("v (r q) -> (v r) q", q=P)),
                             (ROW_CB, g.conv_b[layer].rearrange("(r q) -> r q", q=P))):
                sp.dma_start(rows_a[row:row + src.shape[0]], src).then_inc(vec_in, 16)
            for row, src in ((ROW_SG, g.ssd_g[layer].rearrange("(r q) -> r q", q=P)),
                             (ROW_SUB, g.sub_g[layer].rearrange("(r q) -> r q", q=P)),
                             (ROW_C, g.c_ctx.rearrange("(r q) -> r q", q=P)),
                             (ROW_C + KD, g.c.rearrange("b (r q) -> (b r) q", q=P))):
                sp.dma_start(rows_b[row:row + src.shape[0]], src).then_inc(vec_in, 16)
            with sp.Fori(0, steps // 2) as v:
                for s in range(2):
                    sp.wait_ge(done, 2 * v + s + 1)
                    sp.dma_start(wa[:, s], g.w_ada[layer].rearrange("(k p) n -> p k n", p=P)[
                        :, :, bass.ds((2 * v + s) * STEP, STEP)]).then_inc(wa_in[s], 16)

        @block.gpsimd
        def _(pool):
            pool.dma_start(g.a_neg[:], g.a_log[layer:layer + 1].to_broadcast([P, 2, SH])).then_inc(a_land, 16)
            pool.dma_start(g.dt_bias[:], g.dt_bias_d[layer:layer + 1].to_broadcast([P, 2, SH])).then_inc(a_land, 16)
            pool.dma_start(skip_in[:], g.d_skip[layer:layer + 1].to_broadcast([P, SH])).then_inc(a_land, 16)
            pool.dma_start(lam_in[:], g.lam_d[layer:layer + 1].to_broadcast([P, 4, 64])).then_inc(lam_land, 16)
            pool.wait_ge(lam_land, 16)
            pool.wait_ge(a_land, 16 * 3)

        @block.tensor
        def _(pe):
            pe.sem_inc(done, 2)
            pe.wait_ge(row_done, 2)
            pe.wait_ge(vec_in, 16 * 8)
            nc.tensor.transpose(psv[:, 0], rows_a[:], g.ident[:])
            nc.tensor.transpose(psv[:, 1, 0:21], rows_b[:], g.ident[0:21, 0:21]).then_inc(turned, 1)
            pe.wait_ge(c_silu, 1)
            with pe.Fori(0, steps // 2) as v:
                for s in range(2):
                    pe.wait_ge(wa_in[s], 16 * v + 16)
                    pe.wait_ge(row_done, 2 * v + s + 1)
                    for k in range(KD):
                        last = nc.tensor.matmul(psr[:, s, 0:STEP], silu_c[:, k], wa[:, s, k], start=k == 0, stop=k == KD - 1)
                    last.then_inc(done, 1)
                    pe.wait_ge(row_done, 2 * v + s + 3)
                    pe.wait_ge(mod_done, 2 * v + s + 1)
                    for j in range(sub):
                        last = nc.tensor.matmul(psm[:, s, 2 * j:2 * j + 2], row[:, s, j * P:(j + 1) * P], g.ident[0:2, 0:2],
                                                start=True, stop=True)
                    last.then_inc(columns, 1)

        @block.scalar
        def _(act):
            act.sem_inc(row_done, 2)
            act.wait_ge(cols_done, 1)
            nc.scalar.activation(e_c[:], g.cols_b[:, ROW_C:ROW_C + 2 * KD], ACT.Exp, scale=-1.0).then_inc(c_exp, 1)
            act.wait_ge(a_land, 16 * 3)
            nc.scalar.activation(g.a_neg[:], g.a_neg[:], ACT.Exp).then_inc(a_exp, 1)
            act.wait_ge(lam_sum, 1)
            nc.scalar.activation(lam_s[:], lam_s[:], ACT.Exp).then_inc(lam_exp, 1)
            with act.Fori(0, steps // 2) as v:
                for s in range(2):
                    act.wait_ge(done, 2 * v + s + 3)
                    nc.scalar.activation(row[:, s], psr[:, s, 0:STEP], ACT.Copy).then_inc(row_done, 1)

        @block.vector
        def _(dve):
            chain = Chain(dve, chain_v)
            dve.sem_inc(mod_done, 2)
            dve.wait_ge(turned, 1)
            nc.vector.tensor_copy(g.cols_a[:], psv[:, 0])
            nc.vector.tensor_copy(g.cols_b[:], psv[:, 1, 0:21]).then_inc(cols_done, 1)
            dve.wait_ge(c_exp, 1)
            chain(nc.vector.tensor_scalar_add(e_c[:], e_c[:], 1.0))
            chain(nc.vector.reciprocal(e_c[:], e_c[:]))
            nc.vector.tensor_tensor(silu_c.rearrange("p k v -> p v k"), g.cols_b[:, ROW_C:ROW_C + 2 * KD].rearrange("p (v k) -> p v k", v=2),
                                    e_c.rearrange("p (v k) -> p v k", v=2), ALU.mult).then_inc(c_silu, 1)
            dve.wait_ge(a_exp, 1)
            chain(nc.vector.tensor_scalar(g.a_neg[:], g.a_neg[:], -1.0, None, ALU.mult))
            dve.wait_ge(lam_land, 16)
            pairs = lam_in.rearrange("p (a b) d -> p a b d", b=2)
            chain(nc.vector.tensor_tensor(lam_t[:], pairs[:, :, 0], pairs[:, :, 1], ALU.mult))
            nc.vector.tensor_reduce(lam_s[:], lam_t[:], AX.X, ALU.add).then_inc(lam_sum, 1)
            dve.wait_ge(lam_exp, 1)
            chain(nc.vector.tensor_tensor(g.neg_lam[:], lam_s[:, 1:2], lam_s[:, 0:1], ALU.subtract))
            chain(nc.vector.tensor_scalar_add(g.neg_lam[:], g.neg_lam[:], -LAM_INIT[layer]))
            chain(nc.vector.tensor_scalar(g.sub_col[:], g.cols_b[:, ROW_SUB:ROW_SUB + 1], 1.0 - LAM_INIT[layer], None, ALU.mult))
            for e in range(2):
                half = slice(64 * e, 64 * e + 64)
                chain(nc.vector.tensor_copy(g.dskip_b[half], skip_in[half].rearrange("p (t e) -> p t e", e=2)[:, :, e:e + 1].broadcast_to([64, 4, P])))
            with dve.Fori(0, steps // 2) as v:
                for s in range(2):
                    dve.wait_ge(columns, 2 * v + s + 1)
                    cols = bass.ds((2 * v + s) * sub, sub)
                    nc.vector.tensor_tensor(g.mod[:, :, cols], psm[:, s, 0:2 * sub].rearrange("p (j v) -> p v j", v=2),
                                            g.cols_a[:, cols].unsqueeze(1).broadcast_to([P, 2, sub]), ALU.add).then_inc(mod_done, 1)
            dve.wait_ge(mod_done, steps + 2)
            for which, scale, norm in ((0, SC1, 0), (1, SC2, 2)):
                chain(nc.vector.scalar_tensor_tensor(
                    g.pre[:, which], g.mod[:, :, scale * KD:(scale + 1) * KD], 1.0,
                    g.cols_a[:, ROW_NG + norm * KD:ROW_NG + (norm + 1) * KD].unsqueeze(1).broadcast_to([P, 2, KD]), ALU.add, ALU.mult))
            for which, gate, norm in ((0, G1, 1), (1, G2, 3)):
                chain(nc.vector.tensor_tensor(
                    g.post[:, which], g.mod[:, :, gate * KD:(gate + 1) * KD],
                    g.cols_a[:, ROW_NG + norm * KD:ROW_NG + (norm + 1) * KD].unsqueeze(1).broadcast_to([P, 2, KD]), ALU.mult))


class Prenorm:

    def __init__(self, st, g, name, n, psum, x, sq, norm_bufs, hi, lo):
        self.g, self.n = g, n
        self.x, self.sq, self.hi, self.lo = x[:, :, 0:n], sq[:, :, 0:n], hi[:, :, 0:n], lo[:, :, 0:n]
        self.x_in, self.squared, self.added, self.scaled, self.rounded, self.ready = (st.sem(f"{name}_{x}") for x in (
            "x_in", "squared", "added", "scaled", "h_rounded", "h_ready"))
        self.norm = RowNorm(st, name, n, D_MODEL, psum, g.ones, norm_bufs)

    def load(self, eng, c0):
        eng.dma_start(self.x, self.g.xT.rearrange("(k p) t -> p k t", p=P)[:, :, c0:c0 + self.n]).then_inc(self.x_in, 16)

    def square(self, act, nc, k):
        if k == 0:
            act.wait_ge(self.x_in, 16)
        if k >= 3:
            act.wait_ge(self.added, k - 2)
        nc.scalar.activation(self.sq[:, k % 2] if k else self.norm.ss, self.x[:, k], ACT.Square).then_inc(self.squared, 1)

    def add(self, eng, ops, k):
        eng.wait_ge(self.squared, k + 1)
        if k > 1:
            eng.wait_ge(self.added, k - 1)
        ops.tensor_tensor(self.norm.ss, self.norm.ss, self.sq[:, k % 2], ALU.add).then_inc(self.added, 1)

    def total(self, pe, nc):
        pe.wait_ge(self.added, KD - 1)
        self.norm.add_partitions(nc)

    def high(self, act, nc, k, shift):
        act.wait_ge(self.scaled, k + 1)
        nc.scalar.activation(self.hi[:, k], self.x[:, k], ACT.Identity, bias=shift[:, k:k + 1]).then_inc(self.rounded, 1)

    def scale(self, nc, k, scale):
        nc.vector.scalar_tensor_tensor(self.x[:, k], self.x[:, k], scale[:, k:k + 1], self.norm.r,
                                       ALU.mult, ALU.mult).then_inc(self.scaled, 1)

    def low(self, dve, nc, k, shift):
        dve.wait_ge(self.scaled, k + 1)
        dve.wait_ge(self.rounded, k + 1)
        nc.vector.scalar_tensor_tensor(self.lo[:, k], self.x[:, k], shift[:, k:k + 1], self.hi[:, k],
                                       ALU.add, ALU.subtract).then_inc(self.ready, 1)

    SCALAR_STEPS, VECTOR_STEPS = 5 + KD, 3 + KD

    def scalar_step(self, act, nc, chain, shift, i):
        if i < 4:
            self.square(act, nc, 2 * i)
            self.square(act, nc, 2 * i + 1)
        elif i == 4:
            self.norm.root(act, nc, chain)
        else:
            self.high(act, nc, i - 5, shift)

    def vector_step(self, dve, nc, chain, scale, shift, i):
        if i == 0:
            self.norm.mean_eps(dve, nc)
        elif i == 1:
            self.norm.refine(dve, nc, chain)
        else:
            if i < KD + 2:
                self.scale(nc, i - 2, scale)
            if i > 2:
                self.low(dve, nc, i - 3, shift)

    def scalar(self, act, nc, chain, shift):
        for i in range(self.SCALAR_STEPS):
            self.scalar_step(act, nc, chain, shift, i)

    def vector(self, dve, nc, chain, scale, shift):
        for k in range(1, KD):
            self.add(dve, nc.vector, k)
        for i in range(self.VECTOR_STEPS):
            self.vector_step(dve, nc, chain, scale, shift, i)


class Residual:

    def __init__(self, st, g, name, n, psum, f, x, tmp, norm_bufs, sum_at=0):
        self.g, self.n, self.f, self.x, self.tmp = g, n, f[:, :, 0:n], x[:, :, 0:n], tmp[:, :, 0:n]
        self.x_in, self.scaled, self.summed, self.out, self.zeroed, self.squared, self.added, self.copied = (
            st.sem(f"{name}_{x}") for x in ("in", "scaled", "summed", "out", "zeroed", "squared", "added", "copied"))
        self.drained = [st.sem(f"{name}_drained{s}") for s in range(2)]
        self.norm = RowNorm(st, name, n, D_MODEL, psum, g.ones, norm_bufs, sum_at)

    def view(self, c0):
        return self.g.xT.rearrange("(k p) t -> p k t", p=P)[:, :, c0:c0 + self.n]

    def load(self, eng, c0):
        eng.dma_start(self.x, self.view(c0)).then_inc(self.x_in, 16)

    def start_vector(self, dve):
        for s in range(2):
            dve.sem_inc(self.drained[s], 1)

    def square_tile(self, act, nc, o, half):
        act.wait_ge(self.copied, 2 * o + (half + 1))
        act.wait_ge(self.added, 2 * o + (half + 1))
        nc.scalar.activation(self.tmp[:, half], self.f[:, bass.ds(2 * o + half, 1)].rearrange("p o t -> p (o t)"),
                             ACT.Square).then_inc(self.squared, 1)

    def copy_tile(self, dve, nc, o, half, src):
        nc.vector.tensor_copy(self.f[:, bass.ds(2 * o + half, 1)].rearrange("p o t -> p (o t)"), src).then_inc(self.copied, 1)
        dve.wait_ge(self.copied, 2 * o + (half + 1))
        dve.sem_inc(self.drained[half], 1)

    def bank_free(self, pe, o, half):
        pe.wait_ge(self.drained[half], o + 1)

    def start_sum(self, pool, nc):
        pool.sem_inc(self.added, 2)
        nc.gpsimd.memset(self.norm.ss, 0.0).then_inc(self.zeroed, 1)
        pool.wait_ge(self.zeroed, 1)

    def add_square(self, pool, nc, k):
        pool.wait_ge(self.squared, k + 1)
        pool.wait_ge(self.added, k + 2)
        nc.gpsimd.tensor_tensor(self.norm.ss, self.norm.ss, self.tmp[:, k % 2], ALU.add).then_inc(self.added, 1)

    def sum_squares(self, pool, nc):
        self.start_sum(pool, nc)
        with pool.Fori(0, KD // 2) as o:
            for half in range(2):
                pool.wait_ge(self.squared, 2 * o + (half + 1))
                pool.wait_ge(self.added, 2 * o + (half + 2))
                nc.gpsimd.tensor_tensor(self.norm.ss, self.norm.ss, self.tmp[:, half], ALU.add).then_inc(self.added, 1)

    def add(self, pool, nc, start=0, end=KD):
        pool.wait_ge(self.x_in, 16)
        for k in range(start, end):
            pool.wait_ge(self.scaled, k + 1)
            nc.gpsimd.tensor_tensor(self.x[:, k], self.x[:, k], self.f[:, k], ALU.add).then_inc(self.summed, 1)

    def tensor(self, pe, nc):
        pe.wait_ge(self.added, KD + 2)
        self.norm.add_partitions(nc)

    def scale(self, nc, gate, start=0, end=KD):
        for k in range(start, end):
            nc.vector.scalar_tensor_tensor(self.f[:, k], self.f[:, k], gate[:, k:k + 1], self.norm.r,
                                           ALU.mult, ALU.mult).then_inc(self.scaled, 1)

    def vector(self, dve, nc, chain, gate):
        self.norm.mean_eps(dve, nc)
        self.norm.refine(dve, nc, chain)
        self.scale(nc, gate)

    def store(self, eng, c0):
        eng.wait_ge(self.summed, KD)
        eng.dma_start(self.view(c0), self.x).then_inc(self.out, 16)
        eng.wait_ge(self.out, 16)


def in_proj_stage(nc, g, m, layer):
    N = CHUNKS[-1][1]
    C = len(CHUNKS)
    w_view = g.w_in[layer].rearrange("(k p) n -> p k n", p=P)
    QK, QKV, ALL = 4, 6, 12
    SPLIT, ZX = 2 * QKV, 2 * (ALL - QKV)
    SCALAR_AT = {0: (0,), 1: (1,), 2: (2,), 3: (3,), 7: (4,), 8: (5,), 9: (6, 7), 10: (8,), 11: (9, 10), 12: (11,), 13: (12,)}
    VECTOR_AT = {6: (0,), 7: (1,), 8: (2,), 9: (3, 4), 10: (5,), 11: (6, 7), 12: (8,), 13: (9,), 14: (10,)}
    TOTAL_AT = 1
    with Stage(nc, f"in{layer}") as st:
        psn = st.ps("psn", [P, 512])
        psd = st.ps("psd", [P, 512])
        psu = st.ps("psu", [P, 2, 512])
        x, sq, pre_bufs = st.sb("x", [P, KD, N]), st.sb("sq", [P, 2, N]), st.sb("pre_bufs", [P, 3, N])
        h_hi, h_lo = st.sb("h_hi", [P, 2, KD, N], F32R), st.sb("h_lo", [P, 2, KD, N], F32R)
        pres = [Prenorm(st, g, f"pre{i}", n, psn, x, sq, pre_bufs, h_hi[:, i % 2], h_lo[:, i % 2]) for i, (_, n) in enumerate(CHUNKS)]
        ring = WeightRing(st)
        rope, swap, turn, stage = (st.sb(x, [P, 2, N]) for x in ("rope", "swap", "turn", "stage"))
        split_hi = st.sb("split_hi", [P, 2, N], F32R)
        split_lo = st.sb("split_lo", [P, 2, N])
        wdt = st.sb("wdt", [P, KD, P])
        wdt_hi = st.sb("wdt_hi", [P, KD, P], F32R)
        wdt_lo = st.sb("wdt_lo", [P, KD, P], F32R)
        rope_in, dt_in, dt_zero, dt_round, dt_split, dt_done, dt_out = (st.sem(x) for x in (
            "rope_in", "dt_in", "dt_zero", "dt_round", "dt_split", "dt_done", "dt_out"))
        drained = [st.sem(f"drained{s}") for s in range(2)]
        swapped, cos_made, sin_made, turned, hi_made, lo_made, v_hi, v_lo, staged = (st.sem(x) for x in (
            "swapped", "cos_made", "sin_made", "turned", "hi_made", "lo_made", "v_hi", "v_lo", "staged"))
        split_out = [st.sem(f"split_out{s}") for s in range(2)]
        stored = [st.sem(f"stored{s}") for s in range(2)]
        chain_v, chain_a = st.sem("chain_v"), st.sem("chain_a")
        streams = [0 if i == 0 else 1 for i in range(C)]
        shifts = [g.mod[:, s, SH1 * KD:(SH1 + 1) * KD] for s in streams]
        scales = [g.pre[:, 0, s] for s in streams]
        block = st.block()

        @block.sync
        def _(sp):
            sp.wait_ge(dt_zero, 1)
            for d in range(2):
                sp.dma_start(wdt[:, :, BWD * d:BWD * d + SH], w_view[:, :, DT0 + SH * d:DT0 + SH * (d + 1)]).then_inc(dt_in, 16)

            def load_rope(i):
                c0, n = CHUNKS[i]
                sp.dma_start(rope[:, :, 0:n], g.rope_d.rearrange("r p t -> p r t")[:, :, c0:c0 + n]).then_inc(rope_in, 16)
            for v in range(2):
                for s in range(2):
                    ring.load(sp, v, s, w_view[:, :, (2 * v + s) * P:(2 * v + s + 1) * P])
                if v == 0:
                    load_rope(0)
            for i, (c0, n) in enumerate(CHUNKS):
                with sp.Fori(0, QK) as v:
                    for s in range(2):
                        ring.load(sp, v + (ALL * i + 2), s, w_view[:, :, bass.ds((2 * v + (4 + s)) * P, P)])
                        sp.wait_ge(lo_made, 2 * v + (2 * QK * i + s + 1))
                        for part, src in enumerate((split_hi[:, s, 0:n].bitcast(F32), split_lo[:, s, 0:n])):
                            sp.dma_start(g.qk_d[part, bass.ds(2 * v + s, 1), :, c0:c0 + n].rearrange("o p t -> p (o t)"),
                                         src).then_inc(split_out[s], 16)
                for v in range(QK, QKV):
                    for s in range(2):
                        ring.load(sp, ALL * i + v + 2, s, w_view[:, :, (2 * v + 4 + s) * P:(2 * v + 5 + s) * P])
                        sp.wait_ge(v_lo, 2 * (QKV - QK) * i + 2 * (v - QK) + s + 1)
                        for part, src in enumerate((split_hi[:, s, 0:n].bitcast(F32), split_lo[:, s, 0:n])):
                            sp.dma_start(g.v_d[part, 2 * (v - QK) + s, c0:c0 + n].rearrange("(t p) e -> p t e", p=P),
                                         src.rearrange("p (t e) -> p t e", e=P)).then_inc(split_out[s], 16)
                if i + 1 < C:
                    load_rope(i + 1)

                def store(j, s):
                    sp.wait_ge(staged, 2 * j + (ZX * i + s + 1))
                    sp.dma_start(g.zx_d[bass.ds(2 * j + s, 1), :, c0:c0 + n].rearrange("o p t -> p (o t)"),
                                 stage[:, s, 0:n]).then_inc(stored[s], 16)
                with sp.Fori(0, ALL - QKV - 2) as j:
                    for s in range(2):
                        ring.load(sp, j + (ALL * i + QKV + 2), s, w_view[:, :, bass.ds((2 * j + (2 * QKV + 4 + s)) * P, P)])
                        store(j, s)
                for v in range(2):
                    for s in range(2):
                        if i + 1 < C:
                            ring.load(sp, ALL * (i + 1) + v, s, w_view[:, :, (2 * v + s) * P:(2 * v + s + 1) * P])
                        store(ALL - QKV - 2 + v, s)
            for s in range(2):
                sp.wait_ge(stored[s], 16 + 16 * C * ZX // 2)
                sp.wait_ge(split_out[s], 32 + 32 * C * SPLIT // 2)

        @block.gpsimd
        def _(pool):
            pres[0].load(pool, CHUNKS[0][0])
            nc.gpsimd.memset(wdt[:], 0.0).then_inc(dt_zero, 1)
            for i, (c0, n) in enumerate(CHUNKS):
                pool.wait_ge(pres[i].ready, KD)
                if i + 1 < C:
                    pres[i + 1].load(pool, CHUNKS[i + 1][0])
                pool.wait_ge(rope_in, 16 * i + 16)
                with pool.Fori(0, QK) as v:
                    for s in range(2):
                        pool.wait_ge(swapped, 2 * v + (2 * QK * i + s + 1))
                        nc.gpsimd.tensor_tensor(swap[:, s, 0:n], swap[:, s, 0:n], rope[:, 1, 0:n], ALU.mult).then_inc(sin_made, 1)
                        pool.wait_ge(hi_made, 2 * v + (2 * QK * i + s + 1))
                        nc.gpsimd.tensor_tensor(split_lo[:, s, 0:n], turn[:, s, 0:n], split_hi[:, s, 0:n], ALU.subtract).then_inc(lo_made, 1)
                if i + 1 < C:
                    for k in range(1, KD):
                        pres[i + 1].add(pool, nc.gpsimd, k)

        @block.scalar
        def _(act):
            chain = Chain(act, chain_a)
            for s in range(2):
                act.sem_inc(stored[s], 16)
                act.sem_inc(split_out[s], 32)
            pres[0].scalar(act, nc, chain, shifts[0])
            for s in range(2):
                ring.round(act, nc, 0, s)
            act.wait_ge(dt_in, 32)
            nc.scalar.activation(wdt_hi[:], wdt[:], ACT.Copy).then_inc(dt_round, 1)
            for i, (c0, n) in enumerate(CHUNKS):
                with act.Fori(0, QK) as v:
                    for s in range(2):
                        ring.round(act, nc, v + (ALL * i + 1), s)
                        act.wait_ge(turned, 2 * v + (2 * QK * i + s + 1))
                        for a in range(4):
                            b = a ^ 1
                            last = nc.scalar.activation(swap[32 * a:32 * a + 32, s, 0:n], psu[32 * b:32 * b + 32, s, 0:n], ACT.Copy)
                        last.then_inc(swapped, 1)
                for v in range(QK, QKV):
                    for s in range(2):
                        ring.round(act, nc, ALL * i + v + 1, s)
                        act.wait_ge(split_out[s], 32 * (SPLIT // 2 * i + v) + 32)
                        nc.scalar.activation(split_hi[:, s, 0:n], psu[:, s, 0:n], ACT.Copy).then_inc(v_hi, 1)
                        if i + 1 < C:
                            for step in SCALAR_AT.get(2 * (v - QK) + s, ()):
                                pres[i + 1].scalar_step(act, nc, chain, shifts[i + 1], step)

                def unit(j, s, func, more=True):
                    if more:
                        ring.round(act, nc, j + (ALL * i + QKV + 1), s)
                    act.wait_ge(ring.used, 2 * j + (2 * (ALL * i + QKV) + s + 3))
                    act.wait_ge(stored[s], 16 * j + (16 * ZX // 2 * i + 16))
                    nc.scalar.activation(stage[:, s, 0:n], psu[:, s, 0:n], func).then_inc(staged, 1)
                    act.wait_ge(staged, 2 * j + (ZX * i + s + 1))
                    act.sem_inc(drained[s], 1)
                if i + 1 < C:
                    for j in range(ALL - QKV):
                        for s in range(2):
                            unit(j, s, ACT.Silu if j < 2 else ACT.Copy)
                            for step in SCALAR_AT.get(2 * (QKV - QK + j) + s, ()):
                                pres[i + 1].scalar_step(act, nc, chain, shifts[i + 1], step)
                else:
                    for start, end, func in ((0, 2, ACT.Silu), (2, ALL - QKV - 1, ACT.Copy)):
                        with act.Fori(start, end) as j:
                            for s in range(2):
                                unit(j, s, func)
                    for s in range(2):
                        unit(ALL - QKV - 1, s, ACT.Copy, False)
                act.wait_ge(dt_done, i + 1)
                nc.scalar.activation(m.dt[:, c0:c0 + n], psd[0:DTP, 0:n], ACT.Copy).then_inc(dt_out, 1)

        @block.vector
        def _(dve):
            chain = Chain(dve, chain_v)
            ring.start_vector(dve)
            dve.sem_inc(turned, 2)
            for s in range(2):
                dve.sem_inc(drained[s], 1)
            pres[0].vector(dve, nc, chain, scales[0], shifts[0])
            for s in range(2):
                ring.rest(dve, nc, 0, s)
            dve.wait_ge(dt_round, 1)
            nc.vector.tensor_tensor(wdt_lo[:], wdt[:], wdt_hi[:], ALU.subtract).then_inc(dt_split, 1)
            for i, (c0, n) in enumerate(CHUNKS):
                dve.wait_ge(rope_in, 16 * i + 16)
                with dve.Fori(0, QK) as v:
                    for s in range(2):
                        ring.rest(dve, nc, v + (ALL * i + 1), s)
                        dve.wait_ge(swapped, 2 * v + (2 * QK * i + s + 1))
                        dve.wait_ge(split_out[s], 32 * v + (32 * SPLIT // 2 * i + 32))
                        nc.vector.tensor_tensor(turn[:, s, 0:n], psu[:, s, 0:n], rope[:, 0, 0:n], ALU.mult).then_inc(cos_made, 1)
                        dve.wait_ge(cos_made, 2 * v + (2 * QK * i + s + 1))
                        dve.sem_inc(drained[s], 1)
                        dve.wait_ge(sin_made, 2 * v + (2 * QK * i + s + 1))
                        nc.vector.tensor_tensor(turn[:, s, 0:n], turn[:, s, 0:n], swap[:, s, 0:n], ALU.add).then_inc(turned, 1)
                        dve.wait_ge(turned, 2 * v + (2 * QK * i + s + 3))
                        nc.vector.tensor_copy(split_hi[:, s, 0:n], turn[:, s, 0:n]).then_inc(hi_made, 1)
                for v in range(QK, QKV):
                    for s in range(2):
                        ring.rest(dve, nc, ALL * i + v + 1, s)
                        dve.wait_ge(v_hi, 2 * (QKV - QK) * i + 2 * (v - QK) + s + 1)
                        nc.vector.tensor_tensor(split_lo[:, s, 0:n], psu[:, s, 0:n], split_hi[:, s, 0:n], ALU.subtract).then_inc(v_lo, 1)
                        dve.wait_ge(v_lo, 2 * (QKV - QK) * i + 2 * (v - QK) + s + 1)
                        dve.sem_inc(drained[s], 1)
                if i + 1 < C:
                    for j in range(ALL - QKV):
                        for s in range(2):
                            ring.rest(dve, nc, ALL * i + QKV + 1 + j, s)
                            for step in VECTOR_AT.get(2 * (QKV - QK + j) + s, ()):
                                pres[i + 1].vector_step(dve, nc, chain, scales[i + 1], shifts[i + 1], step)
                else:
                    with dve.Fori(0, ALL - QKV - 1) as j:
                        for s in range(2):
                            ring.rest(dve, nc, j + (ALL * i + QKV + 1), s)

        @block.tensor
        def _(pe):
            ring.start_tensor(pe)
            pres[0].total(pe, nc)
            for i, (c0, n) in enumerate(CHUNKS):
                hi, lo = h_hi[:, i % 2, :, 0:n], h_lo[:, i % 2, :, 0:n]
                pe.wait_ge(pres[i].ready, KD)

                def unit(v, s):
                    ring.ready(pe, v + ALL * i, s)
                    pe.wait_ge(drained[s], v + (ALL * i + 1))

                def columns(v, s):
                    unit(v, s)
                    product3(nc, psu[:, s, 0:n], ring.hi[:, s], ring.lo[:, s], hi, lo, KD).then_inc(ring.used, 1)

                with pe.Fori(0, QK) as v:
                    for s in range(2):
                        columns(v, s)
                for v in range(QK, QKV):
                    for s in range(2):
                        unit(v, s)
                        for t in range(n // P):
                            tok = slice(t * P, (t + 1) * P)
                            last = product3(nc, psu[:, s, tok], hi[:, :, tok], lo[:, :, tok], ring.hi[:, s], ring.lo[:, s], KD)
                        last.then_inc(ring.used, 1)
                for start, end in ((QKV, QKV + TOTAL_AT), (QKV + TOTAL_AT, ALL)):
                    with pe.Fori(start, end) as v:
                        for s in range(2):
                            columns(v, s)
                    if end < ALL and i + 1 < C:
                        pres[i + 1].total(pe, nc)
                pe.wait_ge(dt_split, 1)
                if i:
                    pe.wait_ge(dt_out, i)
                product3(nc, psd[:, 0:n], wdt_hi, wdt_lo, hi, lo, KD).then_inc(dt_done, 1)


def out_proj_stage(nc, g, m, layer, chunks):
    N = CHUNKS[-1][1]
    C = len(chunks)
    HS = KD - HEADS
    w_view = g.w_out[layer].rearrange("(k p) n -> p k n", p=P)
    sizes = [CHUNKS[ci] for ci in chunks]
    with Stage(nc, f"out{layer}") as st:
        psn = st.ps("psn", [P, 512])
        psu = st.ps("psu", [P, 2, 512])
        ring = WeightRing(st)
        hi = st.sb("hi", [P, 2, KD, N], F32R)
        lo = st.sb("lo", [P, 2, KD, N], F32R)
        f = st.sb("f", [P, 2, KD, N])
        x = st.sb("x", [P, KD, N])
        sq = st.sb("sq", [P, 2, N])
        res_tmp = st.sb("res_tmp", [P, 2, N])
        scan_bufs, post_bufs = st.sb("scan_bufs", [P, 3, N]), st.sb("post_bufs", [P, 4, N])
        norms = [RowNorm(st, f"scan{i}", n, SW, psn, g.ones, scan_bufs) for i, (_, n) in enumerate(sizes)]
        ress = [Residual(st, g, f"res{i}", n, psn, f[:, i % 2], x, res_tmp, post_bufs, 3 * (i % 2)) for i, (_, n) in enumerate(sizes)]
        gates = [g.post[:, 0, 0 if ci == 0 else 1] for ci in chunks]
        squared, added, scaled, rounded, ready = (st.sem(x) for x in ("squared", "added", "scaled", "rounded", "ready"))
        chain_v, chain_a = st.sem("chain_v"), st.sem("chain_a")
        block = st.block()

        def scan_tile(i, k):
            return m.ssd[:, k, sizes[i][0]:sizes[i][0] + sizes[i][1]]

        def operand(i, k):
            return m.att[:, k, sizes[i][0]:sizes[i][0] + sizes[i][1]] if k < HEADS else scan_tile(i, k - HEADS)

        @block.sync
        def _(sp):
            for i in range(C):
                with sp.Fori(0, KD // 2) as v:
                    for s in range(2):
                        ring.load(sp, v + KD // 2 * i, s, w_view[:, :, bass.ds((2 * v + s) * P, P)])

        @block.gpsimd
        def _(pool):
            def low(i, tiles):
                for k in tiles:
                    pool.wait_ge(rounded, KD * i + k + 1)
                    nc.gpsimd.tensor_tensor(lo[:, i % 2, k, 0:sizes[i][1]], operand(i, k), hi[:, i % 2, k, 0:sizes[i][1]],
                                            ALU.subtract).then_inc(ready, 1)
            ress[0].load(pool, sizes[0][0])
            low(0, range(KD))
            for i in range(C):
                ress[i].start_sum(pool, nc)
                for n in range(KD):
                    ress[i].add_square(pool, nc, n)
                    if i and n in (2, 3, 4):
                        ress[i - 1].add(pool, nc, 3 * (n - 2), min(KD, 3 * (n - 1)))
                    if i and n == 4:
                        ress[i - 1].store(pool, sizes[i - 1][0])
                        ress[i].load(pool, sizes[i][0])
                    if i + 1 < C:
                        low(i + 1, {5: (0, 1), 6: (2, 3), 7: (4, 5, 6, 7)}.get(n, ()))
            ress[-1].add(pool, nc)
            ress[-1].store(pool, sizes[-1][0])

        @block.scalar
        def _(act):
            chain = Chain(act, chain_a)

            def squares(i):
                for k in range(HS):
                    if k == 3:
                        act.wait_ge(added, (HS - 1) * i + 1)
                    nc.scalar.activation(sq[:, k % 2, 0:sizes[i][1]] if k else norms[i].ss, scan_tile(i, k), ACT.Square).then_inc(squared, 1)

            def high(i, tiles):
                for k in tiles:
                    if k >= HEADS:
                        act.wait_ge(scaled, HS * i + k - HEADS + 1)
                    nc.scalar.activation(hi[:, i % 2, k, 0:sizes[i][1]], operand(i, k), ACT.Copy).then_inc(rounded, 1)
            squares(0)
            high(0, range(HEADS))
            for s in range(2):
                ring.round(act, nc, 0, s)
            norms[0].root(act, nc, chain)
            high(0, range(HEADS, KD))
            for i in range(C):
                for n in range(KD):
                    if i + 1 < C or n < KD - 2:
                        ring.round(act, nc, KD // 2 * i + n // 2 + 1, n % 2)
                    ress[i].square_tile(act, nc, n // 2, n % 2)
                    if i and n == 0:
                        ress[i - 1].norm.root(act, nc, chain)
                    if i + 1 < C:
                        if n == 2:
                            squares(i + 1)
                        if n == 4:
                            norms[i + 1].root(act, nc, chain)
                        high(i + 1, {2: (0, 1), 3: (2, 3), 6: (4, 5), 7: (6, 7)}.get(n, ()))
            ress[-1].norm.root(act, nc, chain)

        @block.vector
        def _(dve):
            chain = Chain(dve, chain_v)
            ring.start_vector(dve)

            def add_squares(i):
                for k in range(1, HS):
                    dve.wait_ge(squared, HS * i + k + 1)
                    if k > 1:
                        dve.wait_ge(added, (HS - 1) * i + k - 1)
                    nc.vector.tensor_tensor(norms[i].ss, norms[i].ss, sq[:, k % 2, 0:sizes[i][1]], ALU.add).then_inc(added, 1)

            def scale(i, tiles):
                for k in tiles:
                    nc.vector.scalar_tensor_tensor(scan_tile(i, k), scan_tile(i, k), g.cols_b[:, ROW_SG + k:ROW_SG + k + 1],
                                                   norms[i].r, ALU.mult, ALU.mult).then_inc(scaled, 1)
            add_squares(0)
            norms[0].mean_eps(dve, nc)
            norms[0].refine(dve, nc, chain)
            scale(0, range(HS))
            for s in range(2):
                ring.rest(dve, nc, 0, s)
            for i in range(C):
                ress[i].start_vector(dve)
                for n in range(KD):
                    if i + 1 < C or n < KD - 2:
                        ring.rest(dve, nc, KD // 2 * i + n // 2 + 1, n % 2)
                    dve.wait_ge(ring.used, KD * i + n + 3)
                    ress[i].copy_tile(dve, nc, n // 2, n % 2, psu[:, n % 2, 0:sizes[i][1]])
                    if i and n == 0:
                        ress[i - 1].norm.mean_eps(dve, nc)
                    if i and n == 1:
                        ress[i - 1].norm.refine(dve, nc, chain)
                    if i and n in (2, 3, 4):
                        ress[i - 1].scale(nc, gates[i - 1], 3 * (n - 2), min(KD, 3 * (n - 1)))
                    if i + 1 < C and n == 2:
                        add_squares(i + 1)
                    if i + 1 < C:
                        if n == 4:
                            norms[i + 1].mean_eps(dve, nc)
                        if n == 5:
                            norms[i + 1].refine(dve, nc, chain)
                        scale(i + 1, {5: (0, 1), 6: (2, 3)}.get(n, ()))
            ress[-1].vector(dve, nc, chain, gates[-1])

        @block.tensor
        def _(pe):
            ring.start_tensor(pe)

            def total(i):
                pe.wait_ge(added, (HS - 1) * (i + 1))
                norms[i].add_partitions(nc)
            total(0)
            for i in range(C):
                n = sizes[i][1]

                def unit(v, s):
                    ring.ready(pe, v + KD // 2 * i, s)
                    ress[i].bank_free(pe, v, s)
                    product3(nc, psu[:, s, 0:n], ring.hi[:, s], ring.lo[:, s], hi[:, i % 2, :, 0:n], lo[:, i % 2, :, 0:n], KD).then_inc(ring.used, 1)
                pe.wait_ge(ready, KD * (i + 1))
                unit(0, 0)
                if i:
                    ress[i - 1].tensor(pe, nc)
                unit(0, 1)
                for s in range(2):
                    unit(1, s)
                if i + 1 < C:
                    total(i + 1)
                with pe.Fori(2, KD // 2) as v:
                    for s in range(2):
                        unit(v, s)
            ress[-1].tensor(pe, nc)


def ffn_stage(nc, g, layer, chunks):
    N = CHUNKS[-1][1]
    C = len(chunks)
    w1 = g.w_ffn_in[layer].rearrange("(k p) n -> p k n", p=P)
    w2 = g.w_ffn_out[layer].rearrange("(k p) n -> p k n", p=P)
    KS = [(0, 8), (8, 8), (16, 6)]
    DOWN = [(i // 3, KS[i % 3]) for i in range(6)]
    PASSES = KD // 2
    PER = KF + 3 * PASSES
    SCALAR_AT = {2: 0, 3: 1, 4: 2, 5: 3, 8: 4, **{10 + k: 5 + k for k in range(KD)}}
    VECTOR_AT = {7: 0, 9: 1, **{10 + k: 2 + k for k in range(KD + 1)}}
    with Stage(nc, f"ffn{layer}") as st:
        psn = st.ps("psn", [P, 512])
        psu = st.ps("psu", [P, 2, 2, 512])
        psf = st.ps("psf", [P, 2, 512])
        x = st.sb("x", [P, KD, N])
        f = st.sb("f", [P, KD, N])
        h_hi = st.sb("h_hi", [P, KD, N], F32R)
        h_lo = st.sb("h_lo", [P, KD, N], F32R)
        sq = st.sb("sq", [P, 2, N])
        pre_bufs, post_bufs = st.sb("pre_bufs", [P, 3, N]), st.sb("post_bufs", [P, 3, N])
        ring = WeightRing(st)
        a_hi = st.sb("a_hi", [P, KF, N], F32R)
        a_lo = st.sb("a_lo", [P, KF, N], F32R)
        sig = st.sb("sig", [P, 2, N])
        act_t = st.sb("act_t", [P, 2, N])
        sizes = [CHUNKS[ci] for ci in chunks]
        pres = [Prenorm(st, g, f"pre{i}", n, psn, x, sq, pre_bufs, h_hi, h_lo) for i, (_, n) in enumerate(sizes)]
        ress = [Residual(st, g, f"post{i}", n, psn, f, x, sq, post_bufs) for i, (_, n) in enumerate(sizes)]
        streams = [0 if ci == 0 else 1 for ci in chunks]
        shifts = [g.mod[:, s, SH2 * KD:(SH2 + 1) * KD] for s in streams]
        scales = [g.pre[:, 1, s] for s in streams]
        gates = [g.post[:, 1, s] for s in streams]
        chain_v, chain_a = st.sem("chain_v"), st.sem("chain_a")
        gated, multiplied, a_rounded, a_ready = st.sem("gated"), st.sem("multiplied"), st.sem("a_rounded"), st.sem("a_ready")
        block = st.block()

        @block.sync
        def _(sp):
            for i in range(C):
                with sp.Fori(0, KF) as v:
                    for s in range(2):
                        ring.load(sp, v + PER * i, s, w1[:, :, bass.ds(v * P + s * DFF, P)])
                with sp.Fori(0, PASSES) as o:
                    for u, (half, (k0, nk)) in enumerate(DOWN):
                        ring.load(sp, 3 * o + (PER * i + KF + u // 2), u % 2, w2[:, k0:k0 + nk, bass.ds((2 * o + half) * P, P)], nk)

        @block.gpsimd
        def _(pool):
            pres[0].load(pool, sizes[0][0])
            for i in range(C):
                pool.wait_ge(pres[i].ready, KD)
                if i:
                    ress[i - 1].load(pool, sizes[i - 1][0])
                    ress[i - 1].add(pool, nc)
                    ress[i - 1].store(pool, sizes[i - 1][0])
                if i + 1 < C:
                    pres[i + 1].load(pool, sizes[i + 1][0])
                    for k in range(1, KD):
                        pres[i + 1].add(pool, nc.gpsimd, k)
                    pool.wait_ge(pres[i + 1].added, KD - 1)
                ress[i].sum_squares(pool, nc)
            ress[-1].load(pool, sizes[-1][0])
            ress[-1].add(pool, nc)
            ress[-1].store(pool, sizes[-1][0])

        @block.scalar
        def _(act):
            chain = Chain(act, chain_a)
            for step in range(4):
                pres[0].scalar_step(act, nc, chain, shifts[0], step)
            for s in range(2):
                ring.round(act, nc, 0, s)
            for step in range(4, Prenorm.SCALAR_STEPS):
                pres[0].scalar_step(act, nc, chain, shifts[0], step)
            for i in range(C):
                n, base, hidden0 = sizes[i][1], PER * i, KF * i

                def gate(t, e):
                    act.wait_ge(ring.used, 2 * t + (2 * base + 3))
                    act.wait_ge(multiplied, t + (hidden0 + 1))
                    nc.scalar.activation(sig[:, e, 0:n], psu[:, e, 0, 0:n], ACT.Silu).then_inc(gated, 1)

                def hidden_hi(t, e):
                    act.wait_ge(multiplied, t + (hidden0 + 3))
                    nc.scalar.activation(a_hi[:, bass.ds(t, 1), 0:n].rearrange("p o t -> p (o t)"), act_t[:, e, 0:n],
                                         ACT.Copy).then_inc(a_rounded, 1)

                def gate_up(t, e):
                    gate(t, e)
                    ring.round(act, nc, t + (base + 1), 0)
                    hidden_hi(t, e)
                    ring.round(act, nc, t + (base + 1), 1)
                for e in range(2):
                    gate_up(e, e)
                    if i and e == 0:
                        ress[i - 1].norm.root(act, nc, chain)
                with act.Fori(1, KF // 2) as w:
                    for e in range(2):
                        gate_up(2 * w + e, e)

                def round_(o, u):
                    ring.round(act, nc, 3 * o + (base + KF + u // 2), u % 2, DOWN[u % 6][1][1])
                    if i + 1 < C and 6 * o + u in SCALAR_AT:
                        pres[i + 1].scalar_step(act, nc, chain, shifts[i + 1], SCALAR_AT[6 * o + u])

                def down(o, more=True):
                    for u in (2, 3, 4, 5):
                        round_(o, u)
                    ress[i].square_tile(act, nc, o, 0)
                    if more:
                        round_(o, 6)
                        round_(o, 7)
                    ress[i].square_tile(act, nc, o, 1)
                if i + 1 < C:
                    for o in range(PASSES):
                        down(o)
                else:
                    with act.Fori(0, PASSES - 1) as o:
                        down(o)
                    down(PASSES - 1, False)
            ress[-1].norm.root(act, nc, chain)

        @block.vector
        def _(dve):
            chain = Chain(dve, chain_v)
            ring.start_vector(dve)
            dve.sem_inc(multiplied, 2)
            for k in range(1, KD):
                pres[0].add(dve, nc.vector, k)
            pres[0].vector_step(dve, nc, chain, scales[0], shifts[0], 0)
            for s in range(2):
                ring.rest(dve, nc, 0, s)
            for step in range(1, Prenorm.VECTOR_STEPS):
                pres[0].vector_step(dve, nc, chain, scales[0], shifts[0], step)
            for i in range(C):
                n, base, hidden0 = sizes[i][1], PER * i, KF * i

                def hidden(t, e):
                    dve.wait_ge(gated, t + (hidden0 + 1))
                    dve.wait_ge(ring.used, 2 * t + (2 * base + 4))
                    nc.vector.tensor_tensor(act_t[:, e, 0:n], sig[:, e, 0:n], psu[:, e, 1, 0:n], ALU.mult).then_inc(multiplied, 1)

                def hidden_lo(t, e):
                    dve.wait_ge(a_rounded, t + (hidden0 + 1))
                    nc.vector.tensor_tensor(a_lo[:, bass.ds(t, 1), 0:n].rearrange("p o t -> p (o t)"), act_t[:, e, 0:n],
                                            a_hi[:, bass.ds(t, 1), 0:n].rearrange("p o t -> p (o t)"), ALU.subtract).then_inc(a_ready, 1)
                    dve.wait_ge(a_ready, t + (hidden0 + 1))

                def gate_up(t, e):
                    ring.rest(dve, nc, t + (base + 1), 0)
                    hidden(t, e)
                    hidden_lo(t, e)
                    ring.rest(dve, nc, t + (base + 1), 1)
                gate_up(0, 0)
                if i:
                    ress[i - 1].norm.mean_eps(dve, nc)
                gate_up(1, 1)
                if i:
                    ress[i - 1].norm.refine(dve, nc, chain)
                    ress[i - 1].scale(nc, gates[i - 1])
                with dve.Fori(1, KF // 2) as w:
                    for e in range(2):
                        gate_up(2 * w + e, e)
                if i:
                    dve.wait_ge(ress[i - 1].summed, KD)
                ress[i].start_vector(dve)

                def copy_out(o, half):
                    dve.wait_ge(ring.used, 6 * o + (2 * (base + KF) + 3 * half + 5))
                    ress[i].copy_tile(dve, nc, o, half, psf[:, half, 0:n])

                def rest(o, u):
                    ring.rest(dve, nc, 3 * o + (base + KF + u // 2), u % 2, DOWN[u % 6][1][1])
                    if i + 1 < C and 6 * o + u in VECTOR_AT:
                        pres[i + 1].vector_step(dve, nc, chain, scales[i + 1], shifts[i + 1], VECTOR_AT[6 * o + u])

                def down(o, more=True):
                    for u in (2, 3, 4):
                        rest(o, u)
                    copy_out(o, 0)
                    rest(o, 5)
                    if more:
                        rest(o, 6)
                        rest(o, 7)
                    copy_out(o, 1)
                if i + 1 < C:
                    for o in range(PASSES):
                        down(o)
                else:
                    with dve.Fori(0, PASSES - 1) as o:
                        down(o)
                    down(PASSES - 1, False)
            ress[-1].vector(dve, nc, chain, gates[-1])

        @block.tensor
        def _(pe):
            ring.start_tensor(pe)
            pres[0].total(pe, nc)
            for i in range(C):
                n, base, hidden0 = sizes[i][1], PER * i, KF * i
                hi, lo = h_hi[:, :, 0:n], h_lo[:, :, 0:n]

                def gate_up(t, e, h_ready=None):
                    pe.wait_ge(multiplied, t + (hidden0 + 1))
                    for s in range(2):
                        ring.ready(pe, t + base, s)
                        product3(nc, psu[:, e, s, 0:n], ring.hi[:, s], ring.lo[:, s], hi, lo, KD,
                                 each=lambda k: pe.wait_ge(h_ready, k + 1) if h_ready and s == 0 else None).then_inc(ring.used, 1)

                def down(o):
                    for u, (half, (k0, nk)) in enumerate(DOWN):
                        pe.wait_ge(ring.split, 6 * o + (2 * (base + KF) + u + 3))
                        if u % 3 == 0:
                            ress[i].bank_free(pe, o, half)
                        last = product3(nc, psf[:, half, 0:n], ring.hi[:, u % 2], ring.lo[:, u % 2],
                                        a_hi[:, k0:k0 + nk, 0:n], a_lo[:, k0:k0 + nk, 0:n], nk, u % 3 == 0, u % 3 == 2)
                        last.then_inc(ring.used, 1)
                gate_up(0, 0, pres[i].ready)
                if i:
                    ress[i - 1].tensor(pe, nc)
                gate_up(1, 1)
                with pe.Fori(1, KF // 2) as w:
                    for e in range(2):
                        gate_up(2 * w + e, e)
                pe.wait_ge(a_ready, hidden0 + KF)
                if i + 1 < C:
                    down(0)
                    pres[i + 1].total(pe, nc)
                    with pe.Fori(1, PASSES) as o:
                        down(o)
                else:
                    with pe.Fori(0, PASSES) as o:
                        down(o)
            ress[-1].tensor(pe, nc)


def attention_stage(nc, g, m, layer):
    tiles = [(t, CTX) for t in range(CTX // P)] if layer == 0 else []
    tiles += [(t, T) for t in range(CTX // P, NT)]
    n_tiles = len(tiles)
    groups = [(i, k, min(4, keys // P - k)) for i, (_, keys) in enumerate(tiles) for k in range(0, keys // P, 4)]
    of_tile = [[j for j, x in enumerate(groups) if x[0] == i] for i in range(n_tiles)]
    n_groups = len(groups)
    ES, GS = 3, 6
    with Stage(nc, f"att{layer}") as st:
        q = st.sb("q", [P, 2, T], F32R)
        k_hi = st.sb("k_hi", [P, 2, T], F32R)
        k_lo = st.sb("k_lo", [P, 2, T], F32R)
        v_hi = st.sb("v_hi", [P, NT, P], F32R)
        v_lo = st.sb("v_lo", [P, NT, P], F32R)
        e = st.sb("e", [P, ES, 2, T])
        pt = st.sb("pt", [P, GS, 4, P])
        pt_hi = st.sb("pt_hi", [P, GS, 4, P], F32R)
        pt_lo = st.sb("pt_lo", [P, GS, 4, P], F32R)
        diag = st.sb("diag", [P, ES, P])
        top = st.sb("top", [P, ES, 2])
        shift = st.sb("shift", [P, ES, 2])
        total = st.sb("total", [P, ES, 2])
        inv = st.sb("inv", [P, ES, 2])
        coef = st.sb("coef", [P, ES])
        ps_s = st.ps("ps_s", [P, 2, 3, 512])
        ps_t = st.ps("ps_t", [P, 4, P])
        ps_o = st.ps("ps_o", [P, 4, P])
        q_in, k_in, v_in = st.sem("q_in"), st.sem("k_in"), st.sem("v_in")
        scored, topped, shifted, exped, mixed, turned, copied, hi_made, lo_made, summed, out = (st.sem(x) for x in (
            "scored", "topped", "shifted", "exped", "mixed", "turned", "copied", "hi_made", "lo_made", "summed", "out"))
        chain_v = st.sem("chain_v")
        block = st.block()

        @block.sync
        def _(sp):
            def load_qk(h):
                for a in range(2):
                    rows = slice(64 * a, 64 * a + 64)
                    for part in range(2):
                        half = slice(64 * part, 64 * part + 64)
                        sp.dma_start(q[half, a].bitcast(F32), g.qk_d[part, bass.ds(h, 1), rows].rearrange("o p t -> p (o t)")).then_inc(q_in, 16)
                        for dst, which in ((k_hi, 0), (k_lo, 1)):
                            sp.dma_start(dst[half, a].bitcast(F32), g.qk_d[which, bass.ds(h + HEADS, 1), rows].rearrange("o p t -> p (o t)")).then_inc(k_in, 16)

            def load_v(h):
                for dst, part in ((v_hi, 0), (v_lo, 1)):
                    sp.dma_start(dst[:].bitcast(F32), g.v_d[part, bass.ds(h, 1)].rearrange("o (t p) e -> p (o t) e", p=P)).then_inc(v_in, 16)
            load_qk(0)
            load_v(0)
            with sp.Fori(1, HEADS) as h:
                sp.wait_ge(scored, 2 * n_tiles * h)
                load_qk(h)
                sp.wait_ge(summed, n_groups * h)
                load_v(h)

        @block.tensor
        def _(pe):
            with pe.Fori(0, HEADS) as h:
                pe.wait_ge(q_in, 64 * h + 64)
                pe.wait_ge(k_in, 128 * h + 128)

                def scores(i, a):
                    if i >= n_tiles:
                        return
                    t, keys = tiles[i]
                    pe.wait_ge(exped, 2 * n_tiles * h + (2 * i + a + 1))
                    for c in range(0, keys, 512):
                        w = min(512, keys - c)
                        nc.tensor.matmul(ps_s[:, a, c // 512, 0:w], q[:, a, t * P:(t + 1) * P], k_hi[:, a, c:c + w], start=True, stop=False)
                        last = nc.tensor.matmul(ps_s[:, a, c // 512, 0:w], q[:, a, t * P:(t + 1) * P], k_lo[:, a, c:c + w], start=False, stop=True)
                    last.then_inc(scored, 1)

                def transposes(j):
                    i, k0, nk = groups[j]
                    pe.wait_ge(mixed, n_tiles * h + (i + 1))
                    pe.wait_ge(copied, n_groups * h + (j + 1))
                    for x in range(nk):
                        last = nc.tensor.matmul(ps_t[:, x], e[:, i % ES, 1, (k0 + x) * P:(k0 + x + 1) * P], diag[:, i % ES], start=True, stop=True)
                    last.then_inc(turned, 1)

                def products(j):
                    i, k0, nk = groups[j]
                    pe.wait_ge(lo_made, n_groups * h + (j + 1))
                    if k0 == 0:
                        pe.wait_ge(out, n_tiles * h + (i + 1))
                    last = product3(nc, ps_o[:, 0], v_hi[:, k0:k0 + nk], v_lo[:, k0:k0 + nk], pt_hi[:, j % GS], pt_lo[:, j % GS], nk,
                                    k0 == 0, (k0 + nk) * P == tiles[i][1])
                    last.then_inc(summed, 1)

                scores(0, 0)
                scores(0, 1)
                pe.wait_ge(v_in, 32 * h + 32)
                for i in range(n_tiles):
                    scores(i + 1, 0)
                    scores(i + 1, 1)
                    late = list(of_tile[i - 1]) if i else []
                    for j in of_tile[i]:
                        if late:
                            products(late.pop(0))
                        transposes(j)
                    for j in late:
                        products(j)
                for j in of_tile[-1]:
                    products(j)

        @block.vector
        def _(dve):
            chain = Chain(dve, chain_v)
            with dve.Fori(0, HEADS) as h, chain.over(h, HEADS, 2 * n_tiles):
                def maximum(i, a):
                    if i >= n_tiles:
                        return
                    dve.wait_ge(scored, 2 * n_tiles * h + (2 * i + a + 1))
                    nc.vector.tensor_reduce(top[:, i % ES, a:a + 1], ps_s[:, a].rearrange("p c w -> p (c w)")[:, 0:tiles[i][1]],
                                            AX.X, ALU.max).then_inc(topped, 1)
                    dve.wait_ge(topped, 2 * n_tiles * h + (2 * i + a + 1))
                    nc.vector.tensor_scalar(shift[:, i % ES, a:a + 1], top[:, i % ES, a:a + 1], -0.125, None,
                                            ALU.mult).then_inc(shifted, 1)

                def mix(i):
                    keys, x = tiles[i][1], i % ES
                    dve.wait_ge(exped, 2 * n_tiles * h + (2 * i + 4))
                    chain(nc.vector.reciprocal(inv[:, x], total[:, x]))
                    chain(nc.vector.scalar_tensor_tensor(coef[:, x:x + 1], inv[:, x, 1:2], g.neg_lam[:], total[:, x, 0:1], ALU.mult, ALU.mult))
                    nc.vector.tensor_scalar(diag[:, x], g.ident[:], inv[:, x, 0:1], None, ALU.mult)
                    nc.vector.scalar_tensor_tensor(e[:, x, 1, 0:keys], e[:, x, 1, 0:keys], coef[:, x:x + 1],
                                                   e[:, x, 0, 0:keys], ALU.mult, ALU.add).then_inc(mixed, 1)

                def high(j):
                    dve.wait_ge(copied, n_groups * h + (j + 2))
                    nk = groups[j][2]
                    nc.vector.tensor_copy(pt_hi[:, j % GS, 0:nk], pt[:, j % GS, 0:nk]).then_inc(hi_made, 1)
                maximum(0, 0)
                maximum(0, 1)
                for i in range(n_tiles):
                    mix(i)
                    for j in of_tile[i - 1][2:] if i else ():
                        high(j)
                    maximum(i + 1, 0)
                    maximum(i + 1, 1)
                    for j in of_tile[i][:2]:
                        high(j)
                for j in of_tile[-1][2:]:
                    high(j)

        @block.gpsimd
        def _(pool):
            with pool.Fori(0, HEADS) as h:
                for j, (_, _, nk) in enumerate(groups):
                    pool.wait_ge(hi_made, n_groups * h + (j + 1))
                    nc.gpsimd.tensor_tensor(pt_lo[:, j % GS, 0:nk], pt[:, j % GS, 0:nk], pt_hi[:, j % GS, 0:nk], ALU.subtract).then_inc(lo_made, 1)

        @block.scalar
        def _(act):
            act.sem_inc(exped, 2)
            act.sem_inc(copied, 1)
            act.sem_inc(out, 1)
            with act.Fori(0, HEADS) as h:
                def exps(i, a):
                    if i >= n_tiles:
                        return
                    keys = tiles[i][1]
                    if i >= ES:
                        act.wait_ge(turned, n_groups * h + (of_tile[i - ES][-1] + 1))
                    act.wait_ge(shifted, 2 * n_tiles * h + (2 * i + a + 1))
                    nc.scalar.activation(e[:, i % ES, a, 0:keys], ps_s[:, a].rearrange("p c w -> p (c w)")[:, 0:keys], ACT.Exp,
                                         bias=shift[:, i % ES, a:a + 1], scale=0.125,
                                         accum_out=total[:, i % ES, a:a + 1]).then_inc(exped, 1)

                def copy_group(j):
                    nk = groups[j][2]
                    act.wait_ge(turned, n_groups * h + (j + 1))
                    if j >= GS:
                        act.wait_ge(summed, n_groups * h + (j - GS + 1))
                    nc.scalar.activation(pt[:, j % GS, 0:nk], ps_t[:, 0:nk], ACT.Copy).then_inc(copied, 1)

                def copy_out(i):
                    act.wait_ge(summed, n_groups * h + (of_tile[i][-1] + 1))
                    t = tiles[i][0]
                    nc.scalar.activation(m.att[:, bass.ds(h, 1), t * P:(t + 1) * P].rearrange("p o t -> p (o t)"), ps_o[:, 0],
                                         ACT.Copy).then_inc(out, 1)
                exps(0, 0)
                exps(0, 1)
                for i in range(n_tiles):
                    js = of_tile[i]
                    copy_group(js[0])
                    exps(i + 1, 0)
                    for j in js[1:2]:
                        copy_group(j)
                    exps(i + 1, 1)
                    for j in js[2:]:
                        copy_group(j)
                    if i:
                        copy_out(i - 1)
                copy_out(n_tiles - 1)


def scan_prep_stage(nc, g, layer, m):
    PAD = T + 6
    CONV_T = 8
    with Stage(nc, f"prep{layer}") as st:
        pad = st.sb("pad", [P, 2, PAD])
        taps = st.sb("taps", [P, 2, 6])
        acc = st.sb("acc", [P, 2, PAD - 4])
        cv = st.sb("cv", [P, 2, T])
        tok = st.sb("tok", [P, 2, NT, P])
        ps = st.ps("ps", [P, 2, 3, 4, P])
        psd = st.ps("psd", [P, 512])
        raw, s1, s2, s3, dta = (st.sb(x, [P, NT, 2, SH]) for x in ("raw", "s1", "s2", "s3", "dta"))
        cum = st.sb("cum", [2 * SH, NT, P])
        ps_cum = st.ps("ps_cum", [2 * SH, 4, P])
        w_tok = st.sb("w_tok", [P, NT, 2, SH])
        pad_in = [st.sem(f"pad_in{s}") for s in range(2)]
        zeroed, tapped, first, summed, sig, done, turned, tok_done = (st.sem(x) for x in (
            "zeroed", "tapped", "first", "summed", "sig", "done", "turned", "tok_done"))
        cv_out = [st.sem(f"cv_out{s}") for s in range(2)]
        tok_out = [st.sem(f"tok_out{s}") for s in range(2)]
        dt_turned, absolute, a_exp, dta_made, cum_made, cum_copied, tot, tot_copied, row_turned, row_copied, cum_out = (st.sem(x) for x in (
            "dt_turned", "absolute", "a_exp", "dta_made", "cum_made", "cum_copied", "tot", "tot_copied", "row_turned", "row_copied", "cum_out"))
        chain_v, chain_a = st.sem("chain_v"), st.sem("chain_a")
        block = st.block()
        PAIRS = CONV_T // 2
        TURNED = 3

        @block.sync
        def _(sp):
            sp.wait_ge(zeroed, 3)

            def load(v, s):
                sp.wait_ge(summed, 2 * v + (s + 1))
                src = g.zx_d[bass.ds(2 * v + (s + 4), 1)].rearrange("o p t -> p (o t)")
                sp.dma_start(pad[:, s, 2:2 + CTX], src[:, 0:CTX]).then_inc(pad_in[s], 16)
                sp.dma_start(pad[:, s, 4 + CTX:4 + T], src[:, CTX:T]).then_inc(pad_in[s], 16)
            def store(v, s):
                sp.wait_ge(done, 2 * v + (s + 1))
                sp.dma_start(g.cv_d[bass.ds(2 * v + s, 1)].rearrange("o p t -> p (o t)"), cv[:, s]).then_inc(cv_out[s], 16)
                sp.wait_ge(tok_done, 6 * v + (3 * s + 7))
                sp.dma_start(g.tok_d.rearrange("c p f -> p c f")[:, :, bass.ds((2 * v + s) * P, P)], tok[:, s]).then_inc(tok_out[s], 16)
            for v in range(2):
                for s in range(2):
                    load(v, s)
            with sp.Fori(0, TURNED - 1) as v:
                for s in range(2):
                    load(v + 2, s)
                    store(v, s)
            for s in range(2):
                store(TURNED - 1, s)
            for s in range(2):
                sp.wait_ge(done, 2 * TURNED + s + 1)
                sp.dma_start(g.cv_d[2 * TURNED + s], cv[:, s]).then_inc(cv_out[s], 16)
            sp.wait_ge(row_copied, 3)
            sp.dma_start(g.cum_d.rearrange("h (c t) -> h c t", t=P), cum[:]).then_inc(cum_out, 16)
            sp.wait_ge(cum_out, 16)
            for s in range(2):
                sp.wait_ge(cv_out[s], 16 * PAIRS + 16)
                sp.wait_ge(tok_out[s], 16 * TURNED + 16)

        @block.gpsimd
        def _(pool):
            for a, b in ((0, 2), (2 + CTX, 4 + CTX), (4 + T, 6 + T)):
                nc.gpsimd.memset(pad[:, :, a:b], 0.0).then_inc(zeroed, 1)

        @block.scalar
        def _(act):
            chain = Chain(act, chain_a)
            for s in range(2):
                act.sem_inc(cv_out[s], 16)
            act.wait_ge(absolute, 1)
            nc.scalar.activation(s1[:], s1[:], ACT.Exp, scale=-1.0).then_inc(a_exp, 1)
            def tap0(v, s):
                act.wait_ge(pad_in[s], 32 * v + 32)
                act.wait_ge(tapped, 2 * v + (s + 1))
                nc.scalar.activation(acc[:, s], pad[:, s, 0:PAD - 4], ACT.Identity, bias=taps[:, s, 5:6],
                                     scale=taps[:, s, 0:1]).then_inc(first, 1)

            def silu(v, s):
                act.wait_ge(summed, 2 * v + (s + 3))
                act.wait_ge(cv_out[s], 16 * v + 16)
                act.wait_ge(turned, 6 * v + (3 * s + 1))
                nc.scalar.activation(cv[:, s, 0:CTX], acc[:, s, 0:CTX], ACT.Silu)
                nc.scalar.activation(cv[:, s, CTX:T], acc[:, s, CTX + 2:T + 2], ACT.Silu).then_inc(done, 1)
            for s in range(2):
                tap0(0, s)
            with act.Fori(0, PAIRS - 1) as v:
                for s in range(2):
                    silu(v, s)
                    act.wait_ge(done, 2 * v + (s + 1))
                    tap0(v + 1, s)
            for s in range(2):
                silu(PAIRS - 1, s)
            act.wait_ge(tot_copied, 1)
            chain(nc.scalar.activation(w_tok[:], w_tok[:], ACT.Exp))
            nc.scalar.activation(m.etot[:], m.etot[:], ACT.Exp).then_inc(a_exp, 1)

        @block.vector
        def _(dve):
            chain = Chain(dve, chain_v)
            dve.sem_inc(summed, 2)
            dve.sem_inc(tok_done, 4)
            for s in range(2):
                dve.sem_inc(tok_out[s], 16)
            dve.wait_ge(dt_turned, 1)
            heads = psd[:, 0:NT * DTP].rearrange("p (c h) -> p c h", h=DTP)
            for d in range(2):
                bias = g.dt_bias[:, d].unsqueeze(1).broadcast_to([P, NT, SH])
                chain(nc.vector.tensor_tensor(raw[:, :, d], heads[:, :, BWD * d:BWD * d + SH], bias, ALU.add))
            chain(nc.vector.tensor_scalar(s2[:], raw[:], -1.0, None, ALU.mult))
            nc.vector.tensor_tensor(s1[:], raw[:], s2[:], ALU.max).then_inc(absolute, 1)
            dve.wait_ge(a_exp, 1)
            chain(nc.vector.tensor_scalar_add(s2[:], s1[:], 2.0))
            chain(nc.vector.reciprocal(s2[:], s2[:]))
            chain(nc.vector.tensor_tensor(s1[:], s1[:], s2[:], ALU.mult))
            chain(nc.vector.tensor_tensor(s2[:], s1[:], s1[:], ALU.mult))
            chain(nc.vector.tensor_scalar(s3[:], s2[:], 2.0 / 17, None, ALU.mult))
            for odd in (15, 13, 11, 9, 7, 5, 3):
                chain(nc.vector.scalar_tensor_tensor(s3[:], s3[:], 2.0 / odd, s2[:], ALU.add, ALU.mult))
            chain(nc.vector.scalar_tensor_tensor(s3[:], s3[:], 2.0, s1[:], ALU.add, ALU.mult))
            chain(nc.vector.scalar_tensor_tensor(m.dt_tok[:], raw[:], 0.0, s3[:], ALU.max, ALU.add))
            nc.vector.tensor_tensor(dta[:], m.dt_tok[:], g.a_neg[:].unsqueeze(1).broadcast_to([P, NT, 2, SH]), ALU.mult).then_inc(dta_made, 1)
            dve.wait_ge(cum_made, 1)
            nc.vector.tensor_copy(m.cum_tok[:], psd[:, 0:NT * 2 * SH].rearrange("p (c d h) -> p c d h", d=2, h=SH)).then_inc(cum_copied, 1)
            dve.wait_ge(tot, 1)
            totals = psd[:, 0:NT * 2 * SH].rearrange("p (c d h) -> p c d h", d=2, h=SH)
            nc.vector.tensor_copy(m.etot[:], totals)
            nc.vector.tensor_tensor(w_tok[:], totals, m.cum_tok[:], ALU.subtract).then_inc(tot_copied, 1)
            for i in range(3):
                k0, nk = 4 * i, min(4, NT - 4 * i)
                dve.wait_ge(row_turned, i + 1)
                nc.vector.tensor_copy(cum[:, k0:k0 + nk], ps_cum[:, 0:nk]).then_inc(row_copied, 1)

            def tile(v, s):
                dve.wait_ge(first, 2 * v + (s + 1))
                for tap in range(1, 5):
                    ins = nc.vector.scalar_tensor_tensor(acc[:, s], pad[:, s, tap:tap + PAD - 4], taps[:, s, tap:tap + 1], acc[:, s],
                                                         ALU.mult, ALU.add)
                    if tap < 4:
                        chain(ins)
                    else:
                        ins.then_inc(summed, 1)

            def get_taps(v, s):
                col = bass.ds(2 * v + s, 1)
                chain(nc.vector.tensor_copy(taps[:, s, 0:5], g.cols_a[:, ROW_CW:ROW_CW + 40].rearrange("p (a t) -> p a t", t=CONV_T)[:, :, col].rearrange("p a o -> p (a o)")))
                nc.vector.tensor_copy(taps[:, s, 5:6], g.cols_a[:, ROW_CB:ROW_CB + CONV_T][:, col]).then_inc(tapped, 1)

            def copies(v, s):
                dve.wait_ge(tok_out[s], 16 * v + 16)
                for i in range(3):
                    k0, nk = 4 * i, min(4, NT - 4 * i)
                    dve.wait_ge(turned, 6 * v + (3 * s + i + 5))
                    nc.vector.tensor_copy(tok[:, s, k0:k0 + nk], ps[:, s, i, 0:nk]).then_inc(tok_done, 1)
            def tile_then_taps(v, s):
                tile(v, s)
                dve.wait_ge(summed, 2 * v + (s + 3))
                get_taps(v + 1, s)
            for s in range(2):
                get_taps(0, s)
            for s in range(2):
                tile_then_taps(0, s)
            with dve.Fori(0, TURNED - 1) as v, chain.over(v, TURNED - 1, 8):
                for s in range(2):
                    tile_then_taps(v + 1, s)
                    copies(v, s)
            for s in range(2):
                tile(PAIRS - 1, s)
                copies(PAIRS - 2, s)
            dve.wait_ge(a_exp, 2)
            nc.vector.tensor_tensor(m.w_tok[:], w_tok[:], m.dt_tok[:], ALU.mult)

        @block.tensor
        def _(pe):
            pe.sem_inc(turned, 4)
            for c in range(NT):
                last = nc.tensor.transpose(psd[:, c * DTP:(c + 1) * DTP], m.dt[:, c * P:(c + 1) * P], g.ident[0:DTP, 0:DTP])
            last.then_inc(dt_turned, 1)
            pe.wait_ge(dta_made, 1)
            sums = psd[:, 0:NT * 2 * SH].rearrange("p (c d h) -> p c d h", d=2, h=SH)
            for d in range(2):
                last = nc.tensor.matmul(sums[:, :, d], g.masks[:, d], dta[:, :, d], start=True, stop=True)
            last.then_inc(cum_made, 1)
            pe.wait_ge(cum_copied, 1)
            nc.tensor.matmul(psd[:, 0:NT * 2 * SH], g.ones[:], dta.rearrange("p c d h -> p (c d h)"), start=True, stop=True).then_inc(tot, 1)
            for i in range(3):
                if i:
                    pe.wait_ge(row_copied, i)
                for k in range(min(4, NT - 4 * i)):
                    last = nc.tensor.transpose(ps_cum[:, k], m.cum_tok[:, 4 * i + k].rearrange("p d h -> p (d h)"), g.ident[:])
                last.then_inc(row_turned, 1)
            with pe.Fori(0, TURNED) as v:
                for s in range(2):
                    pe.wait_ge(done, 2 * v + s + 1)
                    pe.wait_ge(tok_done, 6 * v + (3 * s + 1))
                    for i in range(3):
                        for x in range(min(4, NT - 4 * i)):
                            c = 4 * i + x
                            last = nc.tensor.transpose(ps[:, s, i, x], cv[:, s, c * P:(c + 1) * P], g.ident[:])
                        last.then_inc(turned, 1)


def wait_if(eng, sem, value):
    if not isinstance(value, int) or value > 0:
        eng.wait_ge(sem, value)


def scan_state_stage(nc, g, m, layer):
    XB = SW + NG * P
    with Stage(nc, f"state{layer}") as st:
        tok = st.sb("tok", [P, 2, 2, XB])
        xw = st.sb("xw", [P, 2, 2, SW])
        h = st.sb("h", [P, 2, 2, SW])
        hd = st.sb("hd", [P, 2, 2, SW])
        ps = st.ps("ps", [P, 2, 2, SW])
        tok_in = [[st.sem(f"tok_in{d}{s}") for s in range(2)] for d in range(2)]
        weighted, pushed, updated, decayed = ([st.sem(f"{x}{d}") for d in range(2)] for x in ("weighted", "pushed", "updated", "decayed"))
        stored = [[st.sem(f"stored{d}{s}") for s in range(2)] for d in range(2)]
        zeroed = st.sem("zeroed")
        v0 = 0 if layer == 0 else 1
        NA = 2 * P
        att_sq, att_m, att_r, att_t = (st.sb(x, [P, HEADS, NA]) for x in ("att_sq", "att_m", "att_r", "att_t"))
        ps_a = st.ps("ps_a", [P, HEADS, NA])
        att_squared, att_total, att_mean, att_log, att_guess, att_newton, att_done = (st.sem(f"att_{x}") for x in (
            "squared", "total", "mean", "log", "guess", "newton", "done"))
        block = st.block()

        def att(v):
            return m.att[:, :, bass.ds(v * NA, NA)]

        def no_att(v):
            pass

        def steps(body, eng, mid=no_att, end=no_att):
            body(0, 0, (0, 1))
            if v0 == 0:
                mid(0)
            body(0, 1, (1, 0))
            if v0 == 0:
                end(0)
            down = eng.alloc_register(f"backward_chunk{layer}")
            eng.reg_mov(down, NT + 1)
            with eng.Fori(1, NT // 2) as v:
                eng.reg_sub(down, down, 2)
                back = eng.snap(down, min_val=3, max_val=NT - 1)
                body(v, 0, (2 * v, back))
                mid(v)
                body(v, 1, (2 * v + 1, back - 1))
                end(v)

        @block.scalar
        def _(act):
            def norm(v):
                act.wait_ge(att_done, v + (1 - v0))
                nc.scalar.activation(att_sq[:], att(v), ACT.Square).then_inc(att_squared, 1)
                act.wait_ge(att_mean, v + (1 - v0))
                nc.scalar.activation(att_r[:], att_m[:], ACT.Ln).then_inc(att_log, 1)
                act.wait_ge(att_log, v + (1 - v0))
                nc.scalar.activation(att_r[:], att_r[:], ACT.Exp, scale=-0.5).then_inc(att_guess, 1)
            if v0 == 0:
                norm(0)
            with act.Fori(1, NT // 2) as v:
                norm(v)

        @block.sync
        def _(sp):
            def body(v, s, c):
                for d in range(2):
                    wait_if(sp, pushed[d], 2 * v + (s - 1))
                    sp.dma_start(tok[:, d, s], g.tok_d[bass.ds(c[d], 1)].rearrange("o p f -> p (o f)")).then_inc(tok_in[d][s], 16)
                for d in range(2):
                    wait_if(sp, updated[d], 2 * v + s)
                    if isinstance(v, int) and s == 0:
                        sp.wait_ge(zeroed, 2)
                    sp.dma_start(g.h_d[d, bass.ds(c[d], 1)].rearrange("o p f -> p (o f)"), h[:, d, s]).then_inc(stored[d][s], 16)
            steps(body, sp)
            for d in range(2):
                for s in range(2):
                    sp.wait_ge(stored[d][s], 16 * (NT // 2))

        @block.gpsimd
        def _(pool):
            for d in range(2):
                nc.gpsimd.memset(h[:, d, 0], 0.0).then_inc(zeroed, 1)

            def body(v, s, c):
                for d in range(2):
                    pool.wait_ge(tok_in[d][s], 16 * v + 16)
                    wait_if(pool, pushed[d], 2 * v + (s - 1))
                    nc.gpsimd.tensor_tensor(xw[:, d, s].rearrange("p (h e) -> p h e", h=SH), tok[:, d, s, 0:SW].rearrange("p (h e) -> p h e", h=SH),
                                            m.w_tok[:, bass.ds(c[d], 1), d].rearrange("p o h -> p (o h)").unsqueeze(2).broadcast_to([P, SH, 64]),
                                            ALU.mult).then_inc(weighted[d], 1)
            steps(body, pool)

        @block.tensor
        def _(pe):
            def body(v, s, c):
                for d in range(2):
                    pe.wait_ge(weighted[d], 2 * v + (s + 1))
                    wait_if(pe, updated[d], 2 * v + (s - 1))
                    for q in range(NG):
                        w = SW // NG
                        last = nc.tensor.matmul(ps[:, d, s, q * w:(q + 1) * w], tok[:, d, s, SW + q * P:SW + (q + 1) * P],
                                                xw[:, d, s, q * w:(q + 1) * w], start=True, stop=True)
                    last.then_inc(pushed[d], 1)

            def total(v):
                pe.wait_ge(att_squared, v + (1 - v0))
                for i in range(2):
                    pair = slice(2 * i, 2 * i + 2)
                    last = nc.tensor.matmul(ps_a[:, pair], g.ones[:], att_sq[:, pair], start=True, stop=True)
                last.then_inc(att_total, 1)
            steps(body, pe, total)

        @block.vector
        def _(dve):
            def body(v, s, c):
                for d in range(2):
                    if isinstance(v, int) and s == 0:
                        dve.wait_ge(zeroed, 2)
                    wait_if(dve, updated[d], 2 * v + s)
                    nc.vector.tensor_tensor(hd[:, d, s].rearrange("p (h e) -> p h e", h=SH), h[:, d, s].rearrange("p (h e) -> p h e", h=SH),
                                            m.etot[:, bass.ds(c[d], 1), d].rearrange("p o h -> p (o h)").unsqueeze(2).broadcast_to([P, SH, 64]),
                                            ALU.mult).then_inc(decayed[d], 1)
                for d in range(2):
                    dve.wait_ge(decayed[d], 2 * v + (s + 1))
                    dve.wait_ge(pushed[d], 2 * v + (s + 1))
                    wait_if(dve, stored[d][1 - s], 16 * v + 16 * s)
                    nc.vector.tensor_tensor(h[:, d, 1 - s], hd[:, d, s], ps[:, d, s], ALU.add).then_inc(updated[d], 1)

            def mean(v):
                dve.wait_ge(att_total, v + (1 - v0))
                nc.vector.tensor_scalar(att_m[:], ps_a[:], 1.0 / P, EPS, ALU.mult, ALU.add).then_inc(att_mean, 1)

            def normed(v):
                dve.wait_ge(att_guess, v + (1 - v0))
                nc.vector.tensor_tensor(att_t[:], att_r[:], att_r[:], ALU.mult).then_inc(att_newton, 1)
                dve.wait_ge(att_newton, 3 * v + (1 - 3 * v0))
                nc.vector.scalar_tensor_tensor(att_t[:], att_t[:], -0.5, att_m[:], ALU.mult, ALU.mult).then_inc(att_newton, 1)
                dve.wait_ge(att_newton, 3 * v + (2 - 3 * v0))
                nc.vector.scalar_tensor_tensor(att_r[:], att_t[:], 1.5, att_r[:], ALU.add, ALU.mult).then_inc(att_newton, 1)
                dve.wait_ge(att_newton, 3 * v + (3 - 3 * v0))
                nc.vector.scalar_tensor_tensor(att(v), att(v), g.sub_col[:, 0:1], att_r[:], ALU.mult, ALU.mult).then_inc(att_done, 1)
            dve.sem_inc(att_done, 1)
            steps(body, dve, mean, normed)


def scan_out_stage(nc, g, m, layer):
    v0 = 0 if layer == 0 else 1
    n_v = NT // 2 - v0
    DH = 2 * SH
    with Stage(nc, f"scan{layer}") as st:
        cv = st.sb("cv", [P, 2, 8, P])
        z = st.sb("z", [P, 2, 4, P])
        xt = st.sb("xt", [P, 2, SW])
        h = st.sb("h", [P, 2, 2, SW])
        rows = st.sb("rows", [P, 2, DH, P])
        seg = st.sb("seg", [P, 2, DH, P])
        er = st.sb("er", [P, 2, DH, P])
        xdt = st.sb("xdt", [P, 2, 2, SW])
        cbm = st.sb("cbm", [P, 2, 2, NG, P])
        skip = st.sb("skip", [P, 2, 4, P])
        ps_c = st.ps("ps_c", [P, 2, 4, P])
        ps_y = st.ps("ps_y", [P, 2, 4, P])
        loaded = [st.sem(f"loaded{s}") for s in range(2)]
        rows_in = [st.sem(f"rows_in{s}") for s in range(2)]
        crossed, masked, clipped, diffed, decays, row_decays, c_scaled, x_scaled, intra, summed, skipped, added, gated = (st.sem(x) for x in (
            "crossed", "masked", "clipped", "diffed", "decays", "row_decays", "c_scaled", "x_scaled", "intra", "summed", "skipped", "added", "gated"))
        LOADS = 4
        block = st.block()

        def steps(body, eng):
            for s in range(2):
                body(0, s)
            with eng.Fori(1, n_v) as w:
                for s in range(2):
                    body(w, s)

        @block.sync
        def _(sp):
            def body(w, s):
                c = 2 * w + (2 * v0 + s)
                wait_if(sp, gated, 2 * w + (s - 1))
                toks = bass.ds(c * P, P)
                sp.dma_start(rows[:, s], g.cum_d[:, toks].unsqueeze(0).broadcast_to([P, DH, P])).then_inc(rows_in[s], 16)
                sp.dma_start(cv[:, s], g.cv_d.rearrange("t p k -> p t k")[:, :, toks]).then_inc(loaded[s], 16)
                sp.dma_start(xt[:, s], g.tok_d[bass.ds(c, 1), :, 0:SW].rearrange("o p f -> p (o f)")).then_inc(loaded[s], 16)
                sp.dma_start(h[:, s], g.h_d[:, bass.ds(c, 1)].rearrange("d o p f -> p d (o f)")).then_inc(loaded[s], 16)
                sp.dma_start(z[:, s], g.zx_d[0:4].rearrange("t p k -> p t k")[:, :, toks]).then_inc(loaded[s], 16)
            steps(body, sp)

        @block.tensor
        def _(pe):
            def body(w, s):
                pe.wait_ge(loaded[s], 16 * LOADS * w + 16 * LOADS)
                wait_if(pe, masked, 2 * w + (s - 1))
                for q in range(NG):
                    last = nc.tensor.matmul(ps_c[:, s, q], cv[:, s, 4 + q], cv[:, s, 6 + q], start=True, stop=True)
                last.then_inc(crossed, 1)
                pe.wait_ge(x_scaled, 2 * w + (s + 1))
                pe.wait_ge(c_scaled, 2 * w + (s + 1))
                pe.wait_ge(intra, 2 * w + (s + 1))
                wait_if(pe, added, 2 * w + (s - 1))
                for t in range(4):
                    for e in range(2):
                        hd = 2 * t + e
                        out = ps_y[64 * e:64 * e + 64, s, t]
                        cols = slice(64 * hd, 64 * hd + 64)
                        for d in range(2):
                            nc.tensor.matmul(out, xdt[:, s, d, cols], seg[:, s, SH * d + hd], start=d == 0, stop=False)
                            last = nc.tensor.matmul(out, h[:, s, d, cols], er[:, s, SH * d + hd], start=False, stop=d == 1)
                last.then_inc(summed, 1)
            steps(body, pe)

        @block.scalar
        def _(act):
            def body(w, s):
                act.wait_ge(rows_in[s], 16 * w + 16)
                wait_if(act, summed, 2 * w + (s - 1))
                nc.scalar.activation(er[:, s], rows[:, s], ACT.Exp).then_inc(row_decays, 1)
                act.wait_ge(diffed, 2 * w + (s + 1))
                nc.scalar.activation(seg[:, s], seg[:, s], ACT.Exp).then_inc(decays, 1)
            steps(body, act)

        @block.gpsimd
        def _(pool):
            def body(w, s):
                c = bass.ds(2 * w + (2 * v0 + s), 1)
                pool.wait_ge(loaded[s], 16 * LOADS * w + 16 * LOADS)
                wait_if(pool, summed, 2 * w + (s - 1))
                for d in range(2):
                    last = nc.gpsimd.tensor_tensor(xdt[:, s, d].rearrange("p (h e) -> p h e", h=SH), xt[:, s].rearrange("p (h e) -> p h e", h=SH),
                                                   m.dt_tok[:, c, d].rearrange("p o h -> p (o h)").unsqueeze(2).broadcast_to([P, SH, 64]), ALU.mult)
                last.then_inc(x_scaled, 1)
                wait_if(pool, gated, 2 * w + (s - 1))
                nc.gpsimd.tensor_tensor(skip[:, s], cv[:, s, 0:4], g.dskip_b[:], ALU.mult).then_inc(skipped, 1)
                pool.wait_ge(row_decays, 2 * w + (s + 1))
                for d in range(2):
                    view = er[:, s, SH * d:SH * d + SH].rearrange("p (q r) i -> p q r i", q=NG)
                    last = nc.gpsimd.tensor_tensor(view, view, cv[:, s, 6:8].unsqueeze(2).broadcast_to([P, NG, SH // NG, P]), ALU.mult)
                last.then_inc(c_scaled, 1)
            steps(body, pool)

        @block.vector
        def _(dve):
            def decay(w, s):
                c = bass.ds(2 * w + (2 * v0 + s), 1)
                cum = m.cum_tok[:, c].rearrange("p o d h -> p (o d h)").unsqueeze(2).broadcast_to([P, DH, P])
                dve.wait_ge(rows_in[s], 16 * w + 16)
                wait_if(dve, summed, 2 * w + (s - 1))
                nc.vector.tensor_tensor(seg[:, s], rows[:, s], cum, ALU.min).then_inc(clipped, 1)
                dve.wait_ge(clipped, 2 * w + (s + 1))
                nc.vector.tensor_tensor(seg[:, s], seg[:, s], cum, ALU.subtract).then_inc(diffed, 1)

            def body(w, s, last=False):
                dve.wait_ge(crossed, 2 * w + (s + 1))
                for d in range(2):
                    ins = nc.vector.tensor_tensor(cbm[:, s, d], ps_c[:, s, 0:NG], g.masks[:, d].unsqueeze(1).broadcast_to([P, NG, P]), ALU.mult)
                ins.then_inc(masked, 1)
                dve.wait_ge(masked, 2 * w + (s + 1))
                dve.wait_ge(decays, 2 * w + (s + 1))
                view = seg[:, s].rearrange("p (a r) i -> p a r i", r=SH // NG)
                nc.vector.tensor_tensor(view, view, cbm[:, s].rearrange("p d q i -> p (d q) i").unsqueeze(2).broadcast_to([P, 4, SH // NG, P]),
                                        ALU.mult).then_inc(intra, 1)
                if not last:
                    decay(w + s, 1 - s)
                dve.wait_ge(summed, 2 * w + (s + 1))
                dve.wait_ge(skipped, 2 * w + (s + 1))
                nc.vector.tensor_tensor(skip[:, s], skip[:, s], ps_y[:, s], ALU.add).then_inc(added, 1)
                dve.wait_ge(added, 2 * w + (s + 1))
                out = m.ssd[:, :, bass.ds((2 * w + (2 * v0 + s)) * P, P)]
                nc.vector.tensor_tensor(out, skip[:, s], z[:, s], ALU.mult).then_inc(gated, 1)
            decay(0, 0)
            for s in range(2):
                body(0, s)
            with dve.Fori(1, n_v - 1) as w:
                for s in range(2):
                    body(w, s)
            body(n_v - 1, 0)
            body(n_v - 1, 1, True)


def output_stage(nc, g):
    tiles = LAT // P
    with Stage(nc, "output") as st:
        xt = st.sb("xt", [P, 2, KD, P])
        xtok = st.sb("xtok", [P, 2, KD, P])
        tp = st.ps("tp", [P, 2, KD, P])
        x_in = [st.sem(f"x_in{s}") for s in range(2)]
        stored = [st.sem(f"stored{s}") for s in range(2)]
        turned, copied = st.sem("turned"), st.sem("copied")
        block = st.block()

        @block.sync
        def _(sp):
            with sp.Fori(0, tiles // 2) as v:
                for s in range(2):
                    sp.wait_ge(turned, 2 * v + s + 1)
                    sp.dma_start(xt[:, s], g.xT.rearrange("(k p) t -> p k t", p=P)[:, :, bass.ds((2 * v + s) * P + CTX, P)]).then_inc(x_in[s], 16)

        @block.tensor
        def _(pe):
            pe.sem_inc(turned, 2)
            with pe.Fori(0, tiles // 2) as v:
                for s in range(2):
                    pe.wait_ge(x_in[s], 16 * v + 16)
                    pe.wait_ge(copied, 2 * v + s + 1)
                    for k in range(KD):
                        last = nc.tensor.transpose(tp[:, s, k], xt[:, s, k], g.ident[:])
                    last.then_inc(turned, 1)

        @block.vector
        def _(dve):
            dve.sem_inc(copied, 2)
            for s in range(2):
                dve.sem_inc(stored[s], 16)
            with dve.Fori(0, tiles // 2) as v:
                for s in range(2):
                    dve.wait_ge(turned, 2 * v + s + 3)
                    dve.wait_ge(stored[s], 16 * v + 16)
                    nc.vector.tensor_copy(xtok[:, s], tp[:, s]).then_inc(copied, 1)

        @block.scalar
        def _(act):
            with act.Fori(0, tiles // 2) as v:
                for s in range(2):
                    act.wait_ge(copied, 2 * v + s + 3)
                    act.dma_start(g.out[0, bass.ds((2 * v + s) * P, P), :].rearrange("p (k q) -> p k q", q=P), xtok[:, s]).then_inc(stored[s], 16)
            for s in range(2):
                act.wait_ge(stored[s], 16 * (tiles // 2 + 1))


class Names:
    pass


def backbone(nc, x_in, c, c_ctx, w_ada, b_ada, norm_g, w_in, conv_w, conv_b, a_log, dt_bias, d_skip,
             ssd_norm_g, diff_lambda, subln_g, w_out, w_ffn_in, w_ffn_out, ident, masks, rope, out):
    g = Names()
    g.x_in, g.c, g.c_ctx, g.w_ada, g.b_ada, g.norm_g, g.w_in = x_in, c, c_ctx, w_ada, b_ada, norm_g, w_in
    g.conv_w, g.conv_b, g.a_log, g.dt_bias_d, g.d_skip = conv_w, conv_b, a_log, dt_bias, d_skip
    g.ssd_g, g.lam_d, g.sub_g, g.w_out, g.w_ffn_in, g.w_ffn_out = ssd_norm_g, diff_lambda, subln_g, w_out, w_ffn_in, w_ffn_out
    g.ident_d, g.masks_d, g.rope_d, g.out = ident, masks, rope, out
    g.xT = nc.dram_tensor("xT", [D_MODEL, T], F32).ap()
    g.zx_d = nc.dram_tensor("zx_d", [12, P, T], F32).ap()
    g.qk_d = nc.dram_tensor("qk_d", [2, QK_TILES, P, T], F32).ap()
    g.v_d = nc.dram_tensor("v_d", [2, HEADS, T, P], F32).ap()
    g.cv_d = nc.dram_tensor("cv_d", [8, P, T], F32).ap()
    g.tok_d = nc.dram_tensor("tok_d", [NT, P, SW + NG * P], F32).ap()
    g.cum_d = nc.dram_tensor("cum_d", [2 * SH, T], F32).ap()
    g.h_d = nc.dram_tensor("h_d", [2, NT, P, SW], F32).ap()
    with ExitStack() as ctx:
        def sb(name, shape):
            return ctx.enter_context(nc.sbuf_tensor(name, shape, F32))
        g.ident, g.masks, g.ones = sb("ident", [P, P]), sb("masks", [P, 2, P]), sb("ones", [P, P])
        g.cols_a, g.cols_b = sb("cols_a", [P, P]), sb("cols_b", [P, 21])
        g.mod, g.pre, g.post = sb("mod", [P, 2, 48]), sb("pre", [P, 2, 2, KD]), sb("post", [P, 2, 2, KD])
        g.a_neg, g.dt_bias = sb("a_neg", [P, 2, SH]), sb("dt_bias", [P, 2, SH])
        g.neg_lam, g.sub_col = sb("neg_lam", [P, 1]), sb("sub_col", [P, 1])
        g.dskip_b = sb("dskip_b", [P, 4, P])
        setup_stage(nc, g)
        for layer in range(2):
            ada_stage(nc, g, layer)
            chunks = range(3) if layer == 0 else range(1, 3)
            with ExitStack() as mixer:
                m = Names()

                def keep(stack, name, shape):
                    return stack.enter_context(nc.sbuf_tensor(f"{name}{layer}", shape, F32))
                m.att = keep(mixer, "att", [P, HEADS, T])
                m.ssd = keep(mixer, "ssd", [P, 4, T])
                with ExitStack() as scan:
                    m.dt = keep(scan, "dt", [DTP, T])
                    in_proj_stage(nc, g, m, layer)
                    attention_stage(nc, g, m, layer)
                    m.dt_tok, m.cum_tok, m.w_tok, m.etot = (keep(scan, x, [P, NT, 2, SH]) for x in ("dt_tok", "cum_tok", "w_tok", "etot"))
                    scan_prep_stage(nc, g, layer, m)
                    scan_state_stage(nc, g, m, layer)
                    scan_out_stage(nc, g, m, layer)
                out_proj_stage(nc, g, m, layer, chunks)
            ffn_stage(nc, g, layer, chunks)
        output_stage(nc, g)


_INS = ["c", "c_ctx", "w_ada", "b_ada", "norm_g", "w_in", "conv_w", "conv_b", "a_log", "dt_bias", "d_skip",
        "ssd_norm_g", "diff_lambda", "subln_g", "w_out", "w_ffn_in", "w_ffn_out"]


def _constants():
    import numpy as np
    f = np.float32
    ident = np.eye(P, dtype=f)
    upper = np.triu(np.ones((P, P), f))
    masks = np.stack([upper, np.ascontiguousarray(upper.T)])
    row = np.repeat(np.arange(LAT // 64, dtype=f), 64)
    col = np.tile(np.arange(64, dtype=f), LAT // 64)
    inv = (f(10000.0) ** (-np.arange(16, dtype=f) / f(16))).astype(f)
    ang = np.concatenate([row[:, None] * inv, col[:, None] * inv], axis=-1).T
    cos, sin = np.cos(ang).astype(f), np.sin(ang).astype(f)
    rope = np.zeros((2, P, T), f)
    rope[0, :, 0:CTX] = 1.0
    rope[0, :, CTX:] = np.tile(cos, (4, 1))
    rope[1, :, CTX:] = np.concatenate([-sin, sin, -sin, sin])
    return {"ident": ident, "masks": masks, "rope": rope}


def kernel(**inputs):
    import numpy as _np
    import concourse.bacc as _bacc
    from concourse import mybir as _mybir
    from concourse.bass_utils import run_bass_kernel_spmd as _run

    nc = _bacc.Bacc("TRN2", target_bir_lowering=False, num_devices=1)
    given = {"x_in": _np.concatenate([inputs["ctx"][0], inputs["x"][0]], axis=0)}
    given.update({name: inputs[name] for name in _INS})
    given.update(_constants())
    arrays, args = {}, []
    for name, a in given.items():
        a = _np.ascontiguousarray(a)
        arrays[f"in_{name}_dram"] = a
        args.append(nc.dram_tensor(f"in_{name}_dram", a.shape, _mybir.dt.from_np(a.dtype), kind="ExternalInput").ap())
    args.append(nc.dram_tensor("out_0_dram", (1, LAT, D_MODEL), F32, kind="ExternalOutput").ap())
    backbone(nc, *args)
    r = _run(nc, [arrays], core_ids=[0])
    return r.results[0]["out_0_dram"]
```
